# Optimizing a Trainium2 kernel written in Bass

```python
import jax, jax.numpy as jnp
from jax import lax
import numpy as np

D_MODEL = 1024
BATCH = 1
SEQ = 128
DEPTH = 1
DEC_BATCH = 1
DEC_SEQ = 512
PAST_LEN = 128

GRID_W = 64
HR = 4
DK_R = 128
DV_R = 128
RET_CHUNK = 64
HG = 4
DK_G = 64
DV_G = 128
GATE_RANK = 16
GLA_TAU = 16.0
GLA_CHUNK = 16
MIX_W = HR * DV_R + HG * DV_G
IN_SIZES = (HR * DK_R, HR * DK_R, HR * DV_R, HR * DV_R,
            HG * DK_G, HG * DK_G, HG * DV_G, HG * DV_G,
            GATE_RANK, GATE_RANK)
IN_COLS = sum(IN_SIZES)
N_GROUPS = 4
EXPERTS_PER_GROUP = 8
N_EXPERTS = N_GROUPS * EXPERTS_PER_GROUP
TOP_K_INNER = 2
D_EXPERT = 256
ROPE_BASE = 10000.0
EPS = 1e-6

kernel_name = 'hybrid_retention_gla_hmoe_diffusion_step'

def split_points(sizes):
    pts, run = [], 0
    for s in sizes[:-1]:
        run += s
        pts.append(run)
    return pts

def rmsnorm(x, w):
    xf = x.astype(jnp.float32)
    y = xf * lax.rsqrt(jnp.mean(xf * xf, axis=-1, keepdims=True) + EPS)
    return (y * w.astype(jnp.float32)).astype(x.dtype)

def heads(t, n_heads):
    b, l, _ = t.shape
    return t.reshape(b, l, n_heads, -1).transpose(0, 2, 1, 3).astype(jnp.float32)

def merge_heads(o):
    b, h, l, d = o.shape
    return o.transpose(0, 2, 1, 3).reshape(b, l, h * d)

def flip_seq(t):
    return jnp.flip(t, axis=2)

def rope_2d(x):
    n_tok = x.shape[2]
    rows = n_tok // GRID_W
    row = jnp.repeat(jnp.arange(rows), GRID_W).astype(jnp.float32)
    col = jnp.tile(jnp.arange(GRID_W), rows).astype(jnp.float32)
    half = DK_R // 2
    quarter = DK_R // 4
    freqs = ROPE_BASE ** (-jnp.arange(quarter, dtype=jnp.float32) / quarter)

    def rot(xb, pos):
        ang = pos[:, None] * freqs[None, :]
        cos, sin = jnp.cos(ang), jnp.sin(ang)
        x1, x2 = xb[..., :quarter], xb[..., quarter:]
        return jnp.concatenate([x1 * cos - x2 * sin, x1 * sin + x2 * cos], axis=-1)

    return jnp.concatenate([rot(x[..., :half], row), rot(x[..., half:], col)], axis=-1)

def retention_chunked(q, k, v, log_gamma, s0):
    b, h, l, dk = q.shape
    dv = v.shape[-1]
    c = RET_CHUNK
    n = l // c
    qc = q.reshape(b, h, n, c, dk)
    kc = k.reshape(b, h, n, c, dk)
    vc = v.reshape(b, h, n, c, dv)
    idx = jnp.arange(c, dtype=jnp.float32)
    rel = idx[:, None] - idx[None, :]
    decay = jnp.where(rel >= 0, jnp.exp(log_gamma[:, None, None] * jnp.maximum(rel, 0.0)), 0.0)
    scores = jnp.einsum('bhncd,bhnmd->bhncm', qc, kc) * decay[None, :, None]
    o_intra = jnp.einsum('bhncm,bhnme->bhnce', scores, vc)
    w_state = jnp.exp(log_gamma[:, None] * (c - 1 - idx)[None, :])
    u = jnp.einsum('bhnmd,hm,bhnme->nbhde', kc, w_state, vc)
    chunk_decay = jnp.exp(log_gamma * c)[None, :, None, None]

    def step(s, u_n):
        return chunk_decay * s + u_n, s

    s_final, s_start = lax.scan(step, s0, u)
    q_dec = qc * jnp.exp(log_gamma[:, None] * (idx + 1.0)[None, :])[None, :, None, :, None]
    o_inter = jnp.einsum('bhncd,nbhde->bhnce', q_dec, s_start)
    return (o_intra + o_inter).reshape(b, h, l, dv), s_final

def gla_chunked(q, k, v, log_a, s0):
    b, h, l, dk = q.shape
    dv = v.shape[-1]
    c = GLA_CHUNK
    n = l // c
    qc = q.reshape(b, h, n, c, dk)
    kc = k.reshape(b, h, n, c, dk)
    vc = v.reshape(b, h, n, c, dv)
    cum = jnp.cumsum(log_a.reshape(b, h, n, c, dk), axis=3)
    causal = jnp.tril(jnp.ones((c, c), dtype=bool))
    diff = cum[:, :, :, :, None, :] - cum[:, :, :, None, :, :]
    e = jnp.exp(jnp.where(causal[:, :, None], diff, -jnp.inf))
    scores = jnp.einsum('bhnjd,bhnmd,bhnjmd->bhnjm', qc, kc, e)
    o_intra = jnp.einsum('bhnjm,bhnme->bhnje', scores, vc)
    last = cum[:, :, :, -1:, :]
    u = jnp.einsum('bhnmd,bhnme->nbhde', kc * jnp.exp(last - cum), vc)
    chunk_decay = jnp.exp(last[:, :, :, 0, :]).transpose(2, 0, 1, 3)

    def step(s, inp):
        d_n, u_n = inp
        return d_n[..., None] * s + u_n, s

    s_final, s_start = lax.scan(step, s0, (chunk_decay, u))
    o_inter = jnp.einsum('bhnjd,nbhde->bhnje', qc * jnp.exp(cum), s_start)
    return (o_intra + o_inter).reshape(b, h, l, dv), s_final

def hier_moe(t, router_group_w, router_group_b, router_expert_w, router_expert_b,
             expert_w_gate, expert_w_up, expert_w_down):
    n_tok = t.shape[0]
    g_logits = (t @ router_group_w).astype(jnp.float32) + router_group_b.astype(jnp.float32)
    g_prob = jax.nn.softmax(g_logits, axis=-1)
    g_idx = jnp.argmax(g_logits, axis=-1)
    g_w = jnp.take_along_axis(g_prob, g_idx[:, None], axis=-1)
    e_logits = ((t @ router_expert_w).astype(jnp.float32) + router_expert_b.astype(jnp.float32)
                ).reshape(n_tok, N_GROUPS, EXPERTS_PER_GROUP)
    e_sel = jnp.take_along_axis(e_logits, g_idx[:, None, None], axis=1)[:, 0]
    top_v, top_i = lax.top_k(e_sel, TOP_K_INNER)
    w = g_w * jax.nn.softmax(top_v, axis=-1)
    expert_ids = g_idx[:, None] * EXPERTS_PER_GROUP + top_i
    combine = jnp.einsum('tk,tke->te', w, jax.nn.one_hot(expert_ids, N_EXPERTS, dtype=jnp.float32))
    y = jnp.zeros(t.shape, jnp.float32)
    for e in range(N_EXPERTS):
        hdn = jax.nn.silu(t @ expert_w_gate[e]) * (t @ expert_w_up[e])
        y = y + combine[:, e:e + 1] * (hdn @ expert_w_down[e]).astype(jnp.float32)
    return y.astype(t.dtype)

def trunk_layer(x, cond, s_rf, s_rb, s_gf, s_gb, latent,
                w_ada, b_ada, norm1_w, w_in, ret_decay_fwd, ret_decay_bwd, ret_norm_w,
                gla_gate_w_fwd, gla_gate_b_fwd, gla_gate_w_bwd, gla_gate_b_bwd, gla_norm_w,
                w_out, norm2_w, router_group_w, router_group_b, router_expert_w, router_expert_b,
                expert_w_gate, expert_w_up, expert_w_down):
    f32 = jnp.float32
    b, l, d = x.shape
    mod = (jax.nn.silu(cond) @ w_ada + b_ada)[:, None, :]
    sh1, sc1, g1, sh2, sc2, g2 = jnp.split(mod, 6, axis=-1)
    h = rmsnorm(x, norm1_w) * (1 + sc1) + sh1
    proj = h @ w_in
    rq, rk, rv, rg, gq, gk, gv, gr, glr_f, glr_b = jnp.split(proj, split_points(IN_SIZES), axis=-1)

    q = heads(rq, HR)
    k = heads(rk, HR) * DK_R ** -0.5
    v = heads(rv, HR)
    if latent:
        q = rope_2d(q)
        k = rope_2d(k)
    o_f, srf = retention_chunked(q, k, v, -jnp.exp(ret_decay_fwd.astype(f32)), s_rf)
    o_b, srb = retention_chunked(flip_seq(q), flip_seq(k), flip_seq(v),
                                 -jnp.exp(ret_decay_bwd.astype(f32)), s_rb)
    o = o_f + flip_seq(o_b)
    mu = jnp.mean(o, axis=-1, keepdims=True)
    var = jnp.mean(jnp.square(o - mu), axis=-1, keepdims=True)
    o_ret = merge_heads((o - mu) * lax.rsqrt(var + EPS)) * ret_norm_w.astype(f32) * jax.nn.silu(rg.astype(f32))

    gqh = heads(gq, HG) * DK_G ** -0.5
    gkh = heads(gk, HG)
    gvh = heads(gv, HG)
    la_f = heads(jax.nn.log_sigmoid(glr_f.astype(f32) @ gla_gate_w_fwd.astype(f32)
                                    + gla_gate_b_fwd.astype(f32)) / GLA_TAU, HG)
    la_b = heads(jax.nn.log_sigmoid(glr_b.astype(f32) @ gla_gate_w_bwd.astype(f32)
                                    + gla_gate_b_bwd.astype(f32)) / GLA_TAU, HG)
    u_f, sgf = gla_chunked(gqh, gkh, gvh, la_f, s_gf)
    u_b, sgb = gla_chunked(flip_seq(gqh), flip_seq(gkh), flip_seq(gvh), flip_seq(la_b), s_gb)
    u = u_f + flip_seq(u_b)
    o_gla = merge_heads(u * lax.rsqrt(jnp.mean(u * u, axis=-1, keepdims=True) + EPS)) \
        * gla_norm_w.astype(f32) * jax.nn.silu(gr.astype(f32))

    mix = jnp.concatenate([o_ret, o_gla], axis=-1).astype(x.dtype) @ w_out
    x = x + g1 * mix

    hn = rmsnorm(x, norm2_w) * (1 + sc2) + sh2
    y = hier_moe(hn.reshape(b * l, d), router_group_w, router_group_b, router_expert_w,
                 router_expert_b, expert_w_gate, expert_w_up, expert_w_down).reshape(b, l, d)
    x = x + g2 * y
    return x, (srf, srb, sgf, sgb)

def setup_inputs(seed: int = 0) -> dict:
    key = jax.random.key(seed)
    ks = jax.random.split(key, 40)
    nrm = lambda i, shape, s=1.0: jax.random.normal(ks[i], shape, jnp.float32) * s
    d = D_MODEL
    base_decay = jnp.log(-jnp.log1p(-(2.0 ** (-5.0 - jnp.arange(HR, dtype=jnp.float32)))))
    return {
        'x_prompt': nrm(0, (BATCH, SEQ, d)),
        'x_sample': nrm(1, (DEC_BATCH, DEC_SEQ, d)),
        'state_ret_fwd': nrm(2, (DEC_BATCH, DEPTH, HR, DK_R, DV_R)),
        'state_ret_bwd': nrm(3, (DEC_BATCH, DEPTH, HR, DK_R, DV_R)),
        'state_gla_fwd': nrm(4, (DEC_BATCH, DEPTH, HG, DK_G, DV_G)),
        'state_gla_bwd': nrm(5, (DEC_BATCH, DEPTH, HG, DK_G, DV_G)),
        'c': nrm(6, (DEC_BATCH, d)),
        'c_ctx': nrm(7, (d,)),
        'w_ada': nrm(8, (DEPTH, d, 6 * d), 0.5 * d ** -0.5),
        'b_ada': nrm(9, (DEPTH, 6 * d), 0.02),
        'norm1_w': 1.0 + nrm(10, (DEPTH, d), 0.02),
        'w_in': nrm(11, (DEPTH, d, IN_COLS), d ** -0.5),
        'ret_decay_fwd': base_decay[None, :] + nrm(12, (DEPTH, HR), 0.05),
        'ret_decay_bwd': base_decay[None, :] + nrm(13, (DEPTH, HR), 0.05),
        'ret_norm_w': 1.0 + nrm(14, (DEPTH, HR * DV_R), 0.02),
        'gla_gate_w_fwd': nrm(15, (DEPTH, GATE_RANK, HG * DK_G), GATE_RANK ** -0.5),
        'gla_gate_b_fwd': nrm(16, (DEPTH, HG * DK_G), 0.1),
        'gla_gate_w_bwd': nrm(17, (DEPTH, GATE_RANK, HG * DK_G), GATE_RANK ** -0.5),
        'gla_gate_b_bwd': nrm(18, (DEPTH, HG * DK_G), 0.1),
        'gla_norm_w': 1.0 + nrm(19, (DEPTH, HG * DV_G), 0.02),
        'w_out': nrm(20, (DEPTH, MIX_W, d), MIX_W ** -0.5),
        'norm2_w': 1.0 + nrm(21, (DEPTH, d), 0.02),
        'router_group_w': nrm(22, (DEPTH, d, N_GROUPS), d ** -0.5),
        'router_group_b': nrm(23, (DEPTH, N_GROUPS), 0.01),
        'router_expert_w': nrm(24, (DEPTH, d, N_EXPERTS), d ** -0.5),
        'router_expert_b': nrm(25, (DEPTH, N_EXPERTS), 0.01),
        'expert_w_gate': nrm(26, (DEPTH, N_EXPERTS, d, D_EXPERT), d ** -0.5),
        'expert_w_up': nrm(27, (DEPTH, N_EXPERTS, d, D_EXPERT), d ** -0.5),
        'expert_w_down': nrm(28, (DEPTH, N_EXPERTS, D_EXPERT, d), D_EXPERT ** -0.5),
        'final_norm_w': 1.0 + nrm(29, (d,), 0.02),
    }

def reference(x_prompt, x_sample, state_ret_fwd, state_ret_bwd, state_gla_fwd, state_gla_bwd, c,
              c_ctx, w_ada, b_ada, norm1_w, w_in, ret_decay_fwd, ret_decay_bwd, ret_norm_w,
              gla_gate_w_fwd, gla_gate_b_fwd, gla_gate_w_bwd, gla_gate_b_bwd, gla_norm_w, w_out,
              norm2_w, router_group_w, router_group_b, router_expert_w, router_expert_b,
              expert_w_gate, expert_w_up, expert_w_down, final_norm_w):
    f32 = jnp.float32
    xp = x_prompt
    bp = xp.shape[0]
    rf_list, rb_list, gf_list, gb_list = [], [], [], []
    for li in range(DEPTH):
        z_r = jnp.zeros((bp, HR, DK_R, DV_R), f32)
        z_g = jnp.zeros((bp, HG, DK_G, DV_G), f32)
        xp, (srf, srb, sgf, sgb) = trunk_layer(
            xp, c_ctx[None, :], z_r, z_r, z_g, z_g, False,
            w_ada[li], b_ada[li], norm1_w[li], w_in[li], ret_decay_fwd[li], ret_decay_bwd[li],
            ret_norm_w[li], gla_gate_w_fwd[li], gla_gate_b_fwd[li], gla_gate_w_bwd[li],
            gla_gate_b_bwd[li], gla_norm_w[li], w_out[li], norm2_w[li], router_group_w[li],
            router_group_b[li], router_expert_w[li], router_expert_b[li], expert_w_gate[li],
            expert_w_up[li], expert_w_down[li])
        rf_list.append(srf.astype(x_prompt.dtype))
        rb_list.append(srb.astype(x_prompt.dtype))
        gf_list.append(sgf.astype(x_prompt.dtype))
        gb_list.append(sgb.astype(x_prompt.dtype))
    y_prompt = rmsnorm(xp, final_norm_w)
    new_ret_fwd = jnp.stack(rf_list, axis=1)
    new_ret_bwd = jnp.stack(rb_list, axis=1)
    new_gla_fwd = jnp.stack(gf_list, axis=1)
    new_gla_bwd = jnp.stack(gb_list, axis=1)

    xs = x_sample
    for li in range(DEPTH):
        xs, _ = trunk_layer(
            xs, c, state_ret_fwd[:, li].astype(f32), state_ret_bwd[:, li].astype(f32),
            state_gla_fwd[:, li].astype(f32), state_gla_bwd[:, li].astype(f32), True,
            w_ada[li], b_ada[li], norm1_w[li], w_in[li], ret_decay_fwd[li], ret_decay_bwd[li],
            ret_norm_w[li], gla_gate_w_fwd[li], gla_gate_b_fwd[li], gla_gate_w_bwd[li],
            gla_gate_b_bwd[li], gla_norm_w[li], w_out[li], norm2_w[li], router_group_w[li],
            router_group_b[li], router_expert_w[li], router_expert_b[li], expert_w_gate[li],
            expert_w_up[li], expert_w_down[li])
    y_sample = rmsnorm(xs, final_norm_w)
    return (y_prompt, y_sample, new_ret_fwd, new_ret_bwd, new_gla_fwd, new_gla_bwd)


_drawn_inputs = setup_inputs


def setup_inputs(seed=0):
    import zlib

    import numpy as np

    out = dict(_drawn_inputs(seed))
    spreads = {}
    factors = {'state_gla_fwd': 8.0,
     'state_gla_bwd': 8.0,
     'ret_norm_w': 8.0,
     'gla_norm_w': 8.0,
     'norm2_w': 4.994,
     'router_group_b': 8.0,
     'router_expert_b': 7.99,
     'final_norm_w': 2.927}
    for name, (base, spread) in spreads.items():
        noise = np.random.default_rng([zlib.crc32(name.encode()), seed]).standard_normal(out[name].shape)
        drawn = base * np.exp(spread * noise) if base else spread * noise
        out[name] = __import__('jax').numpy.asarray(drawn.astype(out[name].dtype))
    for name, factor in factors.items():
        out[name] = (out[name] * factor).astype(out[name].dtype)
    return out
```

```python
from contextlib import ExitStack

import concourse.bass as bass
from concourse import mybir

P = 128
D = 1024
KC = D // P
N_LAT = 512
N_CTX = 128
T = N_LAT + N_CTX
TILES = T // P
CTX = TILES - 1
LT = N_LAT // P
HEADS = 4
GLA_DK = 64
GRID_W = 64
RANK = 16
NE = 32
NG = 4
EPG = NE // NG
DE = 256
FC = DE // P
SLOTS = 64
MAX_OVER = 19
BLOCKS = NE + MAX_OVER
EPS = 1e-6
ITEM = 256
UNIT = KC * ITEM
RING = 4
ADA_FIRST = 2 * D // ITEM
ADA_ALL = 6 * D // ITEM
STRIP = N_LAT + N_LAT - P
LEVELS = [64, 32, 16, 8, 4, 2, 1]
LEV_TILES = [(0, 2), (2, 4), (4, 5)]
IN_COLS = 3616

IN_ITEMS = [("gq", 2048, 256), ("gk", 2304, 256), ("glr", 3584, 32),
            ("rq", 0, 256), ("rq", 256, 256), ("rk", 512, 256), ("rk", 768, 256),
            ("gv", 2560, 256), ("gv", 2816, 256), ("rv", 1024, 256), ("rv", 1280, 256),
            ("gr", 3072, 256), ("gr", 3328, 256), ("rg", 1536, 256), ("rg", 1792, 256)]
IN_BASE = {"gq": 2048, "gk": 2304, "rq": 0, "rk": 512, "gv": 2560, "rv": 1024, "gr": 3072, "rg": 1536, "glr": 3584}
LEVEL_AFTER = 4

C_IDENT, C_ROT, C_COS, C_SIN, C_MASK = 0, 128, 256, 768, 1280
C_ONES = C_MASK + 7 * P
C_TRI = C_ONES + P
C_IOTA = C_TRI + P
C_TOK = C_IOTA + 64 + 9
C_POS = C_TOK + TILES
C_ONE = C_POS + 2
C_END = C_ONE + 2
R_RELF, R_RELB, R_TF, R_TB = 0, STRIP, 2 * STRIP, 2 * STRIP + N_LAT
R_END = 2 * STRIP + 2 * N_LAT

F32 = mybir.dt.float32
I32 = mybir.dt.int32
U32 = mybir.dt.uint32
ALU = mybir.AluOpType
ACT = mybir.ActivationFunctionType
AX = mybir.AxisListType.X


class Steps:

    def __init__(self, sem, order):
        self.sem, self.order, self.n = sem, list(order), 0

    def done(self, ins, key):
        assert self.order[self.n] == key, (self.order[self.n], key)
        self.n += 1
        ins.then_inc(self.sem, 1)

    def wait(self, eng, key):
        eng.wait_ge(self.sem, self.order.index(key) + 1)


def rots_after(i, c):
    seq = [(i, c) for i in range(3, 7) for c in range(2)] + [(7, 0)]
    return seq[seq.index((i, c)) - 1] if (i, c) in seq[1:] else None


def plan_banks():
    jobs = [("modT", 0)]
    jobs += [("xT", k) for k in range(KC)] + [("xTc", 0), ("xTc", 1)]
    for i, (name, _, w) in enumerate(IN_ITEMS):
        if name in ("gv", "rv"):
            if rots_after(i, 0) is not None:
                jobs.append(("rot", *rots_after(i, 0)))
            jobs += [("v", i, t) for t in range(TILES)]
        else:
            for c in range(max(1, w // P)):
                jobs += [("p", i, c, "lat"), ("p", i, c, "ctx")]
                if rots_after(i, c) is not None:
                    jobs.append(("rot", *rots_after(i, c)))
        if name == "glr":
            jobs += [("z", d, g, part) for d in range(2) for g in range(2) for part in ("lat", "ctx")]
        n = i - LEVEL_AFTER
        if 0 <= n <= len(LEVELS):
            jobs += [("lev", n, m, a) for m in range(len(LEV_TILES)) for a in range(2)]
    jobs += [("kT", d, g) for d in range(2) for g in range(2)]
    jobs += [("gu", d, n) for n in range(4) for d in range(2)]
    jobs += [("go", "ctx")]
    for h in range(HEADS):
        jobs += [("go", h)]
        jobs += [("gT", "ctx") if h == 0 else ("gT", h - 1)]
    jobs += [("gT", HEADS - 1), ("modT", 1)]
    jobs += [("rs", "ctx"), ("rkT",), ("rst", 0), ("rst", 1), ("ro", "ctx")]
    for h in range(HEADS):
        jobs += [("rs", h, s) for s in range(LT)]
        jobs += [("rT", "ctx") if h == 0 else ("rT", h - 1)]
        jobs += [("ro", h)]
    jobs += [("rT", HEADS - 1)]
    for t in range(TILES):
        jobs += [("mix", t, n) for n in range(4)]
        if t >= 1:
            jobs += [("hT", t - 1, 0), ("hT", t - 1, 1), ("lg", t - 1)]
    jobs += [("hT", CTX, 0), ("hT", CTX, 1), ("lg", CTX)]
    jobs += [("pos",), ("idx",)]
    return jobs


def build(nc, inp, outs):
    (x_prompt, x_sample, srf, srb, sgf, sgb, c_in, c_ctx, w_ada, b_ada, norm1_w, w_in, rdf, rdb,
     ret_norm_w, ggwf, ggbf, ggwb, ggbb, gla_norm_w, w_out, norm2_w, rgw, rgb, rew, reb,
     ewg, ewu, ewd, final_w, consts, rconsts) = inp
    y_prompt, y_sample, new_rf, new_rb, new_gf, new_gb = outs

    JOBS = plan_banks()
    NB1 = 7
    job_at = {j: n for n, j in enumerate(JOBS)}
    assert len(job_at) == len(JOBS)

    with ExitStack() as ctx:
        def sb(name, shape, dt=F32):
            return ctx.enter_context(nc.sbuf_tensor(name, shape, dt))

        def sem(name):
            return ctx.enter_context(nc.semaphore(name))

        mod_dram = nc.dram_tensor("mod_rows", (2, 6 * D), F32).ap()
        hn_dram = nc.dram_tensor("hn_rows", (T, D), F32).ap()
        ys_dram = nc.dram_tensor("expert_rows", (BLOCKS * SLOTS, D), F32).ap()

        W = sb("weights", [P, 6 * UNIT])
        X = sb("x_rows", [P, TILES, D])
        H = sb("h_cols", [P, KC * T])
        Q = sb("qkv_gates", [P, 3 * KC * T])
        G = sb("attention", [P, 5 * 4 * T])
        ident = sb("ident", [P, P])
        r_used = [0]

        def rs(*shape):
            n = 1
            for v in shape:
                n *= v
            ap = G[:, r_used[0]:r_used[0] + n]
            r_used[0] += n
            return ap if len(shape) == 1 else ap.rearrange("p (a b) -> p a b", a=shape[0]) if len(shape) == 2 else \
                ap.rearrange("p (a b c) -> p a b c", a=shape[0], b=shape[1])

        onorm = [sb(f"onorm{n}", [P, 4, P]) for n in range(2)]
        idx = sb("slot_tokens", [SLOTS, BLOCKS], I32)
        idxc = [sb(f"slot_tokens_now{n}", [SLOTS, 1], I32) for n in range(4)]
        dest = sb("pick_rows", [P, 2 * TILES], I32)
        destc = sb("pick_rows_now", [P, 2 * TILES], I32)
        pickw = sb("pick_weights", [P, 2, TILES])
        over = sb("overflow", [1, 1 + MAX_OVER], I32)

        S = sb("small", [P, 1000])
        at = [0]

        def small(*shape):
            n = 1
            for v in shape:
                n *= v
            ap = S[:, at[0]:at[0] + n]
            at[0] += n
            if len(shape) == 2:
                ap = ap.rearrange("p (a b) -> p a b", a=shape[0])
            if len(shape) == 3:
                ap = ap.rearrange("p (a b c) -> p a b c", a=shape[0], b=shape[1])
            return ap

        ring = [W[:, u * UNIT:(u + 1) * UNIT] for u in range(RING)]
        tail = W[:, RING * UNIT:6 * UNIT]
        rot_m = tail[:, 0:P]
        cosT, sinT = tail[:, P:P + N_LAT], tail[:, P + N_LAT:P + 2 * N_LAT]
        masks = [tail[:, P + 2 * N_LAT + n * P:P + 2 * N_LAT + (n + 1) * P] for n in range(7)]
        glrT = tail[0:2 * RANK, 2048:2048 + T]
        wgate = tail[0:2 * RANK, 2688:3200].rearrange("p (d n) -> p d n", d=2)
        ones_s = tail[:, 3200:3328]
        sq = tail[:, 3584:4096].rearrange("p (a b) -> p a b", a=4)
        rstate = tail[:, 0:1024].rearrange("p (d h e) -> p d h e", d=2, h=HEADS)
        kdec = tail[:, 1024:2048].rearrange("p (d h e) -> p d h e", d=2, h=HEADS)
        rsout = tail[:, 2048:3072].rearrange("p (d h e) -> p d h e", d=2, h=HEADS)
        cmask = tail[:, 3072:3584].rearrange("p (h t) -> p h t", h=HEADS)

        hT = H[:, :].rearrange("p (k t) -> p k t", k=KC)
        rqk = Q[:, 0:KC * T].rearrange("p (a h t) -> p a h t", a=2, h=HEADS)
        vv = Q[:, KC * T:2 * KC * T].rearrange("p (t c) -> p t c", t=TILES)
        gates = Q[:, 2 * KC * T:3 * KC * T].rearrange("p (h t) -> p h t", h=2 * HEADS)
        xn = Q[:, 2 * KC * T:3 * KC * T].rearrange("p (t c) -> p t c", t=TILES)
        g0 = 2 * KC * T
        raw = [Q[:, g0 + n * N_LAT:g0 + (n + 1) * N_LAT] for n in range(2)]
        rsin = Q[:, g0 + 2 * N_LAT:g0 + 3 * N_LAT]
        g4 = 4 * T
        gqk_f, cum_f, lx_f, lqk_f = (G[:, n * g4:(n + 1) * g4] for n in range(4))
        gqk, cum, lx, lqk = (v.rearrange("p (a g t) -> p a g t", a=2, g=2) for v in (gqk_f, cum_f, lx_f, lqk_f))
        att = G[:, 4 * g4:5 * g4].rearrange("p (t h q) -> p t h q", t=TILES, h=HEADS)
        kTok = H[:, 0:2048].rearrange("p (n g c) -> p n g c", n=8, g=2)
        gst = G[:, g4:g4 + 2048].rearrange("p (d n g e) -> p d n g e", d=2, n=4, g=2)
        gsout = G[:, g4 + 2048:g4 + 2560].rearrange("p (d g e) -> p d g e", d=2, g=2)
        strips = G[:, 0:4 * STRIP].rearrange("p (h x) -> p h x", h=HEADS)
        rc = G[:, 3584:3584 + R_END]
        qd = [G[:, 3584 + n * N_LAT:3584 + (n + 1) * N_LAT] for n in range(2)]
        stmp = [G[:, 6400 + n * STRIP:6400 + (n + 1) * STRIP] for n in range(2)]
        qtab = [G[:, 6400 + n * N_LAT:6400 + (n + 1) * N_LAT] for n in range(2)]
        rmask = G[:, 8192:8192 + 4096].rearrange("p (n s t) -> p n s t", n=2, s=LT)
        g1b = [G[:, n * D:(n + 1) * D] for n in range(2)]
        a2b = [G[:, (2 + n) * D:(3 + n) * D] for n in range(2)]
        b2b = [G[:, (4 + n) * D:(5 + n) * D] for n in range(2)]
        hn = [G[:, (6 + n) * D:(7 + n) * D] for n in range(2)]
        mt = [G[:, (8 + n) * D:(9 + n) * D] for n in range(2)]
        hnT = G[:, 10 * D:11 * D].rearrange("p (k t) -> p k t", k=KC)
        rtw = G[:, 11 * D:11 * D + KC * 36].rearrange("p (k n) -> p k n", k=KC)
        rk0 = 11 * D + KC * 36
        kones, ktri = G[:, rk0:rk0 + P], G[:, rk0 + P:rk0 + 2 * P]
        kiota = G[:, rk0 + 2 * P:rk0 + 2 * P + C_END - C_IOTA]
        rbias = G[:, rk0 + 400:rk0 + 436]
        lgt = G[:, rk0 + 440:rk0 + 440 + TILES * 36].rearrange("p (t n) -> p t n", t=TILES)
        g2b = [Q[:, 12288 + n * D:12288 + (n + 1) * D] for n in range(2)]
        fnb = Q[:, 12288 + 2 * D:12288 + 3 * D]
        exb = [Q[:, 0:3 * UNIT], Q[:, 3 * UNIT:6 * UNIT], W[:, 0:3 * UNIT], W[:, 3 * UNIT:6 * UNIT]]
        exg = [v[:, 0:UNIT].rearrange("p (k f) -> p k f", k=KC) for v in exb]
        exu = [v[:, UNIT:2 * UNIT].rearrange("p (k f) -> p k f", k=KC) for v in exb]
        exd = [v[:, 2 * UNIT:3 * UNIT].rearrange("p (j n) -> p j n", j=FC) for v in exb]
        xg = [H[0:SLOTS, n * D:(n + 1) * D] for n in range(4)]
        xte = [H[:, 4 * D + n * 512:4 * D + (n + 1) * 512].rearrange("p (k s) -> p k s", k=KC) for n in range(2)]
        yb = [G[0:SLOTS, (6 + n) * D:(7 + n) * D] for n in range(2)]
        sil = [G[:, 8 * D + n * P:8 * D + (n + 1) * P] for n in range(2)]
        hid = [G[:, 8 * D + (2 + n) * P:8 * D + (3 + n) * P].rearrange("p (j s) -> p j s", j=FC) for n in range(2)]
        yp = [[W[:, (2 * n + k) * D:(2 * n + k + 1) * D] for k in range(2)] for n in range(2)]
        yo = [W[:, (4 + n) * D:(5 + n) * D] for n in range(2)]

        cT, cS = small(2, KC), small(2, KC)
        modc, modr = small(64), small(P)
        brow = [small(P), small(P)]
        wrow = [small(P), small(P)]
        mcol = small(2 * 2, KC)
        ccol = small(C_END - C_IOTA)
        ss, rstd = small(TILES), small(TILES)
        lg = small(2, HEADS)
        gbias = small(2, 2)
        nw = small(2 * HEADS)
        tot, dec = small(4, TILES), small(4, TILES)
        wcol = small(2, HEADS)
        power = small(TILES)
        st1, st2, st3 = small(4), small(4), small(4)

        rdiff = rs(TILES * (NG + 1))
        oo = rs(TILES, NE)
        oh_slot = rs(2 * TILES, SLOTS)
        oh_block = rs(2 * TILES, BLOCKS)

        bank = [ctx.enter_context(nc.psum_tensor(f"bank{n}", [P, 512], F32)) for n in range(8)]
        mod_ps = bank[7]

        filled = [sem(f"bank{n}_filled") for n in range(NB1)]
        drained = [sem(f"bank{n}_drained") for n in range(NB1)]

        def where(job):
            n = job_at[job]
            return n % NB1, n // NB1

        def bk(job):
            return bank[where(job)[0]]

        def is_filled(eng, job):
            b, turn = where(job)
            eng.wait_ge(filled[b], turn + 1)

        def is_drained(eng, job):
            b, turn = where(job)
            eng.wait_ge(drained[b], turn + 1)

        def drains(ins, job):
            ins.then_inc(drained[where(job)[0]], 1)

        landed = [sem(f"ring{n}_landed") for n in range(RING)]
        w_used = sem("ring_used")
        s_cond, s_ident, s_tail, s_cols, s_gate, s_row = (
            sem(n) for n in ("cond_landed", "ident_landed", "tables_landed", "columns_landed", "gate_landed", "rows_landed"))
        s_x = [sem(f"x{t}_landed") for t in range(TILES)]
        s_modw = [sem(f"mod_written{n}") for n in range(2)]
        s_modl, s_mset = sem("mod_columns_landed"), sem("rows_set")
        s_gs0, s_rc, s_rs0 = sem("gla_states_landed"), sem("strip_inputs_landed"), sem("ret_states_landed")
        s_zero = sem("zeros_written")
        s_out = sem("outputs_written")
        s_bc, s_rt, s_fin = sem("norm2_rows_landed"), sem("router_landed"), sem("final_rows_landed")
        s_hnw = [sem(f"hn_written{n}") for n in range(2)]
        dve_chain, act_chain, pool_chain = sem("vector_chain"), sem("scalar_chain"), sem("gpsimd_chain")

        blocks = [("g", "ctx")] + [("g", h) for h in range(HEADS)] + [("r", "ctx")] + [("r", h) for h in range(HEADS)]
        NL = len(LEVELS)
        dve = Steps(sem("vector_steps"),
                    ["modc0", "ms0", "hT", "zb", "cum"] + [("lqk", n) for n in range(NL + 1)]
                    + ["qkF", "qkB"]
                    + [k for b in blocks[:5] for k in (("cen", b), ("ms", b), ("on", b))] + ["modc1"]
                    + [("strip", h) for h in range(HEADS)] + ["cmask", "kdec"]
                    + [k for k in sum([[("cen", ("r", "ctx")), ("ms", ("r", "ctx")), ("on", ("r", "ctx"))]] +
                                      [[("rm", h), ("cen", ("r", h)), ("ms", ("r", h)), ("on", ("r", h))] for h in range(HEADS)], [])]
                    + [k for t in range(TILES) for k in (("x2", t), ("ms2", t), ("hn", t))]
                    + ["diffs", "OO", "onehots", "idx", "dest"])
        act = Steps(sem("scalar_steps"),
                    ["cS"] + [("ss", t) for t in range(TILES)] + [("xn", t) for t in range(TILES)]
                    + ["lg", "softplus"] + [("exp", n) for n in range(NL)] + ["dec", "expF", "expB"]
                    + [("sq", b) for b in blocks[:5]] + ["wcol"]
                    + [("strip", h, d) for h in range(HEADS) for d in range(2)]
                    + [("sq", blocks[5])]
                    + sum([[("qtab", h), ("sq", ("r", h))] for h in range(HEADS)], [])
                    + [("ss2", t) for t in range(TILES)] + ["rexp"])
        pool_s = Steps(sem("gpsimd_steps"),
                     ["rs0"]
                     + sum([[("cos", i, c) for c in range(2)] + ([("sub", i - 3)] if i >= 3 else []) for i in range(3, 7)], [])
                     + [("sub", n) for n in range(4, NL)] + ["subF", "subB"] + [("rs", b) for b in blocks[:5]]
                     + [("sel", h, d) for h in range(HEADS) for d in range(2)]
                     + sum([[("qd", h), ("rs", blocks[5 + h])] for h in range(HEADS)], []) + [("rs", blocks[9])]
                     + [("rs2", t) for t in range(TILES)])
        pool_done = pool_s.done

        def w_src(n):
            slot = ring[n % RING]
            if n < ADA_FIRST:
                return w_ada[0, :, n * ITEM:(n + 1) * ITEM].rearrange("(p k) c -> p k c", k=KC), slot, ITEM
            n -= ADA_FIRST
            if n < len(IN_ITEMS):
                _, c0, w = IN_ITEMS[n]
                return w_in[0, :, c0:c0 + w].rearrange("(p k) c -> p k c", k=KC), slot[:, 0:KC * w], w
            n -= len(IN_ITEMS)
            if n < ADA_ALL - ADA_FIRST:
                c0 = (n + ADA_FIRST) * ITEM
                return w_ada[0, :, c0:c0 + ITEM].rearrange("(p k) c -> p k c", k=KC), slot, ITEM
            n -= ADA_ALL - ADA_FIRST
            return w_out[0, :, n * ITEM:(n + 1) * ITEM].rearrange("(k p) c -> p k c", k=KC), slot, ITEM

        IN0 = ADA_FIRST
        ADA1 = IN0 + len(IN_ITEMS)
        OUT0 = ADA1 + ADA_ALL - ADA_FIRST
        N_LOADS = OUT0 + D // ITEM

        def load_ready(eng, n):
            eng.wait_ge(landed[n % RING], 16 * (n // RING + 1))

        ex_landed = [sem(f"expert_weights{n}_landed") for n in range(4)]
        xg_landed = [sem(f"tokens{n}_landed") for n in range(4)]
        xg_turned, xte_ready, gu_filled = sem("tokens_turned"), sem("tokens_ready"), sem("gate_up_filled")
        sil_ready, hid_ready, y_filled = sem("silu_ready"), sem("hidden_ready"), sem("expert_done")
        y_half0, y_half1 = sem("y_half0"), sem("y_half1")
        ys_written = [sem(f"expert_rows_written{n}") for n in range(2)]
        ov_landed = sem("overflow_weights_landed")
        idxc_set = sem("slot_tokens_set")
        turns_begun, gathers_begun = sem("turns_begun"), sem("gathers_begun")
        yp_landed = [sem(f"pick_rows{n}_landed") for n in range(2)]
        y_used, x3_ready, ss3_ready, yo_ready = sem("picks_used"), sem("x3_ready"), sem("ss3_ready"), sem("final_ready")
        ms3_ready, rs3_ready = sem("final_squares_ready"), sem("final_roots_ready")
        yo_written = [sem(f"final_written{n}") for n in range(2)]

        block = ctx.enter_context(nc.Block())

        @block.sync
        def _(sp):
            for n in range(N_LOADS):
                src, dst, w = w_src(n)
                if n >= RING:
                    sp.wait_ge(w_used, n - RING + 1)
                sp.dma_start(dst.rearrange("p (k c) -> p k c", k=KC), src).then_inc(landed[n % RING], 16)

            def load_expert(e, b, s):
                sp.dma_start(exb[b][:, 0:UNIT], ewg_v[bass.ds(e * P, P), :]).then_inc(s, 16)
                sp.dma_start(exb[b][:, UNIT:2 * UNIT], ewu_v[bass.ds(e * P, P), :]).then_inc(s, 16)
                sp.dma_start(exb[b][:, 2 * UNIT:3 * UNIT], ewd_v[bass.ds(e * P, P), :]).then_inc(s, 16)

            ewg_v = ewg.rearrange("a e (p k) f -> (a e p) (k f)", p=P)
            ewu_v = ewu.rearrange("a e (p k) f -> (a e p) (k f)", p=P)
            ewd_v = ewd.rearrange("a e (p j) n -> (a e p) (j n)", p=P)
            is_drained(sp, ("rT", HEADS - 1))
            for b in range(2):
                load_expert(b, b, ex_landed[b])
            sp.wait_ge(w_used, N_LOADS)
            sp.wait_ge(s_out, 16 * 4)
            for b in range(2, 4):
                load_expert(b, b, ex_landed[b])
            with sp.Fori(1, NE // 4) as it:
                for b in range(4):
                    sp.wait_ge(y_filled, 4 * it + b - 3)
                    load_expert(4 * it + b, b, ex_landed[b])
            dve.wait(sp, "dest")
            n_over = sp.value_load(over[0:1, 0:1], min_val=0, max_val=MAX_OVER)
            with sp.If(n_over > 0):
                with sp.Fori(0, n_over) as i:
                    e = sp.value_load(over[0:1, bass.ds(i + 1, 1)], min_val=0, max_val=NE - 1)
                    sp.wait_ge(y_filled, NE + i)
                    load_expert(e, 0, ov_landed)
            ya = y_sample.rearrange("a t d -> (a t) d")
            yc = y_prompt.rearrange("a t d -> (a t) d")
            for t in range(TILES):
                sp.wait_ge(yo_ready, t + 1)
                dst = ya[t * P:(t + 1) * P, :] if t < LT else yc[:, :]
                sp.dma_start(dst, yo[t % 2]).then_inc(yo_written[t % 2], 16)
            sp.wait_ge(yo_written[0], 16 * 3)
            sp.wait_ge(yo_written[1], 16 * 2)
            sp.wait_ge(s_out, 16 * 4)

        @block.gpsimd
        def _(pool):
            chain = [0]

            def link(ins):
                chain[0] += 1
                ins.then_inc(pool_chain, 1)
                pool.wait_ge(pool_chain, chain[0])

            for n, half in enumerate((0, 1)):
                nch = 16 if n == 0 else 32
                link(nc.gpsimd.memset(wrow[n], 1.0))
                for cond in range(2):
                    pool.dma_start(brow[n][cond * nch:(cond + 1) * nch, :],
                                   b_ada[0, (0 if n == 0 else 2 * D):(2 * D if n == 0 else 6 * D)].rearrange("(c n) -> c n", n=P)
                                   ).then_inc(s_row, 16)
                    r0 = cond * nch + (8 if n == 0 else 16)
                    pool.dma_start(wrow[n][r0:r0 + 8, :],
                                   (norm1_w if n == 0 else norm2_w)[0].rearrange("(c n) -> c n", n=P)).then_inc(s_row, 16)
            with nc.allow_non_contiguous_dma(reason="small columns"):
                for d, v in enumerate((ggbf, ggbb)):
                    pool.dma_start(gbias[:, d, :], v[0].rearrange("(g p) -> p g", p=P)).then_inc(s_cols, 16)
                for d, v in enumerate((ret_norm_w, gla_norm_w)):
                    pool.dma_start(nw[:, 4 * d:4 * d + 4], v[0].rearrange("(h p) -> p h", p=P)).then_inc(s_cols, 16)
            for d, v in enumerate((rdf, rdb)):
                pool.dma_start(lg[:, d, :], v[0:1, :].partition_broadcast(P)).then_inc(s_cols, 16)
            link(nc.gpsimd.memset(wgate, 0.0))
            for d, v in enumerate((ggwf, ggwb)):
                pool.dma_start(wgate[RANK * d:RANK * (d + 1), d, :], v[0]).then_inc(s_gate, 16)
            link(nc.gpsimd.memset(power, -0.5))
            zero = onorm[0][0:SLOTS].rearrange("p a e -> p (a e)")
            link(nc.gpsimd.memset(zero, 0.0))
            for half in range(2):
                pool.dma_start(ys_dram[NE * SLOTS:, half * 512:(half + 1) * 512].rearrange("(b s) d -> s b d", s=SLOTS),
                               zero.unsqueeze(1).to_broadcast([SLOTS, MAX_OVER, 512])).then_inc(s_zero, 16)

            def root(ap, key, rkey):
                dve.wait(pool, key)
                pool_done(nc.gpsimd.tensor_tensor(ap, ap, power[:, 0:ap.shape[1]], ALU.pow), rkey)

            root(rstd, "ms0", "rs0")

            is_drained(pool, ("modT", 0))
            for cond in range(2):
                pool.dma_start(mod_dram[cond:cond + 1, 0:2 * D].rearrange("a (c n) -> (a c) n", n=P),
                               modr[cond * 16:(cond + 1) * 16, :]).then_inc(s_modw[0], 16)
            pool.wait_ge(s_modw[0], 32)
            for m in range(2):
                for cond in range(2):
                    pool.dma_start(mcol[:, 2 * m + cond, :],
                                   mod_dram[cond, m * D:(m + 1) * D].rearrange("(p k) -> p k", k=KC)).then_inc(s_modl, 16)

            def level_exponents(n):
                h = LEVELS[n]
                nb = T // (2 * h)
                v = [cum[:, d].rearrange("p g (b two h) -> p g b two h", two=2, h=h) for d in range(2)]
                o = [lx[:, a].rearrange("p g (b two h) -> p g b two h", two=2, h=h) for a in range(2)]
                shape = [P, 2, nb, h]
                ref = [v[0][:, :, :, 0, h - 1:h].to_broadcast(shape), v[1][:, :, :, 1, 0:1].to_broadcast(shape)]
                if n == 0:
                    dve.wait(pool, "cum")
                else:
                    dve.wait(pool, ("lqk", n - 1))
                nc.gpsimd.tensor_tensor(o[0][:, :, :, 1], v[0][:, :, :, 1], ref[0], ALU.subtract)
                nc.gpsimd.tensor_tensor(o[0][:, :, :, 0], ref[1], v[1][:, :, :, 0], ALU.subtract)
                nc.gpsimd.tensor_tensor(o[1][:, :, :, 0], ref[0], v[0][:, :, :, 0], ALU.subtract)
                pool_done(nc.gpsimd.tensor_tensor(o[1][:, :, :, 1], v[1][:, :, :, 1], ref[1], ALU.subtract), ("sub", n))

            pool.wait_ge(s_tail, 16 * 2)
            for i, (name, _, w) in enumerate(IN_ITEMS):
                if name in ("rq", "rk"):
                    for c in range(2):
                        a, h = ("rq", "rk").index(name), 2 * ((i - 3) % 2) + c
                        n = 2 * (i - 3) + c
                        is_drained(pool, ("p", i, c, "lat"))
                        pool_done(nc.gpsimd.tensor_tensor(rqk[:, a, h, 0:N_LAT], raw[n % 2], cosT, ALU.mult), ("cos", i, c))
                if 0 <= i - LEVEL_AFTER + 1 < NL:
                    level_exponents(i - LEVEL_AFTER + 1)
            tb = [tot[:, 2 * d:2 * d + 2, :].unsqueeze(3).to_broadcast([P, 2, TILES, P]) for d in range(2)]
            tv = [cum[:, d].rearrange("p g (t n) -> p g t n", n=P) for d in range(2)]
            ov = [lx[:, a].rearrange("p g (t n) -> p g t n", n=P) for a in range(2)]
            dve.wait(pool, ("lqk", NL - 1))
            pool_done(nc.gpsimd.tensor_tensor(ov[1], tb[0], tv[0], ALU.subtract), "subF")
            dve.wait(pool, "qkF")
            pool_done(nc.gpsimd.tensor_tensor(ov[0], tb[1], tv[1], ALU.subtract), "subB")
            act.wait(pool, "expB")
            for d, v in enumerate((sgf, sgb)):
                pool.dma_start(gst[:, d, 0], v[0, 0].rearrange("(g a) d e -> (a d) g e", a=2)).then_inc(s_gs0, 16)
            for b in blocks[:5]:
                root(st2, ("ms", b), ("rs", b))
            is_filled(pool, ("go", HEADS - 1))
            pool.wait_ge(s_out, 32)
            pool.dma_start(rc, rconsts[:, :]).then_inc(s_rc, 16)
            for d, v in enumerate((srf, srb)):
                pool.dma_start(rstate[:, d], v[0, 0].rearrange("h d e -> d h e")).then_inc(s_rs0, 16)
            for h in range(HEADS):
                for d in range(2):
                    o = strips[:, h, :] if d == 0 else stmp[h % 2]
                    act.wait(pool, ("strip", h, d))
                    sgn = 1 - 2 * d
                    pool_done(nc.gpsimd.affine_select(out=o, in_=o, compare_op=ALU.is_ge, fill=0.0,
                                                      base=-sgn * (N_LAT - P), pattern=[[sgn, STRIP]],
                                                      channel_multiplier=-sgn), ("sel", h, d))
            is_drained(pool, ("modT", 1))
            for cond in range(2):
                pool.dma_start(mod_dram[cond:cond + 1, 2 * D:6 * D].rearrange("a (c n) -> (a c) n", n=P),
                               modr[cond * 32:(cond + 1) * 32, :]).then_inc(s_modw[1], 16)
            for h in range(HEADS):
                act.wait(pool, ("qtab", h))
                if h >= 1:
                    is_filled(pool, ("ro", h - 1))
                link(nc.gpsimd.tensor_tensor(qd[0], rqk[:, 0, h, 0:N_LAT], qtab[0], ALU.mult))
                pool_done(nc.gpsimd.tensor_tensor(qd[1], rqk[:, 0, h, 0:N_LAT], qtab[1], ALU.mult), ("qd", h))
                root(st2, ("ms", blocks[5 + h]), ("rs", blocks[5 + h]))
            root(st2, ("ms", blocks[9]), ("rs", blocks[9]))
            is_filled(pool, ("ro", HEADS - 1))
            pool.wait_ge(s_modw[1], 32)
            for cond in range(2):
                for m, dst in ((2, g1b), (4, a2b), (3, b2b)):
                    pool.dma_start(dst[cond], mod_dram[cond:cond + 1, m * D:(m + 1) * D].partition_broadcast(P)).then_inc(s_bc, 16)
            pool.dma_start(rtw[:, :, 0:NG], rgw[0].rearrange("(p k) n -> p k n", k=KC)).then_inc(s_rt, 16)
            pool.dma_start(rtw[:, :, NG:NG + NE], rew[0].rearrange("(p k) n -> p k n", k=KC)).then_inc(s_rt, 16)
            pool.dma_start(G[:, rk0:rk0 + C_END - C_ONES], consts[:, C_ONES:C_END]).then_inc(s_rt, 16)
            pool.dma_start(rbias[:, 0:NG], rgb[0:1, :].partition_broadcast(P)).then_inc(s_rt, 16)
            pool.dma_start(rbias[:, NG:NG + NE], reb[0:1, :].partition_broadcast(P)).then_inc(s_rt, 16)
            is_drained(pool, ("rT", HEADS - 1))
            for cond in range(2):
                pool.dma_start(g2b[cond], mod_dram[cond:cond + 1, 5 * D:6 * D].partition_broadcast(P)).then_inc(s_fin, 16)
            pool.dma_start(fnb, final_w.rearrange("(a n) -> a n", a=1).partition_broadcast(P)).then_inc(s_fin, 16)

            for t in range(TILES):
                root(rstd[:, t:t + 1], ("ms2", t), ("rs2", t))

            def gather_block(col, b):
                nc.gpsimd.tensor_copy(idxc[b][:, :], idx[:, col]).then_inc(idxc_set, 1)

            def gather_rows(b, count):
                pool.wait_ge(idxc_set, count)
                pool.sem_inc(gathers_begun, 1)
                pool.indirect_dma_start(xg[b], None, hn_dram[:, :], bass.IndirectOffsetOnAxis(ap=idxc[b][:, :].bitcast(U32), axis=0)
                                        ).then_inc(xg_landed[b], 16)

            dve.wait(pool, "idx")
            for n in range(2):
                pool.wait_ge(s_hnw[n], 16 * (3 - n))
            is_filled(pool, ("mix", CTX, 3))
            for b in range(4):
                gather_block(slice(b, b + 1), b)
                gather_rows(b, b + 1)
            with pool.Fori(1, NE // 4) as it:
                for b in range(4):
                    pool.wait_ge(xg_turned, 4 * it + b - 3)
                    gather_block(bass.ds(4 * it + b, 1), b)
                    gather_rows(b, 4 * it + b + 1)
            pool.wait_ge(xg_turned, NE - 3)
            gather_block(slice(NE, NE + 1), 0)
            gather_rows(0, NE + 1)
            dve.wait(pool, "dest")
            n_over = pool.value_load(over[0:1, 0:1], min_val=0, max_val=MAX_OVER)
            with pool.If(n_over > 0):
                with pool.Fori(0, n_over) as i:
                    pool.wait_ge(xg_turned, NE + 1 + i)
                    gather_block(bass.ds(NE + i, 1), 0)
                    gather_rows(0, NE + 2 + i)
            link(nc.gpsimd.tensor_copy(destc[:, :], dest[:, :]))
            pool.wait_ge(ys_written[0], n_over * 16 + 16 * (NE // 2))
            pool.wait_ge(ys_written[1], 16 * (NE // 2))
            pool.wait_ge(y_filled, n_over + NE)
            pool.sem_inc(gathers_begun, 1)

            def final_root(t):
                pool.wait_ge(ms3_ready, t + 1)
                nc.gpsimd.tensor_tensor(rstd[:, t:t + 1], rstd[:, t:t + 1], power[:, 0:1], ALU.pow).then_inc(rs3_ready, 1)

            for t in range(TILES):
                if t >= 2:
                    pool.wait_ge(y_used, t - 1)
                for k in range(2):
                    pool.indirect_dma_start(yp[t % 2][k], None, ys_dram[:, :],
                                            bass.IndirectOffsetOnAxis(ap=destc[:, k * TILES + t:k * TILES + t + 1].bitcast(U32), axis=0)
                                            ).then_inc(yp_landed[t % 2], 16)
                if t >= 1:
                    final_root(t - 1)
            final_root(CTX)

        @block.scalar
        def _(sc):
            chain = [0]

            def link(ins):
                chain[0] += 1
                ins.then_inc(act_chain, 1)
                sc.wait_ge(act_chain, chain[0])

            f = nc.scalar.activation
            for cond, v in enumerate((c_in[0], c_ctx)):
                sc.dma_start(cT[:, cond, :], v.rearrange("(p k) -> p k", k=KC)).then_inc(s_cond, 16)
            sc.dma_start(ident[:, :], consts[:, C_IDENT:C_IDENT + P]).then_inc(s_ident, 16)
            xs = x_sample.rearrange("a t d -> (a t) d")
            for t in range(TILES):
                sc.dma_start(X[:, t, :], xs[t * P:(t + 1) * P, :] if t < LT else x_prompt[0]).then_inc(s_x[t], 16)
            sc.dma_start(ccol, consts[:, C_IOTA:C_END]).then_inc(s_ident, 16)
            sc.dma_start(tail[:, 0:2048], consts[:, C_ROT:C_ONES]).then_inc(s_tail, 16)
            sc.dma_start(ones_s, consts[:, C_ONES:C_ONES + P]).then_inc(s_tail, 16)
            sc.wait_ge(s_cond, 32)
            act.done(f(cS, cT, ACT.Silu), "cS")
            for t in range(TILES):
                sc.wait_ge(s_x[t], 16)
                act.done(f(xn[:, t, :], X[:, t, :], ACT.Square, accum_out=ss[:, t:t + 1]), ("ss", t))
            pool_s.wait(sc, "rs0")
            for t in range(TILES):
                act.done(f(xn[:, t, :].rearrange("p (k j) -> p k j", k=KC), X[:, t, :].rearrange("p (j k) -> p k j", k=KC),
                           ACT.Copy, scale=rstd[:, t:t + 1]), ("xn", t))
            sc.wait_ge(s_cols, 16 * 6)
            link(f(lg, lg, ACT.Exp))
            act.done(f(lg, lg, ACT.Copy, scale=-1.0), "lg")

            for i, (name, _, w) in enumerate(IN_ITEMS):
                if name in ("gv", "rv"):
                    off = (512 if name == "gv" else 0) + ITEM * ((i - 7) % 2)
                    for t in range(TILES):
                        is_filled(sc, ("v", i, t))
                        drains(f(vv[:, t, off:off + ITEM], bk(("v", i, t))[:, 0:ITEM], ACT.Copy), ("v", i, t))
                else:
                    for c in range(max(1, w // P)):
                        n = 2 * (i - 3) + c
                        for part, lo, hi in (("lat", 0, N_LAT), ("ctx", N_LAT, T)):
                            job = ("p", i, c, part)
                            src = bk(job)[:, 0:hi - lo]
                            is_filled(sc, job)
                            if name == "gq":
                                drains(f(gqk[:, 0, c, lo:hi], src, ACT.Copy, scale=GLA_DK ** -0.5), job)
                            elif name == "gk":
                                drains(f(gqk[:, 1, c, lo:hi], src, ACT.Copy), job)
                            elif name == "glr":
                                drains(f(glrT[:, lo:hi], src[0:2 * RANK, :], ACT.Copy), job)
                            elif name in ("rq", "rk"):
                                a, h = ("rq", "rk").index(name), 2 * ((i - 3) % 2) + c
                                s = float(P) ** -0.5 if a else 1.0
                                if part == "lat":
                                    if n == 0:
                                        is_filled(sc, ("xTc", 1))
                                    if n >= 2:
                                        j = (3 + (n - 2) // 2, (n - 2) % 2)
                                        pool_s.wait(sc, ("cos", *j))
                                        is_filled(sc, ("rot", *j))
                                    drains(f(raw[n % 2], src, ACT.Copy, scale=s), job)
                                else:
                                    drains(f(rqk[:, a, h, lo:hi], src, ACT.Copy, scale=s), job)
                            else:
                                h = 2 * ((i - 11) % 2) + c + (4 if name == "gr" else 0)
                                if i == 11 and c == 0 and part == "lat":
                                    is_drained(sc, ("rot", 6, 1))
                                drains(f(gates[:, h, lo:hi], src, ACT.Silu), job)
                if name == "glr":
                    dve.wait(sc, "zb")
                    link(f(lx_f, cum_f, ACT.Abs))
                    link(f(lx_f, lx_f, ACT.Exp, scale=-1.0))
                    act.done(f(lx_f, lx_f, ACT.Ln, bias=1.0), "softplus")
                n = i - LEVEL_AFTER + 1
                if 0 <= n < NL:
                    pool_s.wait(sc, ("sub", n))
                    act.done(f(lx_f, lx_f, ACT.Exp, scale=1.0 / 16.0), ("exp", n))
            act.done(f(dec, tot, ACT.Exp, scale=1.0 / 16.0), "dec")
            pool_s.wait(sc, "subF")
            link(f(lx[:, 1], lx[:, 1], ACT.Exp, scale=1.0 / 16.0))
            act.done(f(lx[:, 0], cum[:, 0], ACT.Exp, scale=1.0 / 16.0), "expF")
            pool_s.wait(sc, "subB")
            link(f(lx[:, 0], lx[:, 0], ACT.Exp, scale=1.0 / 16.0))
            act.done(f(lx[:, 1], cum[:, 1], ACT.Exp, scale=1.0 / 16.0), "expB")
            for d in range(2):
                for g in range(2):
                    job = ("kT", d, g)
                    is_filled(sc, job)
                    drains(f(kTok[:, 4 * d:4 * d + 4, g, :], bk(job)[:, :].rearrange("p (n c) -> p n c", n=4), ACT.Copy), job)
            for d, v in enumerate((new_gf, new_gb)):
                is_drained(sc, ("gu", d, 0))
                sc.dma_start(v[0, 0].rearrange("(g a) d e -> (a d) g e", a=2), gsout[:, d]).then_inc(s_out, 16)

            def square(b, n):
                dve.wait(sc, ("cen", b))
                act.done(f(sq, onorm[n % 2][:, :, :], ACT.Square), ("sq", b))

            for n in range(5):
                square(blocks[n], n)
            for d in range(2):
                for h in range(HEADS):
                    link(f(wcol[:, d, h:h + 1], ccol[:, C_POS - C_IOTA + 1 - d:C_POS - C_IOTA + 2 - d], ACT.Exp,
                           scale=lg[:, d, h:h + 1]))
            act.done(f(st3[:, 0:1], lg[:, 0, 0:1], ACT.Copy), "wcol")
            sc.wait_ge(s_rc, 16)
            for h in range(HEADS):
                for d in range(2):
                    o = strips[:, h, :] if d == 0 else stmp[h % 2]
                    if d == 1 and h >= 2:
                        dve.wait(sc, ("strip", h - 2))
                    act.done(f(o, rc[:, (R_RELF, R_RELB)[d]:(R_RELF, R_RELB)[d] + STRIP], ACT.Exp, scale=lg[:, d, h:h + 1]),
                             ("strip", h, d))
            for d, v in enumerate((new_rf, new_rb)):
                job = ("rst", d)
                is_filled(sc, job)
                drains(f(rsout[:, d], bk(job)[:, :].rearrange("p (h e) -> p h e", h=HEADS), ACT.Copy), job)
                is_drained(sc, job)
                sc.dma_start(v[0, 0].rearrange("h d e -> d h e"), rsout[:, d]).then_inc(s_out, 16)
            square(blocks[5], 5)
            for h in range(HEADS):
                if h == 0:
                    dve.wait(sc, ("strip", HEADS - 1))
                else:
                    pool_s.wait(sc, ("qd", h - 1))
                link(f(qtab[0], rc[:, R_TF:R_TF + N_LAT], ACT.Exp, scale=lg[:, 0, h:h + 1]))
                act.done(f(qtab[1], rc[:, R_TB:R_TB + N_LAT], ACT.Exp, scale=lg[:, 1, h:h + 1]), ("qtab", h))
                square(("r", h), 6 + h)
            for t in range(TILES):
                dve.wait(sc, ("x2", t))
                if t >= 2:
                    dve.wait(sc, ("hn", t - 2))
                act.done(f(mt[t % 2], X[:, t, :], ACT.Square, accum_out=ss[:, t:t + 1]), ("ss2", t))
                dve.wait(sc, ("hn", t))
                sc.dma_start(hn_dram[t * P:(t + 1) * P, :].rearrange("t d -> t d"), hn[t % 2]).then_inc(s_hnw[t % 2], 16)
                for half in range(2):
                    job = ("hT", t, half)
                    is_filled(sc, job)
                    if t >= 1:
                        is_filled(sc, ("lg", t - 1))
                    drains(f(hnT[:, 4 * half:4 * half + 4, :], bk(job)[:, :].rearrange("p (k t) -> p k t", k=4), ACT.Copy), job)
            dve.wait(sc, "diffs")
            act.done(f(rdiff, rdiff, ACT.Exp), "rexp")

            def turned_tokens(e, n, free):
                sc.wait_ge(xg_turned, e + 1)
                if free is not None:
                    sc.wait_ge(gu_filled, free)
                f(xte[n], bank[n][:, :].rearrange("p (k s) -> p k s", k=KC), ACT.Copy).then_inc(xte_ready, 1)

            def silu(e, n, free):
                sc.wait_ge(gu_filled, e + 1)
                if free is not None:
                    sc.wait_ge(hid_ready, free)
                f(sil[n], bank[2 + n][:, 0:P], ACT.Silu).then_inc(sil_ready, 1)

            def half_rows(e, n, row, written):
                sc.wait_ge(y_filled, e + 1)
                if written is not None:
                    sc.wait_ge(ys_written[n], written)
                f(yb[n][:, 0:512], bank[4 + 2 * n][0:SLOTS, :], ACT.Copy).then_inc(y_half0, 1)
                sc.wait_ge(y_half0, e + 1)
                sc.wait_ge(y_half1, e + 1)
                sc.dma_start(ys_dram[bass.ds(row, SLOTS), :], yb[n]).then_inc(ys_written[n], 16)

            def experts(it, first):
                for b in range(4):
                    e = 4 * it + b
                    silu(e, b % 2, None if first and b < 2 else e - 1)
                    turned_tokens(e + 1, (b + 1) % 2, None if first and b < 1 else e)
                    half_rows(e, b % 2, e * SLOTS, None if first and b < 2 else 32 * it + 16 * (b // 2))

            for h in range(2):
                sc.wait_ge(s_hnw[h], 16 * (3 - h))
            sc.wait_ge(s_zero, 32)
            turned_tokens(0, 0, None)
            experts(0, True)
            with sc.Fori(1, NE // 4) as it:
                experts(it, False)
            dve.wait(sc, "dest")
            n_over = sc.value_load(over[0:1, 0:1], min_val=0, max_val=MAX_OVER)
            with sc.If(n_over > 0):
                with sc.Fori(0, n_over) as i:
                    turned_tokens(NE + 1 + i, 0, NE + i)
                    silu(NE + i, 0, NE + i)
                    half_rows(NE + i, 0, (NE + i) * SLOTS, 16 * (NE // 2) + 16 * i)
            for t in range(TILES):
                sc.wait_ge(x3_ready, t + 1)
                if t >= 2:
                    sc.wait_ge(yo_written[t % 2], 16 * (t // 2))
                f(yo[t % 2], X[:, t, :], ACT.Square, accum_out=ss[:, t:t + 1]).then_inc(ss3_ready, 1)

        @block.vector
        def _(dv):
            chain = [0]

            def link(ins):
                chain[0] += 1
                ins.then_inc(dve_chain, 1)
                dv.wait_ge(dve_chain, chain[0])

            v = nc.vector

            def mean_square(out, total, n):
                return v.tensor_scalar(out, total, 1.0 / n, EPS, ALU.mult, ALU.add)

            def turned_mod(n):
                nch = (16, 32)[n]
                dv.wait_ge(w_used, (ADA_FIRST, OUT0)[n])
                dve.done(v.tensor_copy(modc[:, 0:2 * nch], mod_ps[:, 0:2 * nch]), f"modc{n}")
                if n == 0:
                    dv.wait_ge(s_row, 16 * 8)
                    dv.wait_ge(s_ident, 32)
                job = ("modT", n)
                is_filled(dv, job)
                if n == 1:
                    dv.wait_ge(s_modw[0], 32)
                r = slice(0, 2 * nch)
                link(v.tensor_tensor(modr[r, :], bk(job)[r, 0:P], brow[n][r, :], ALU.add))
                o = C_ONE - C_IOTA + n
                drains(v.scalar_tensor_tensor(modr[r, :], modr[r, :], ccol[r, o:o + 1], wrow[n][r, :], ALU.add, ALU.mult), job)

            turned_mod(0)
            act.wait(dv, ("ss", CTX))
            dve.done(mean_square(rstd, ss, D), "ms0")
            dv.wait_ge(s_modl, 16 * 4)
            for k in range(KC):
                job = ("xT", k)
                is_filled(dv, job)
                drains(v.tensor_scalar(hT[:, k, 0:N_LAT], bk(job)[:, :], mcol[:, 2, k:k + 1], mcol[:, 0, k:k + 1],
                                       ALU.mult, ALU.add), job)
            for half in range(2):
                job = ("xTc", half)
                is_filled(dv, job)
                for k in range(4 * half, 4 * half + 4):
                    ins = v.tensor_scalar(hT[:, k, N_LAT:T], bk(job)[:, (k % 4) * P:(k % 4 + 1) * P],
                                          mcol[:, 3, k:k + 1], mcol[:, 1, k:k + 1], ALU.mult, ALU.add)
                drains(ins, job)
            dve.done(v.tensor_copy(st3[:, 1:2], st3[:, 2:3]) if False else v.memset(st3[:, 1:2], 0.0), "hT")

            def level_scores(n):
                for m, (t0, t1) in enumerate(LEV_TILES):
                    for a in range(2):
                        job = ("lev", n, m, a)
                        is_filled(dv, job)
                        w = 2 * (t1 - t0) * P
                        src = bk(job)[:, 0:w].rearrange("p (t g q) -> p t g q", g=2, q=P)
                        dst = att[:, t0:t1, a::2, :]
                        if n == 0:
                            drains(v.tensor_copy(dst, src), job)
                        else:
                            mask = masks[n - 1].bitcast(U32).unsqueeze(1).unsqueeze(1).to_broadcast([P, t1 - t0, 2, P])
                            if (m, a) == (0, 0):
                                is_drained(dv, ("lev", n - 1, 2, 1))
                            drains(v.copy_predicated(dst, mask, src), job)

            for i, (name, _, w) in enumerate(IN_ITEMS):
                if name == "glr":
                    dv.wait_ge(s_cols, 16 * 6)
                    for d in range(2):
                        for g in range(2):
                            for part, lo, hi in (("lat", 0, N_LAT), ("ctx", N_LAT, T)):
                                job = ("z", d, g, part)
                                is_filled(dv, job)
                                ins = v.tensor_scalar(cum[:, d, g, lo:hi], bk(job)[:, 0:hi - lo], gbias[:, d, g:g + 1], None, ALU.add)
                                drains(ins, job)
                    is_drained(dv, ("z", 1, 1, "ctx"))
                    dve.done(v.memset(st3[:, 2:3], 0.0), "zb")
                    act.wait(dv, "softplus")
                    link(v.scalar_tensor_tensor(lqk_f, cum_f, 0.0, lx_f, ALU.min, ALU.subtract))
                    dv.wait_ge(s_tail, 32)
                    for d in range(2):
                        for g in range(2):
                            for t in range(TILES):
                                tt = slice(t * P, (t + 1) * P)
                                ins = v.tensor_tensor_scan(cum[:, d, g, tt], ones_s, lqk[:, d, g, tt], 0.0, ALU.mult, ALU.add)
                    link(ins)
                    link(v.tensor_copy(tot, cum_f.rearrange("p (a t n) -> p a t n", a=4, n=P)[:, :, :, P - 1]))
                    dve.done(v.tensor_tensor(cum[:, 1], cum[:, 1], lqk[:, 1], ALU.subtract), "cum")
                if rots_after(i, 0) is not None or i in (3, 4, 5, 6):
                    for c in range(2):
                        j = rots_after(i, c)
                        if j is None:
                            continue
                        a, h = ("rq", "rk").index(IN_ITEMS[j[0]][0]), 2 * ((j[0] - 3) % 2) + j[1]
                        job = ("rot", *j)
                        is_filled(dv, job)
                        link(v.tensor_tensor(rsin, bk(job)[:, :], sinT, ALU.mult))
                        pool_s.wait(dv, ("cos", *j))
                        drains(v.tensor_tensor(rqk[:, a, h, 0:N_LAT], rqk[:, a, h, 0:N_LAT], rsin, ALU.add), job)
                        is_drained(dv, job)
                n = i - LEVEL_AFTER
                if 0 <= n <= NL:
                    level_scores(n)
                if 0 <= n + 1 < NL:
                    act.wait(dv, ("exp", n + 1))
                    if n >= 0:
                        is_filled(dv, ("lev", n, 2, 1))
                    dve.done(v.tensor_tensor(lqk_f, gqk_f, lx_f, ALU.mult), ("lqk", n + 1))
                elif n + 1 == NL:
                    is_filled(dv, ("lev", n, 2, 1))
                    dve.done(v.tensor_scalar(lqk[:, 0], gqk[:, 0], 2.0, None, ALU.mult), ("lqk", NL))
            act.wait(dv, "expF")
            is_filled(dv, ("lev", NL, 2, 1))
            dve.done(v.tensor_tensor(lqk_f, gqk_f, lx_f, ALU.mult), "qkF")
            act.wait(dv, "expB")
            dve.done(v.tensor_tensor(lx_f, gqk_f, lx_f, ALU.mult), "qkB")
            dv.wait_ge(s_gs0, 32)
            for n in range(4):
                for d in range(2):
                    job = ("gu", d, n)
                    is_filled(dv, job)
                    src = bk(job)[:, 0:2 * P].rearrange("p (g e) -> p g e", g=2)
                    if n == 0:
                        drains(v.tensor_copy(gsout[:, d], src), job)
                        continue
                    t = (n - 1, LT - n)[d]
                    if n >= 2:
                        is_drained(dv, ("gu", d, n - 1))
                    link(v.scalar_tensor_tensor(gst[:, d, n, 0], gst[:, d, n - 1, 0], dec[:, 2 * d, t:t + 1], src[:, 0],
                                                ALU.mult, ALU.add))
                    ins = v.scalar_tensor_tensor(gst[:, d, n, 1], gst[:, d, n - 1, 1], dec[:, 2 * d + 1, t:t + 1], src[:, 1],
                                                 ALU.mult, ALU.add)
                    drains(ins, job)

            def turn_job(b):
                return ("gT" if b[0] == "g" else "rT", b[1])

            def normalise(b, n):
                job = ("go" if b[0] == "g" else "ro", b[1])
                is_filled(dv, job)
                if n >= 2:
                    is_filled(dv, turn_job(blocks[n - 2]))
                src, o = bk(job)[:, :].rearrange("p (a e) -> p a e", a=4), onorm[n % 2][:, :, :]
                if b[0] == "r":
                    link(v.tensor_reduce(st1, src, AX, ALU.add))
                    link(v.tensor_scalar(st1, st1, 1.0 / P, None, ALU.mult))
                    link(v.tensor_tensor(o, src, st1.unsqueeze(2).to_broadcast([P, 4, P]), ALU.subtract))
                else:
                    link(v.tensor_copy(o, src))
                drains(v.memset(st1, 0.0), job)
                is_drained(dv, job)
                dve.done(v.memset(st3[:, 3:4], 0.0), ("cen", b))
                act.wait(dv, ("sq", b))
                link(v.tensor_reduce(st2, sq, AX, ALU.add))
                dve.done(mean_square(st2, st2, P), ("ms", b))
                pool_s.wait(dv, ("rs", b))
                dve.done(v.tensor_tensor(o, o, st2.unsqueeze(2).to_broadcast([P, 4, P]), ALU.mult), ("on", b))

            def gate_block(b):
                job = turn_job(b)
                is_filled(dv, job)
                h0 = 4 if b[0] == "g" else 0
                if b[1] == "ctx":
                    for h in range(HEADS):
                        ins = v.scalar_tensor_tensor(hT[:, h0 + h, N_LAT:T], bk(job)[:, h * P:(h + 1) * P], nw[:, h0 + h:h0 + h + 1],
                                                     gates[:, h0 + h, N_LAT:T], ALU.mult, ALU.mult)
                    drains(ins, job)
                else:
                    h = h0 + b[1]
                    drains(v.scalar_tensor_tensor(hT[:, h, 0:N_LAT], bk(job)[:, :], nw[:, h:h + 1], gates[:, h, 0:N_LAT],
                                                  ALU.mult, ALU.mult), job)

            dv.wait_ge(s_zero, 32)
            normalise(blocks[0], 0)
            for n in range(1, 5):
                normalise(blocks[n], n)
                gate_block(blocks[n - 1])
            gate_block(blocks[4])
            turned_mod(1)
            for h in range(HEADS):
                pool_s.wait(dv, ("sel", h, 1))
                dve.done(v.tensor_tensor(strips[:, h, :], strips[:, h, :], stmp[h % 2], ALU.add), ("strip", h))
            dve.wait(dv, ("strip", HEADS - 1))
            job = ("rs", "ctx")
            is_filled(dv, job)
            drains(v.tensor_tensor(cmask, bk(job)[:, :].rearrange("p (h t) -> p h t", h=HEADS),
                                   strips[:, :, N_LAT - P:N_LAT], ALU.mult), job)
            is_drained(dv, job)
            dve.done(v.memset(st3[:, 0:1], 0.0), "cmask")
            job = ("rkT",)
            is_filled(dv, job)
            act.wait(dv, "wcol")
            for d in range(2):
                link(v.tensor_tensor(kdec[:, d], bk(job)[:, :].rearrange("p (h c) -> p h c", h=HEADS),
                                     wcol[:, d].unsqueeze(2).to_broadcast([P, HEADS, P]), ALU.mult))
            drains(v.memset(st3[:, 1:2], 0.0), job)
            dve.done(v.memset(st3[:, 2:3], 0.0), "kdec")
            normalise(blocks[5], 5)
            for h in range(HEADS):
                for s in range(LT):
                    job = ("rs", h, s)
                    is_filled(dv, job)
                    if h >= 2:
                        is_filled(dv, ("ro", h - 2))
                    x0 = N_LAT - P - s * P
                    drains(v.tensor_tensor(rmask[:, h % 2, s], bk(job)[:, :], strips[:, h, x0:x0 + N_LAT], ALU.mult), job)
                is_drained(dv, job)
                dve.done(v.memset(st3[:, 3:4], 0.0), ("rm", h))
                gate_block(blocks[5 + h])
                normalise(blocks[6 + h], 6 + h)
            gate_block(blocks[9])

            dv.wait_ge(s_bc, 16 * 6)
            dv.wait_ge(s_rt, 16 * 5)
            for t in range(TILES):
                cond = int(t == CTX)
                for n in range(4):
                    job = ("mix", t, n)
                    cc = slice(n * ITEM, (n + 1) * ITEM)
                    is_filled(dv, job)
                    drains(v.tensor_tensor(mt[t % 2][:, cc], bk(job)[:, 0:ITEM], g1b[cond][:, cc], ALU.mult), job)
                is_drained(dv, job)
                dve.done(v.tensor_tensor(X[:, t, :], X[:, t, :], mt[t % 2], ALU.add), ("x2", t))
                act.wait(dv, ("ss2", t))
                dve.done(mean_square(rstd[:, t:t + 1], ss[:, t:t + 1], D), ("ms2", t))
                pool_s.wait(dv, ("rs2", t))
                link(v.scalar_tensor_tensor(mt[t % 2], X[:, t, :], rstd[:, t:t + 1], a2b[cond], ALU.mult, ALU.mult))
                if t >= 2:
                    is_filled(dv, ("hT", t - 2, 1))
                    dv.wait_ge(s_hnw[t % 2], 16 * (t // 2))
                o = hn[t % 2].rearrange("p (k j) -> p k j", k=KC)
                dve.done(v.tensor_tensor(o, mt[t % 2].rearrange("p (j k) -> p k j", k=KC),
                                         b2b[cond].rearrange("p (j k) -> p k j", k=KC), ALU.add), ("hn", t))
                if t >= 1:
                    job = ("lg", t - 1)
                    is_filled(dv, job)
                    drains(v.tensor_tensor(lgt[:, t - 1, :], bk(job)[:, 0:36], rbias, ALU.add), job)
            job = ("lg", CTX)
            is_filled(dv, job)
            drains(v.tensor_tensor(lgt[:, CTX, :], bk(job)[:, 0:36], rbias, ALU.add), job)
            is_drained(dv, job)

            def bc(ap, n):
                return ap.unsqueeze(2).to_broadcast([P, ap.shape[1], n])

            def iota(n, rows=TILES):
                return kiota[:, 0:n].unsqueeze(1).to_broadcast([P, rows, n])

            def first_max(x, n):
                m, eq, i = rs(TILES), rs(TILES, n), rs(TILES)
                link(v.tensor_reduce(m, x, AX, ALU.max))
                link(v.tensor_tensor(eq, x, bc(m, n), ALU.is_equal))
                link(v.scalar_tensor_tensor(eq, eq, -100.0, iota(n), ALU.mult, ALU.add))
                link(v.tensor_reduce(i, eq, AX, ALU.min))
                link(v.tensor_scalar(i, i, 100.0, None, ALU.add))
                link(v.tensor_tensor(eq, iota(n), bc(i, n), ALU.is_equal))
                return m, i, eq

            gl = lgt[:, :, 0:NG]
            gm, gi, g_hot = first_max(gl, NG)
            gd = rdiff[:, 0:TILES * NG].rearrange("p (t g) -> p t g", t=TILES)
            link(v.tensor_tensor(gd, gl, bc(gm, NG), ALU.subtract))
            em, es = rs(TILES, NG, EPG), rs(TILES, EPG)
            for t in range(TILES):
                ins = v.tensor_tensor(em[:, t], lgt[:, t, NG:].rearrange("p (g j) -> p g j", g=NG), bc(g_hot[:, t], EPG), ALU.mult)
            link(ins)
            for t in range(TILES):
                ins = v.tensor_reduce(es[:, t], em[:, t].rearrange("p g j -> p j g"), AX, ALU.add)
            link(ins)
            m1, i1, hot1 = first_max(es, EPG)
            es2 = rs(TILES, EPG)
            link(v.scalar_tensor_tensor(es2, hot1, -3.0e38, es, ALU.mult, ALU.add))
            m2, i2, _ = first_max(es2, EPG)
            dve.done(v.tensor_tensor(rdiff[:, TILES * NG:], m2, m1, ALU.subtract), "diffs")
            pk_e, hot = rs(2 * TILES), rs(2 * TILES, NE)
            for k, i in enumerate((i1, i2)):
                link(v.scalar_tensor_tensor(pk_e[:, k * TILES:(k + 1) * TILES], gi, float(EPG), i, ALU.mult, ALU.add))
            link(v.tensor_tensor(hot, iota(NE, 2 * TILES), bc(pk_e, NE), ALU.is_equal))
            dve.done(v.tensor_tensor(oo, hot[:, 0:TILES], hot[:, TILES:], ALU.add), "OO")
            job = ("pos",)
            is_filled(dv, job)
            place = rs(TILES + 1, NE)
            drains(v.tensor_copy(place, bk(job)[:, 0:(TILES + 1) * NE].rearrange("p (t e) -> p t e", e=NE)), job)
            is_drained(dv, job)
            count = place[:, TILES]
            tmp = rs(2 * TILES, NE)
            for k in range(2):
                ks = slice(k * TILES, (k + 1) * TILES)
                link(v.tensor_tensor(tmp[:, ks], hot[:, ks], place[:, 0:TILES], ALU.mult))
            pk_p, q, slot = rs(2 * TILES), rs(2 * TILES), rs(2 * TILES)
            link(v.tensor_reduce(pk_p, tmp, AX, ALU.add))
            steps9 = kiota[:, 64:73]
            cmp9, n_ov, ov_end, ov_at = rs(NE, 9), rs(NE), rs(NE), rs(NE)
            link(v.tensor_tensor(cmp9, bc(count, 9), steps9.unsqueeze(1).to_broadcast([P, NE, 9]), ALU.is_gt))
            link(v.tensor_reduce(n_ov, cmp9, AX, ALU.add))
            link(v.tensor_tensor_scan(ov_end, kones[:, 0:NE], n_ov, 0.0, ALU.mult, ALU.add))
            link(v.tensor_tensor(ov_at, ov_end, n_ov, ALU.subtract))
            c2 = rs(2 * TILES, 9)
            link(v.tensor_tensor(c2, bc(pk_p, 9), steps9.unsqueeze(1).to_broadcast([P, 2 * TILES, 9]), ALU.is_ge))
            link(v.tensor_reduce(q, c2, AX, ALU.add))
            link(v.scalar_tensor_tensor(slot, q, -float(SLOTS), pk_p, ALU.mult, ALU.add))
            link(v.tensor_tensor(tmp, hot, ov_at.unsqueeze(1).to_broadcast([P, 2 * TILES, NE]), ALU.mult))
            va, blk, row = rs(2 * TILES), rs(2 * TILES), rs(2 * TILES)
            link(v.tensor_reduce(va, tmp, AX, ALU.add))
            link(v.tensor_tensor(va, va, q, ALU.add))
            link(v.scalar_tensor_tensor(va, va, float(NE - 1), pk_e, ALU.add, ALU.subtract))
            link(v.tensor_scalar(q, q, 1.0, None, ALU.min))
            link(v.tensor_tensor(va, va, q, ALU.mult))
            link(v.tensor_tensor(blk, va, pk_e, ALU.add))
            link(v.scalar_tensor_tensor(row, blk, float(SLOTS), slot, ALU.mult, ALU.add))
            link(v.tensor_tensor(oh_slot, iota(SLOTS, 2 * TILES), bc(slot, SLOTS), ALU.is_equal))
            link(v.tensor_tensor(oh_block, iota(BLOCKS, 2 * TILES), bc(blk, BLOCKS), ALU.is_equal))
            tok = kiota[:, C_TOK - C_IOTA:C_TOK - C_IOTA + TILES]
            for k in range(2):
                ks = slice(k * TILES, (k + 1) * TILES)
                ins = v.tensor_tensor(oh_block[:, ks], oh_block[:, ks], bc(tok, BLOCKS), ALU.mult)
            dve.done(ins, "onehots")
            job = ("idx",)
            is_filled(dv, job)
            drains(v.tensor_copy(idx[:, :], bk(job)[0:SLOTS, 0:BLOCKS]), job)
            is_drained(dv, job)
            dve.done(v.memset(st3[:, 3:4], 0.0), "idx")
            link(v.tensor_copy(dest[:, :], row))
            link(v.tensor_copy(over[0:1, 0:1], ov_end[0:1, NE - 1:NE]))
            cmpo, eob = rs(MAX_OVER, NE), rs(MAX_OVER)
            link(v.tensor_tensor(cmpo[0:1], ov_end[0:1].unsqueeze(1).to_broadcast([1, MAX_OVER, NE]),
                                 kiota[0:1, 0:MAX_OVER].unsqueeze(2).to_broadcast([1, MAX_OVER, NE]), ALU.is_le))
            link(v.tensor_reduce(eob[0:1], cmpo[0:1], AX, ALU.add))
            link(v.tensor_scalar(over[0:1, 1:], eob[0:1], float(NE - 1), None, ALU.min))
            act.wait(dv, "rexp")
            gs, p2 = rs(TILES), rdiff[:, TILES * NG:]
            link(v.tensor_reduce(gs, gd, AX, ALU.add))
            den = rs(TILES)
            link(v.tensor_scalar(den, p2, 1.0, None, ALU.add))
            link(v.tensor_tensor(den, den, gs, ALU.mult))
            link(v.reciprocal(pickw[:, 0, :], den))
            link(v.tensor_tensor(pickw[:, 1, :], pickw[:, 0, :], p2, ALU.mult))
            dve.done(v.memset(st3[:, 0:1], 0.0), "dest")

            def hidden(e, n, free):
                dv.wait_ge(sil_ready, e + 1)
                if free is not None:
                    dv.wait_ge(y_filled, free)
                v.tensor_tensor(hid[n], sil[n].rearrange("p (j s) -> p j s", j=FC),
                                bank[2 + n][:, P:2 * P].rearrange("p (j s) -> p j s", j=FC), ALU.mult).then_inc(hid_ready, 1)

            def half_rows(e, n, written):
                dv.wait_ge(y_filled, e + 1)
                if written is not None:
                    dv.wait_ge(ys_written[n], written)
                v.tensor_copy(yb[n][:, 512:D], bank[5 + 2 * n][0:SLOTS, :]).then_inc(y_half1, 1)

            def experts(it, first):
                for b in range(4):
                    e = 4 * it + b
                    hidden(e, b % 2, None if first and b < 2 else e - 1)
                    half_rows(e, b % 2, None if first and b < 2 else 32 * it + 16 * (b // 2))

            for h in range(2):
                dv.wait_ge(s_hnw[h], 16 * (3 - h))
            experts(0, True)
            with dv.Fori(1, NE // 4) as it:
                experts(it, False)
            n_over = dv.value_load(over[0:1, 0:1], min_val=0, max_val=MAX_OVER)
            with dv.If(n_over > 0):
                with dv.Fori(0, n_over) as i:
                    hidden(NE + i, 0, NE + i)
                    half_rows(NE + i, 0, 16 * (NE // 2) + 16 * i)
            dv.wait_ge(s_fin, 16 * 3)
            for t in range(TILES):
                cond = int(t == CTX)
                y1, y2 = yp[t % 2]
                dv.wait_ge(yp_landed[t % 2], 32 * (t // 2 + 1))
                link(v.tensor_scalar(y1, y1, pickw[:, 0, t:t + 1], None, ALU.mult))
                link(v.scalar_tensor_tensor(y2, y2, pickw[:, 1, t:t + 1], y1, ALU.mult, ALU.add))
                link(v.tensor_tensor(y2, y2, g2b[cond], ALU.mult))
                link(v.tensor_tensor(X[:, t, :], X[:, t, :], y2, ALU.add))
                v.memset(st3[:, 0:1], 0.0).then_inc(y_used, 1)
                v.memset(st3[:, 1:2], 0.0).then_inc(x3_ready, 1)
                dv.wait_ge(ss3_ready, t + 1)
                mean_square(rstd[:, t:t + 1], ss[:, t:t + 1], D).then_inc(ms3_ready, 1)
                dv.wait_ge(rs3_ready, t + 1)
                v.scalar_tensor_tensor(yo[t % 2], X[:, t, :], rstd[:, t:t + 1], fnb, ALU.mult, ALU.mult).then_inc(yo_ready, 1)

        @block.tensor
        def _(te):
            order = [0]

            def starts(job):
                assert JOBS[order[0]] == job, (JOBS[order[0]], job)
                order[0] += 1
                b, turn = where(job)
                if turn:
                    te.wait_ge(drained[b], turn)
                return bank[b]

            def fills(ins, job):
                ins.then_inc(filled[where(job)[0]], 1)

            mm, tr = nc.tensor.matmul, nc.tensor.transpose

            def turn_small(n):
                nch = (16, 32)[n]
                dve.wait(te, f"modc{n}")
                if n == 0:
                    te.wait_ge(s_ident, 32)
                ps = starts(("modT", n))
                fills(tr(ps[0:2 * nch, 0:P], modc[:, 0:2 * nch], ident[:, :]), ("modT", n))

            def modulation(n, first, chunk, nch, slot):
                w = ring[slot].rearrange("p (k c) -> p k c", k=KC)
                for c in range(2):
                    o = mod_ps[:, 0:2 * nch].rearrange("p (a n) -> p a n", a=2)[:, :, bass.ds(chunk + c, 1)]
                    for k in range(KC):
                        ins = mm(o, w[:, k, c * P:(c + 1) * P], cS[:, :, k:k + 1], start=(k == 0), stop=(k == KC - 1))
                ins.then_inc(w_used, 1)

            act.wait(te, "cS")
            with te.Fori(0, ADA_FIRST // RING) as it:
                for b in range(RING):
                    te.wait_ge(landed[b], 16 * it + 16)
                    modulation(b, 0, 8 * it + 2 * b, 16, b)
            turn_small(0)
            act.wait(te, ("xn", CTX))
            for k in range(KC):
                ps = starts(("xT", k))
                for t in range(LT):
                    ins = tr(ps[:, t * P:(t + 1) * P], xn[:, t, k * P:(k + 1) * P], ident[:, :])
                fills(ins, ("xT", k))
            for half in range(2):
                ps = starts(("xTc", half))
                for k in range(4 * half, 4 * half + 4):
                    ins = tr(ps[:, (k % 4) * P:(k % 4 + 1) * P], xn[:, CTX, k * P:(k + 1) * P], ident[:, :])
                fills(ins, ("xTc", half))

            def rotate(i, c):
                job = ("rot", i, c)
                is_drained(te, ("p", i, c, "lat"))
                if (i, c) == (3, 0):
                    te.wait_ge(s_tail, 32)
                ps = starts(job)
                fills(mm(ps[:, :], rot_m, raw[(2 * (i - 3) + c) % 2], start=True, stop=True), job)

            dve.wait(te, "hT")
            for i, (name, _, w) in enumerate(IN_ITEMS):
                n = IN0 + i
                load_ready(te, n)
                wt = ring[n % RING][:, 0:KC * w].rearrange("p (k c) -> p k c", k=KC)
                if name in ("gv", "rv"):
                    if rots_after(i, 0) is not None:
                        rotate(*rots_after(i, 0))
                    for t in range(TILES):
                        ps = starts(("v", i, t))
                        for k in range(KC):
                            ins = mm(ps[:, 0:ITEM], hT[:, k, t * P:(t + 1) * P], wt[:, k, :], start=(k == 0), stop=(k == KC - 1))
                        if t < CTX:
                            fills(ins, ("v", i, t))
                    fills(ins, ("v", i, CTX))
                    is_filled(te, ("v", i, CTX))
                    te.sem_inc(w_used, 1)
                else:
                    for c in range(max(1, w // P)):
                        m = min(P, w)
                        for part, lo, hi in (("lat", 0, N_LAT), ("ctx", N_LAT, T)):
                            ps = starts(("p", i, c, part))
                            for k in range(KC):
                                ins = mm(ps[0:m, 0:hi - lo], wt[:, k, c * m:(c + 1) * m], hT[:, k, lo:hi],
                                         start=(k == 0), stop=(k == KC - 1))
                            fills(ins, ("p", i, c, part))
                        if rots_after(i, c) is not None:
                            rotate(*rots_after(i, c))
                    is_filled(te, ("p", i, c, "ctx"))
                    te.sem_inc(w_used, 1)
                if name == "glr":
                    te.wait_ge(s_gate, 32)
                    is_drained(te, ("p", i, 0, "ctx"))
                    is_drained(te, ("p", i, 0, "lat"))
                    for d in range(2):
                        for g in range(2):
                            for part, lo, hi in (("lat", 0, N_LAT), ("ctx", N_LAT, T)):
                                job = ("z", d, g, part)
                                ps = starts(job)
                                fills(mm(ps[:, 0:hi - lo], wgate[:, d, g * P:(g + 1) * P], glrT[:, lo:hi], start=True, stop=True), job)
                n = i - LEVEL_AFTER
                if 0 <= n <= NL:
                    dve.wait(te, ("lqk", n))
                    for m, (t0, t1) in enumerate(LEV_TILES):
                        for a in range(2):
                            job = ("lev", n, m, a)
                            ps = starts(job)
                            pp = slice(GLA_DK * a, GLA_DK * (a + 1))
                            for t in range(t0, t1):
                                for g in range(2):
                                    tt, o = slice(t * P, (t + 1) * P), (2 * (t - t0) + g) * P
                                    keys = (lqk if n < NL else gqk)[pp, 1, g, tt]
                                    ins = mm(ps[:, o:o + P], keys, lqk[pp, 0, g, tt], start=True, stop=True)
                            fills(ins, job)

            for d in range(2):
                dve.wait(te, ("qkF", "qkB")[d])
                for g in range(2):
                    job = ("kT", d, g)
                    ps = starts(job)
                    for n in range(4):
                        t = CTX if n == 0 else (n - 1, LT - n)[d]
                        ins = tr(ps[:, n * P:(n + 1) * P], (lqk, lx)[d][:, 1, g, t * P:(t + 1) * P], ident[:, :])
                    fills(ins, job)
            for n in range(4):
                for d in range(2):
                    if n == 0:
                        is_drained(te, ("kT", d, 0))
                        is_drained(te, ("kT", d, 1))
                    job = ("gu", d, n)
                    ps = starts(job)
                    t = CTX if n == 0 else (n - 1, LT - n)[d]
                    for h in range(HEADS):
                        g, a = h // 2, h % 2
                        ins = mm(ps[GLA_DK * a:GLA_DK * (a + 1), g * P:(g + 1) * P],
                                 kTok[:, 4 * d + n, g, GLA_DK * a:GLA_DK * (a + 1)],
                                 vv[:, t, 512 + h * P:512 + (h + 1) * P], start=True, stop=True)
                    fills(ins, job)

            def turn_block(b, n):
                job = ("gT" if b[0] == "g" else "rT", b[1])
                dve.wait(te, ("on", b))
                ps = starts(job)
                for a in range(4):
                    ins = tr(ps[:, a * P:(a + 1) * P], onorm[n % 2][:, a, :], ident[:, :])
                fills(ins, job)

            ps = starts(("go", "ctx"))
            for h in range(HEADS):
                ins = mm(ps[:, h * P:(h + 1) * P], att[:, CTX, h, :], vv[:, CTX, 512 + h * P:512 + (h + 1) * P], start=True, stop=True)
            fills(ins, ("go", "ctx"))
            te.wait_ge(s_gs0, 32)
            for d in range(2):
                is_drained(te, ("gu", d, 3))
            for h in range(HEADS):
                g, pp = h // 2, slice(GLA_DK * (h % 2), GLA_DK * (h % 2 + 1))
                ps = starts(("go", h))
                for t in range(LT):
                    o, tt = ps[:, t * P:(t + 1) * P], slice(t * P, (t + 1) * P)
                    mm(o, att[:, t, h, :], vv[:, t, 512 + h * P:512 + (h + 1) * P], start=True, stop=False)
                    mm(o, lqk[pp, 0, g, tt], gst[pp, 0, t, g, :], start=False, stop=False)
                    ins = mm(o, lx[pp, 0, g, tt], gst[pp, 1, LT - 1 - t, g, :], start=False, stop=True)
                fills(ins, ("go", h))
                turn_block(blocks[h], h)
            turn_block(blocks[4], 4)
            a0 = ADA1 % RING
            with te.Fori(0, (ADA_ALL - ADA_FIRST) // RING) as it:
                for b in range(RING):
                    te.wait_ge(landed[(a0 + b) % RING], 16 * it + 16 * ((ADA1 + b) // RING + 1))
                    modulation(b, 0, 8 * it + 2 * b, 32, (a0 + b) % RING)
            turn_small(1)

            job = ("rs", "ctx")
            ps = starts(job)
            for h in range(HEADS):
                ins = mm(ps[:, h * P:(h + 1) * P], rqk[:, 1, h, N_LAT:T], rqk[:, 0, h, N_LAT:T], start=True, stop=True)
            fills(ins, job)
            ps = starts(("rkT",))
            for h in range(HEADS):
                ins = tr(ps[:, h * P:(h + 1) * P], rqk[:, 1, h, N_LAT:T], ident[:, :])
            fills(ins, ("rkT",))
            dve.wait(te, "kdec")
            for d in range(2):
                ps = starts(("rst", d))
                for h in range(HEADS):
                    ins = mm(ps[:, h * P:(h + 1) * P], kdec[:, d, h, :], vv[:, CTX, h * P:(h + 1) * P], start=True, stop=True)
                fills(ins, ("rst", d))
            ps = starts(("ro", "ctx"))
            for h in range(HEADS):
                ins = mm(ps[:, h * P:(h + 1) * P], cmask[:, h, :], vv[:, CTX, h * P:(h + 1) * P], start=True, stop=True)
            fills(ins, ("ro", "ctx"))
            te.wait_ge(s_rs0, 32)
            for h in range(HEADS):
                for s in range(LT):
                    job = ("rs", h, s)
                    ps = starts(job)
                    fills(mm(ps[:, :], rqk[:, 1, h, s * P:(s + 1) * P], rqk[:, 0, h, 0:N_LAT], start=True, stop=True), job)
                turn_block(blocks[5 + h], 5 + h)
                dve.wait(te, ("rm", h))
                pool_s.wait(te, ("qd", h))
                ps = starts(("ro", h))
                for t in range(LT):
                    o, tt = ps[:, t * P:(t + 1) * P], slice(t * P, (t + 1) * P)
                    for s in range(LT):
                        mm(o, rmask[:, h % 2, s, tt], vv[:, s, h * P:(h + 1) * P], start=(s == 0), stop=False)
                    for d in range(2):
                        ins = mm(o, qd[d][:, tt], rstate[:, d, h, :], start=False, stop=(d == 1))
                fills(ins, ("ro", h))
            turn_block(blocks[9], 9)

            def router(t):
                dve.wait(te, ("hn", t))
                for half in range(2):
                    ps = starts(("hT", t, half))
                    for k in range(4 * half, 4 * half + 4):
                        ins = tr(ps[:, (k % 4) * P:(k % 4 + 1) * P], hn[t % 2][:, k * P:(k + 1) * P], ident[:, :])
                    fills(ins, ("hT", t, half))
                te.wait_ge(s_rt, 16 * 5)
                ps = starts(("lg", t))
                for half in range(2):
                    is_drained(te, ("hT", t, half))
                for k in range(KC):
                    ins = mm(ps[:, 0:36], hnT[:, k, :], rtw[:, k, :], start=(k == 0), stop=(k == KC - 1))
                fills(ins, ("lg", t))

            is_drained(te, ("rT", HEADS - 1))
            for t in range(TILES):
                for n in range(4):
                    load_ready(te, OUT0 + n)
                    wt = ring[(OUT0 + n) % RING].rearrange("p (k c) -> p k c", k=KC)
                    ps = starts(("mix", t, n))
                    for k in range(KC):
                        ins = mm(ps[:, 0:ITEM], hT[:, k, t * P:(t + 1) * P], wt[:, k, :], start=(k == 0), stop=(k == KC - 1))
                    fills(ins, ("mix", t, n))
                if t >= 1:
                    router(t - 1)
                if t == CTX:
                    is_filled(te, ("mix", CTX, 3))
                    for n in range(4):
                        te.sem_inc(w_used, 1)
            router(CTX)
            dve.wait(te, "OO")
            ps = starts(("pos",))
            for t in range(TILES):
                o = ps[:, t * NE:(t + 1) * NE]
                for s in range(t):
                    mm(o, kones, oo[:, s, :], start=(s == 0), stop=False)
                mm(o, ktri, oo[:, t, :], start=(t == 0), stop=True)
            for s in range(TILES):
                ins = mm(ps[:, TILES * NE:(TILES + 1) * NE], kones, oo[:, s, :], start=(s == 0), stop=(s == TILES - 1))
            fills(ins, ("pos",))
            dve.wait(te, "onehots")
            ps = starts(("idx",))
            for n in range(2 * TILES):
                ins = mm(ps[0:SLOTS, 0:BLOCKS], oh_slot[:, n, :], oh_block[:, n, :], start=(n == 0), stop=(n == 2 * TILES - 1))
            fills(ins, ("idx",))
            assert order[0] == len(JOBS)
            for j in JOBS[-NB1:]:
                is_drained(te, j)

            def turn_tokens(e, n, b, gathered, free):
                te.wait_ge(xg_landed[b], gathered)
                if free is not None:
                    te.wait_ge(xte_ready, free)
                te.sem_inc(turns_begun, 1)
                for k in range(KC):
                    ins = tr(bank[n][:, k * SLOTS:(k + 1) * SLOTS], xg[b][:, k * P:(k + 1) * P], ident[0:SLOTS, 0:SLOTS])
                ins.then_inc(xg_turned, 1)

            def gate_up(e, n, b, free):
                te.wait_ge(xte_ready, e + 1)
                if free is not None:
                    te.wait_ge(hid_ready, free)
                for a, w in enumerate((exg[b], exu[b])):
                    for j in range(FC):
                        o = bank[2 + n][:, (2 * a + j) * SLOTS:(2 * a + j + 1) * SLOTS]
                        for k in range(KC):
                            ins = mm(o, w[:, k, j::FC], xte[n][:, k, :], start=(k == 0), stop=(k == KC - 1))
                ins.then_inc(gu_filled, 1)

            def down(e, n, b, free):
                te.wait_ge(hid_ready, e + 1)
                if free is not None:
                    te.wait_ge(y_half0, free)
                    te.wait_ge(y_half1, free)
                for half in range(2):
                    for j in range(FC):
                        ins = mm(bank[4 + 2 * n + half][0:SLOTS, :], hid[n][:, j, :], exd[b][:, j, half * 512:(half + 1) * 512],
                                 start=(j == 0), stop=(j == FC - 1))
                ins.then_inc(y_filled, 1)

            def experts(it, first):
                for b in range(4):
                    e = 4 * it + b
                    te.wait_ge(ex_landed[b], 48 * it + 48)
                    gate_up(e, b % 2, b, None if first and b < 2 else e - 1)
                    nb = (b + 1) % 4
                    turn_tokens(e + 1, (b + 1) % 2, nb, 16 * it + (16 if b < 3 else 32), None if first and b == 0 else e)
                    down(e, b % 2, b, None if first and b < 2 else e - 1)

            turn_tokens(0, 0, 0, 16, None)
            experts(0, True)
            with te.Fori(1, NE // 4) as it:
                experts(it, False)
            dve.wait(te, "dest")
            n_over = te.value_load(over[0:1, 0:1], min_val=0, max_val=MAX_OVER)
            with te.If(n_over > 0):
                with te.Fori(0, n_over) as i:
                    turn_tokens(NE + 1 + i, 0, 0, 16 * (NE // 4 + 2) + 16 * i, NE + 1 + i)
                    te.wait_ge(ov_landed, 48 * i + 48)
                    te.wait_ge(xte_ready, NE + 2 + i)
                    for a, w in enumerate((exg[0], exu[0])):
                        for j in range(FC):
                            o = bank[2][:, (2 * a + j) * SLOTS:(2 * a + j + 1) * SLOTS]
                            for k in range(KC):
                                ins = mm(o, w[:, k, j::FC], xte[0][:, k, :], start=(k == 0), stop=(k == KC - 1))
                    ins.then_inc(gu_filled, 1)
                    down(NE + i, 0, 0, NE + i)


def host_constants():
    import numpy as np
    f = np.float32
    c = np.zeros((P, C_END), f)
    c[:, C_IDENT:C_IDENT + P] = np.eye(P)
    half, quarter = P // 2, P // 4
    rot = np.zeros((P, P), f)
    for base in (0, half):
        for i in range(quarter):
            rot[base + quarter + i, base + i] = -1.0
            rot[base + i, base + quarter + i] = 1.0
    c[:, C_ROT:C_ROT + P] = rot
    freqs = f(10000.0) ** (-np.arange(quarter, dtype=f) / f(quarter))
    t = np.arange(N_LAT)
    pos = np.stack([(t // GRID_W).astype(f), (t % GRID_W).astype(f)])
    for p in range(P):
        ang = (pos[p // half] * freqs[p % quarter]).astype(f)
        c[p, C_COS:C_COS + N_LAT] = np.cos(ang)
        c[p, C_SIN:C_SIN + N_LAT] = np.sin(ang)
    i, j = np.arange(P)[:, None], np.arange(P)[None, :]
    for n, h in enumerate(LEVELS[1:]):
        c[:, C_MASK + n * P:C_MASK + (n + 1) * P] = (i // (2 * h) == j // (2 * h)) & (i // h != j // h)
    c[:, C_MASK + 6 * P:C_MASK + 7 * P] = np.eye(P)
    c[:, C_ONES:C_ONES + P] = 1.0
    c[:, C_TRI:C_TRI + P] = i < j
    c[:, C_IOTA:C_IOTA + 64] = np.arange(64)
    c[:, C_IOTA + 64:C_IOTA + 73] = SLOTS * np.arange(1, 10)
    c[:, C_TOK:C_TOK + TILES] = np.arange(P)[:, None] + P * np.arange(TILES)
    c[:, C_POS] = np.arange(P)
    c[:, C_POS + 1] = P - 1 - np.arange(P)
    for n, (nch, first) in enumerate(((16, 8), (32, 16))):
        r = np.arange(P) % nch
        c[:, C_ONE + n] = (r >= first) & (r < first + 8) & (np.arange(P) < 2 * nch)
    rc = np.zeros((P, R_END), f)
    rel = (np.arange(STRIP)[None, :] - np.arange(P)[:, None] - (N_LAT - P)).astype(f)
    rc[:, R_RELF:R_RELF + STRIP] = np.maximum(rel, 0)
    rc[:, R_RELB:R_RELB + STRIP] = np.maximum(-rel, 0)
    rc[:, R_TF:R_TF + N_LAT] = t + 1
    rc[:, R_TB:R_TB + N_LAT] = N_LAT - t
    return c, rc


_INS = ["x_prompt", "x_sample", "state_ret_fwd", "state_ret_bwd", "state_gla_fwd", "state_gla_bwd", "c", "c_ctx",
        "w_ada", "b_ada", "norm1_w", "w_in", "ret_decay_fwd", "ret_decay_bwd", "ret_norm_w", "gla_gate_w_fwd",
        "gla_gate_b_fwd", "gla_gate_w_bwd", "gla_gate_b_bwd", "gla_norm_w", "w_out", "norm2_w", "router_group_w",
        "router_group_b", "router_expert_w", "router_expert_b", "expert_w_gate", "expert_w_up", "expert_w_down",
        "final_norm_w"]
_OUTS = [(1, N_CTX, D), (1, N_LAT, D), (1, 1, HEADS, P, P), (1, 1, HEADS, P, P), (1, 1, HEADS, GLA_DK, P),
         (1, 1, HEADS, GLA_DK, P)]


def kernel(**inputs):
    import numpy as np
    import concourse.bacc as bacc
    from concourse.bass_utils import run_bass_kernel_spmd

    nc = bacc.Bacc("TRN2", target_bir_lowering=False, num_devices=1)
    arrays, ins = {}, []
    given = [(name, np.ascontiguousarray(inputs[name])) for name in _INS]
    for name, a in given + list(zip(("consts", "rconsts"), host_constants())):
        arrays[f"in_{name}"] = a
        ins.append(nc.dram_tensor(f"in_{name}", a.shape, mybir.dt.from_np(a.dtype), kind="ExternalInput").ap())
    outs = [nc.dram_tensor(f"out_{i}", shape, F32, kind="ExternalOutput").ap() for i, shape in enumerate(_OUTS)]
    build(nc, ins, outs)
    r = run_bass_kernel_spmd(nc, [arrays], core_ids=[0])
    return tuple(r.results[0][f"out_{i}"] for i in range(len(_OUTS)))
```

```python
from contextlib import ExitStack

import concourse.bass as bass
from concourse import mybir

P = 128
D = 1024
KC = D // P
N_LAT = 512
N_CTX = 128
T = N_LAT + N_CTX
TILES = T // P
CTX = TILES - 1
LT = N_LAT // P
HEADS = 4
GLA_DK = 64
GRID_W = 64
RANK = 16
NE = 32
NG = 4
EPG = NE // NG
DE = 256
FC = DE // P
SLOTS = 64
MAX_OVER = 19
BLOCKS = NE + MAX_OVER
EPS = 1e-6
ITEM = 256
UNIT = KC * ITEM
RING = 4
STRIP = N_LAT + N_LAT - P
LEVELS = [64, 32, 16, 8, 4, 2, 1]
LEV_TILES = [(0, 2), (2, 4), (4, 5)]
IN_COLS = 3616

IN_ITEMS = [("gq", 2048, 256), ("gk", 2304, 256), ("glr", 3584, 32),
            ("rq", 0, 256), ("rq", 256, 256), ("rk", 512, 256), ("rk", 768, 256),
            ("gv", 2560, 256), ("gv", 2816, 256), ("rv", 1024, 256), ("rv", 1280, 256),
            ("gr", 3072, 256), ("gr", 3328, 256), ("rg", 1536, 256), ("rg", 1792, 256)]
IN_BASE = {"gq": 2048, "gk": 2304, "rq": 0, "rk": 512, "gv": 2560, "rv": 1024, "gr": 3072, "rg": 1536, "glr": 3584}
CARRY_AFTER = 12
LEVEL_AFTER = 4

C_IDENT, C_ROT, C_COS, C_SIN, C_MASK = 0, 128, 256, 768, 1280
C_ONES = C_MASK + 7 * P
C_TRI = C_ONES + P
C_IOTA = C_TRI + P
C_TOK = C_IOTA + 64 + 9
C_POS = C_TOK + TILES
C_ONE = C_POS + 2
C_END = C_ONE + 1
R_RELF, R_RELB, R_TF, R_TB = 0, STRIP, 2 * STRIP, 2 * STRIP + N_LAT
R_END = 2 * STRIP + 2 * N_LAT

F32 = mybir.dt.float32
I32 = mybir.dt.int32
U32 = mybir.dt.uint32
ALU = mybir.AluOpType
ACT = mybir.ActivationFunctionType
AX = mybir.AxisListType.X


class Steps:

    def __init__(self, sem, order):
        self.sem, self.order, self.n = sem, list(order), 0

    def done(self, ins, key):
        assert self.order[self.n] == key, (self.order[self.n], key)
        self.n += 1
        ins.then_inc(self.sem, 1)

    def wait(self, eng, key):
        eng.wait_ge(self.sem, self.order.index(key) + 1)


def rots_after(i, c):
    seq = [(i, c) for i in range(3, 7) for c in range(2)] + [(7, 0)]
    return seq[seq.index((i, c)) - 1] if (i, c) in seq[1:] else None


def plan_loads():
    loads = [("ada", m, i) for m in range(2) for i in range(4)]
    rest = [("ada", m, i) for m in range(2, 6) for i in range(4)]
    for i in range(len(IN_ITEMS)):
        loads += [("in", i), rest.pop(0)]
    return loads + rest + [("out", n) for n in range(D // ITEM)]


def plan_banks():
    jobs = [("xT", k) for k in range(KC)] + [("xTc", 0), ("xTc", 1)]
    for i, (name, _, w) in enumerate(IN_ITEMS):
        if name in ("gv", "rv"):
            if rots_after(i, 0) is not None:
                jobs.append(("rot", *rots_after(i, 0)))
            jobs += [("v", i, t) for t in range(TILES)]
        else:
            for c in range(max(1, w // P)):
                jobs += [("p", i, c, "lat"), ("p", i, c, "ctx")]
                if rots_after(i, c) is not None:
                    jobs.append(("rot", *rots_after(i, c)))
        if name == "glr":
            jobs += [("z", d, g, part) for d in range(2) for g in range(2) for part in ("lat", "ctx")]
        n = i - LEVEL_AFTER
        if 0 <= n <= len(LEVELS):
            jobs += [("lev", n, m, a) for m in range(len(LEV_TILES)) for a in range(2)]
        if i == CARRY_AFTER + 1:
            jobs += [("kT", d, g) for d in range(2) for g in range(2)]
            jobs += [("gu", d, n) for n in range(4) for d in range(2)]
    jobs += [("modT",)]
    jobs += [job for job, _ in plan_outputs()]
    for t in range(TILES):
        jobs += [("mix", t, n) for n in range(4)]
        if t >= 1:
            jobs += [("hT", t - 1, 0), ("hT", t - 1, 1), ("lg", t - 1)]
    jobs += [("hT", CTX, 0), ("hT", CTX, 1), ("lg", CTX)]
    jobs += [("pos",), ("idx",)]
    return jobs


def plan_outputs():
    order = [("o", "g", "ctx"), ("rs", "ctx"), ("o", "g", 0), ("T", "g", "ctx"), ("rkT",), ("o", "g", 1), ("T", "g", 0),
             ("rst", 0), ("rst", 1), ("o", "g", 2), ("T", "g", 1)] + [("rs", 0, s) for s in range(LT)]
    order += [("o", "g", 3), ("T", "g", 2), ("o", "r", "ctx"), ("T", "g", 3), ("o", "r", 0)]
    for h in range(1, HEADS):
        order += [("rs", h, s) for s in range(LT)] + [("T", "r", "ctx" if h == 1 else h - 2), ("o", "r", h)]
    order += [("T", "r", 2), ("T", "r", 3)]
    return [(job, job[1:] if job[0] in "oT" else None) for job in order]


BLOCKS_OUT = [block for job, block in plan_outputs() if job[0] == "o"]


def build(nc, inp, outs):
    (x_prompt, x_sample, srf, srb, sgf, sgb, c_in, c_ctx, w_ada, b_ada, norm1_w, w_in, rdf, rdb,
     ret_norm_w, ggwf, ggbf, ggwb, ggbb, gla_norm_w, w_out, norm2_w, rgw, rgb, rew, reb,
     ewg, ewu, ewd, final_w, consts, rconsts) = inp
    y_prompt, y_sample, new_rf, new_rb, new_gf, new_gb = outs

    JOBS, LOADS = plan_banks(), plan_loads()
    NB1 = 7
    job_at = {j: n for n, j in enumerate(JOBS)}
    assert len(job_at) == len(JOBS)

    with ExitStack() as ctx:
        def sb(name, shape, dt=F32):
            return ctx.enter_context(nc.sbuf_tensor(name, shape, dt))

        def sem(name):
            return ctx.enter_context(nc.semaphore(name))

        mod_dram = nc.dram_tensor("mod_rows", (2, 6 * D), F32).ap()
        hn_dram = nc.dram_tensor("hn_rows", (T, D), F32).ap()
        ys_dram = nc.dram_tensor("expert_rows", (BLOCKS * SLOTS, D), F32).ap()

        W = sb("weights", [P, 6 * UNIT])
        X = sb("x_rows", [P, TILES, D])
        H = sb("h_cols", [P, KC * T])
        Q = sb("qkv_gates", [P, 3 * KC * T])
        G = sb("attention", [P, 5 * 4 * T])
        ident = sb("ident", [P, P])
        r_used = [0]

        def rs(*shape):
            n = 1
            for v in shape:
                n *= v
            ap = G[:, 5 * D + r_used[0]:5 * D + r_used[0] + n]
            r_used[0] += n
            return ap if len(shape) == 1 else ap.rearrange("p (a b) -> p a b", a=shape[0]) if len(shape) == 2 else \
                ap.rearrange("p (a b c) -> p a b c", a=shape[0], b=shape[1])

        onorm = [sb(f"onorm{n}", [P, 4, P]) for n in range(2)]
        idx = sb("slot_tokens", [SLOTS, BLOCKS], I32)
        idxc = [sb(f"slot_tokens_now{n}", [SLOTS, 1], I32) for n in range(4)]
        dest = sb("pick_rows", [P, 2 * TILES], I32)
        destc = sb("pick_rows_now", [P, 2 * TILES], I32)
        pickw = sb("pick_weights", [P, 2, TILES])
        over = sb("overflow", [1, 1 + MAX_OVER], I32)

        S = sb("small", [P, 1000])
        at = [0]

        def small(*shape):
            n = 1
            for v in shape:
                n *= v
            ap = S[:, at[0]:at[0] + n]
            at[0] += n
            if len(shape) == 2:
                ap = ap.rearrange("p (a b) -> p a b", a=shape[0])
            if len(shape) == 3:
                ap = ap.rearrange("p (a b c) -> p a b c", a=shape[0], b=shape[1])
            return ap

        ring = [W[:, u * UNIT:(u + 1) * UNIT] for u in range(RING)]
        tail = W[:, RING * UNIT:6 * UNIT]
        rot_m = tail[:, 0:P]
        cosT, sinT = tail[:, P:P + N_LAT], tail[:, P + N_LAT:P + 2 * N_LAT]
        masks = [tail[:, P + 2 * N_LAT + n * P:P + 2 * N_LAT + (n + 1) * P] for n in range(7)]
        glrT = tail[0:2 * RANK, 2048:2048 + T]
        wgate = tail[0:2 * RANK, 2688:3200].rearrange("p (d n) -> p d n", d=2)
        ones_s = tail[:, 3200:3328]
        sq = tail[:, 3584:4096].rearrange("p (a b) -> p a b", a=4)
        rstate = tail[:, 0:1024].rearrange("p (d h e) -> p d h e", d=2, h=HEADS)
        kdec = tail[:, 1024:2048].rearrange("p (d h e) -> p d h e", d=2, h=HEADS)
        rsout = tail[:, 2048:3072].rearrange("p (d h e) -> p d h e", d=2, h=HEADS)
        cmask = tail[:, 3072:3584].rearrange("p (h t) -> p h t", h=HEADS)

        hT = H[:, :].rearrange("p (k t) -> p k t", k=KC)
        rqk = Q[:, 0:KC * T].rearrange("p (a h t) -> p a h t", a=2, h=HEADS)
        vv = Q[:, KC * T:2 * KC * T].rearrange("p (t c) -> p t c", t=TILES)
        gates = Q[:, 2 * KC * T:3 * KC * T].rearrange("p (h t) -> p h t", h=2 * HEADS)
        xn = Q[:, 2 * KC * T:3 * KC * T].rearrange("p (t c) -> p t c", t=TILES)
        g0 = 2 * KC * T
        raw = [Q[:, g0 + n * N_LAT:g0 + (n + 1) * N_LAT] for n in range(2)]
        rsin = Q[:, g0 + 2 * N_LAT:g0 + 3 * N_LAT]
        g4 = 4 * T
        gqk_f, cum_f, lx_f, lqk_f = (G[:, n * g4:(n + 1) * g4] for n in range(4))
        gqk, cum, lx, lqk = (v.rearrange("p (a g t) -> p a g t", a=2, g=2) for v in (gqk_f, cum_f, lx_f, lqk_f))
        att = G[:, 4 * g4:5 * g4].rearrange("p (t h q) -> p t h q", t=TILES, h=HEADS)
        kTok = tail[:, 0:2048].rearrange("p (n g c) -> p n g c", n=8, g=2)
        gst = G[:, g4:g4 + 2048].rearrange("p (d n g e) -> p d n g e", d=2, n=4, g=2)
        gsout = G[:, g4 + 2048:g4 + 2560].rearrange("p (d g e) -> p d g e", d=2, g=2)
        xf = X[:, :, :].rearrange("p t c -> p (t c)")
        strips = xf[:, 0:4 * STRIP].rearrange("p (h x) -> p h x", h=HEADS)
        tft = [xf[:, 4 * STRIP + n * N_LAT:4 * STRIP + (n + 1) * N_LAT] for n in range(2)]
        rel = [Q[:, g0 + 3 * N_LAT + n * STRIP:g0 + 3 * N_LAT + (n + 1) * STRIP] for n in range(2)]
        stmp = [Q[:, g0 + 3 * N_LAT + n * STRIP:g0 + 3 * N_LAT + (n + 1) * STRIP] for n in range(2, 4)]
        qd = [G[:, n * N_LAT:(n + 1) * N_LAT] for n in range(2)]
        qtab = [G[:, (2 + n) * N_LAT:(3 + n) * N_LAT] for n in range(2)]
        rmask = [v.rearrange("p (s t) -> p s t", s=LT)
                 for v in (H[:, 0:2048], G[:, g4:g4 + 2048], G[:, g4 + 2048:g4 + 4096], G[:, g4:g4 + 2048])]
        hnT = G[:, 0:D].rearrange("p (k t) -> p k t", k=KC)
        mt = [G[:, (1 + n) * D:(2 + n) * D] for n in range(2)]
        hn = [G[:, (3 + n) * D:(4 + n) * D] for n in range(2)]
        a2b = [G[:, (5 + n) * D:(6 + n) * D] for n in range(2)]
        g1b = [G[:, (7 + n) * D:(8 + n) * D] for n in range(2)]
        b2b = [G[:, (9 + n) * D:(10 + n) * D] for n in range(2)]
        rtw = G[:, 11 * D:11 * D + KC * 36].rearrange("p (k n) -> p k n", k=KC)
        rk0 = 11 * D + KC * 36
        kones, ktri = G[:, rk0:rk0 + P], G[:, rk0 + P:rk0 + 2 * P]
        kiota = G[:, rk0 + 2 * P:rk0 + 2 * P + C_END - C_IOTA]
        rbias = G[:, rk0 + 400:rk0 + 436]
        lgt = G[:, rk0 + 440:rk0 + 440 + TILES * 36].rearrange("p (t n) -> p t n", t=TILES)
        g2b = [Q[:, 12288 + n * D:12288 + (n + 1) * D] for n in range(2)]
        fnb = Q[:, 12288 + 2 * D:12288 + 3 * D]
        exb = [Q[:, 0:3 * UNIT], Q[:, 3 * UNIT:6 * UNIT], W[:, 0:3 * UNIT], W[:, 3 * UNIT:6 * UNIT]]
        exg = [v[:, 0:UNIT].rearrange("p (k f) -> p k f", k=KC) for v in exb]
        exu = [v[:, UNIT:2 * UNIT].rearrange("p (k f) -> p k f", k=KC) for v in exb]
        exd = [v[:, 2 * UNIT:3 * UNIT].rearrange("p (j n) -> p j n", j=FC) for v in exb]
        xg = [H[0:SLOTS, n * D:(n + 1) * D] for n in range(4)]
        xte = [H[:, 4 * D + n * 512:4 * D + (n + 1) * 512].rearrange("p (k s) -> p k s", k=KC) for n in range(2)]
        yb = [G[0:SLOTS, (3 + n) * D:(4 + n) * D] for n in range(2)]
        sil = [G[:, D + n * P:D + (n + 1) * P] for n in range(2)]
        hid = [G[:, D + (2 + n) * P:D + (3 + n) * P].rearrange("p (j s) -> p j s", j=FC) for n in range(2)]
        yp = [[W[:, (2 * n + k) * D:(2 * n + k + 1) * D] for k in range(2)] for n in range(2)]
        yo = [W[:, (4 + n) * D:(5 + n) * D] for n in range(2)]

        cT, cS = small(2, KC), small(2, KC)
        modc, modr = small(64), small(P)
        brow, wrow = small(P), small(P)
        bcol, n1col = small(2, KC), small(KC)
        mcol = small(2 * 2, KC)
        ccol = small(C_END - C_IOTA)
        ss, rstd = small(TILES), small(TILES)
        lg = small(2, HEADS)
        gbias = small(2, 2)
        nw = small(2 * HEADS)
        tot, dec = small(4, TILES), small(4, TILES)
        wcol = small(2, HEADS)
        power = small(TILES)
        st1, st2, st3 = small(4), small(4), small(4)

        rdiff = rs(TILES * (NG + 1))
        oo = rs(TILES, NE)
        oh_slot = rs(2 * TILES, SLOTS)
        oh_block = rs(2 * TILES, BLOCKS)

        bank = [ctx.enter_context(nc.psum_tensor(f"bank{n}", [P, 512], F32)) for n in range(8)]
        mod_ps = bank[7]

        filled = [sem(f"bank{n}_filled") for n in range(NB1)]
        drained = [sem(f"bank{n}_drained") for n in range(NB1)]

        def where(job):
            n = job_at[job]
            return n % NB1, n // NB1

        def bk(job):
            return bank[where(job)[0]]

        def is_filled(eng, job):
            b, turn = where(job)
            eng.wait_ge(filled[b], turn + 1)

        def is_drained(eng, job):
            b, turn = where(job)
            eng.wait_ge(drained[b], turn + 1)

        def drains(ins, job):
            ins.then_inc(drained[where(job)[0]], 1)

        landed = [sem(f"ring{n}_landed") for n in range(RING)]
        ada_used = sem("ada_used")
        s_cond, s_ident, s_tail, s_cols, s_gate, s_row = (
            sem(n) for n in ("cond_landed", "ident_landed", "tables_landed", "columns_landed", "gate_landed", "rows_landed"))
        s_x = [sem(f"x{t}_landed") for t in range(TILES)]
        s_x2 = [sem(f"x{t}_again") for t in range(TILES)]
        s_modw = sem("mod_written")
        s_gs0, s_rc, s_rs0 = sem("gla_states_landed"), sem("strip_inputs_landed"), sem("ret_states_landed")
        s_zero, s_mrow = sem("zeros_written"), sem("mod_rows_landed")
        s_out = sem("outputs_written")
        s_bc, s_rt, s_fin = sem("norm2_rows_landed"), sem("router_landed"), sem("final_rows_landed")
        s_hnw = [sem(f"hn_written{n}") for n in range(2)]
        dve_chain, act_chain, pool_chain = sem("vector_chain"), sem("scalar_chain"), sem("gpsimd_chain")

        NL = len(LEVELS)
        dve_order = ["ms0", "mcol", "hT", "zb", "cum"]
        act_order = ["cS"] + [("ss", t) for t in range(TILES)] + [("xn", t) for t in range(TILES)] + ["lg", "softplus"]
        pool_order = ["rs0"]
        for i in range(len(IN_ITEMS)):
            n = i - LEVEL_AFTER + 1
            if IN_ITEMS[i][0] in ("rq", "rk"):
                pool_order += [("cos", i, c) for c in range(2)]
            if 7 <= i < 7 + HEADS:
                act_order += [("strip", i - 7, d) for d in range(2)]
                pool_order += [("sel", i - 7, d) for d in range(2)]
                dve_order += [("strip", i - 7)]
            if 0 <= n < NL:
                pool_order += [("sub", n)]
                act_order += [("exp", n)]
            if 0 <= n <= NL:
                dve_order += [("lqk", n)]
            if i == CARRY_AFTER:
                pool_order += ["subF", "subB"]
                act_order += ["expF", "expB"]
                dve_order += ["qkF", "qkB"]
        dve_order += ["modc"]
        act_order += ["wcol", ("qtab", 0)]
        pool_order += [("qd", 0)]
        for job, block in plan_outputs():
            n = BLOCKS_OUT.index(block) if block else None
            if job[0] == "o":
                dve_order += [("cen", block)] + ([("on", BLOCKS_OUT[n - 1])] if n else []) + [("ms", block)]
                if block[0] == "r" and block[1] != "ctx" and block[1] < HEADS - 1:
                    act_order += [("qtab", block[1] + 1)]
                    pool_order += [("qd", block[1] + 1)]
                act_order += [("sq", block)]
                pool_order += [("rs", block)]
            elif job == ("rs", "ctx"):
                dve_order += ["cmask"]
            elif job == ("rkT",):
                dve_order += ["kdec"]
            elif job[0] == "rs" and job[2] == LT - 1:
                dve_order += [("rm", job[1])]
            if job == ("T", "r", 2):
                dve_order += [("on", BLOCKS_OUT[-1])]
        dve_order += [k for t in range(TILES) for k in (("x2", t), ("ms2", t), ("hn", t))]
        dve_order += ["diffs", "OO", "onehots", "idx", "dest"]
        act_order += [("ss2", t) for t in range(TILES)] + ["rexp"]
        pool_order += [("rs2", t) for t in range(TILES)]
        dve = Steps(sem("vector_steps"), dve_order)
        act = Steps(sem("scalar_steps"), act_order)
        pool_s = Steps(sem("gpsimd_steps"), pool_order)
        pool_done = pool_s.done

        def w_src(n):
            load, slot = LOADS[n], ring[n % RING]
            if load[0] == "ada":
                _, m, i = load
                return (w_ada[0].rearrange("(p k) c -> p k c", k=KC)[:, 2 * i:2 * i + 2, m * D:(m + 1) * D],
                        slot.rearrange("p (k c) -> p k c", k=2))
            if load[0] == "in":
                _, c0, w = IN_ITEMS[load[1]]
                return (w_in[0, :, c0:c0 + w].rearrange("(p k) c -> p k c", k=KC),
                        slot[:, 0:KC * w].rearrange("p (k c) -> p k c", k=KC))
            return (w_out[0, :, load[1] * ITEM:(load[1] + 1) * ITEM].rearrange("(k p) c -> p k c", k=KC),
                    slot.rearrange("p (k c) -> p k c", k=KC))

        def load_used(eng, n):
            load = LOADS[n]
            if load[0] == "ada":
                eng.wait_ge(ada_used, len([v for v in LOADS[:n] if v[0] == "ada"]) + 1)
            elif load[0] == "in":
                name, _, w = IN_ITEMS[load[1]]
                is_filled(eng, ("v", load[1], CTX) if name in ("gv", "rv") else ("p", load[1], max(1, w // P) - 1, "ctx"))
            else:
                is_filled(eng, ("mix", CTX, load[1]))

        def load_ready(eng, n):
            eng.wait_ge(landed[n % RING], 16 * (n // RING + 1))

        ex_landed = [sem(f"expert_weights{n}_landed") for n in range(4)]
        xg_landed = [sem(f"tokens{n}_landed") for n in range(4)]
        xg_turned, xte_ready, gu_filled = sem("tokens_turned"), sem("tokens_ready"), sem("gate_up_filled")
        sil_ready, hid_ready, y_filled = sem("silu_ready"), sem("hidden_ready"), sem("expert_done")
        y_half0, y_half1 = sem("y_half0"), sem("y_half1")
        ys_written = [sem(f"expert_rows_written{n}") for n in range(2)]
        ov_landed = sem("overflow_weights_landed")
        idxc_set = sem("slot_tokens_set")
        turns_begun, gathers_begun = sem("turns_begun"), sem("gathers_begun")
        yp_landed = [sem(f"pick_rows{n}_landed") for n in range(2)]
        y_used, x3_ready, ss3_ready, yo_ready = sem("picks_used"), sem("x3_ready"), sem("ss3_ready"), sem("final_ready")
        ms3_ready, rs3_ready = sem("final_squares_ready"), sem("final_roots_ready")
        yo_written = [sem(f"final_written{n}") for n in range(2)]

        block = ctx.enter_context(nc.Block())

        @block.sync
        def _(sp):
            for n in range(len(LOADS)):
                src, dst = w_src(n)
                if n >= RING:
                    load_used(sp, n - RING)
                sp.dma_start(dst, src).then_inc(landed[n % RING], 16)

            def load_expert(e, b, s):
                sp.dma_start(exb[b][:, 0:UNIT], ewg_v[bass.ds(e * P, P), :]).then_inc(s, 16)
                sp.dma_start(exb[b][:, UNIT:2 * UNIT], ewu_v[bass.ds(e * P, P), :]).then_inc(s, 16)
                sp.dma_start(exb[b][:, 2 * UNIT:3 * UNIT], ewd_v[bass.ds(e * P, P), :]).then_inc(s, 16)

            ewg_v = ewg.rearrange("a e (p k) f -> (a e p) (k f)", p=P)
            ewu_v = ewu.rearrange("a e (p k) f -> (a e p) (k f)", p=P)
            ewd_v = ewd.rearrange("a e (p j) n -> (a e p) (j n)", p=P)
            is_drained(sp, ("T", "r", HEADS - 1))
            for b in range(2):
                load_expert(b, b, ex_landed[b])
            load_used(sp, len(LOADS) - 1)
            sp.wait_ge(s_out, 16 * 4)
            for b in range(2, 4):
                load_expert(b, b, ex_landed[b])
            with sp.Fori(1, NE // 4) as it:
                for b in range(4):
                    sp.wait_ge(y_filled, 4 * it + b - 3)
                    load_expert(4 * it + b, b, ex_landed[b])
            dve.wait(sp, "dest")
            n_over = sp.value_load(over[0:1, 0:1], min_val=0, max_val=MAX_OVER)
            with sp.If(n_over > 0):
                with sp.Fori(0, n_over) as i:
                    e = sp.value_load(over[0:1, bass.ds(i + 1, 1)], min_val=0, max_val=NE - 1)
                    sp.wait_ge(y_filled, NE + i)
                    load_expert(e, 0, ov_landed)
            ya = y_sample.rearrange("a t d -> (a t) d")
            yc = y_prompt.rearrange("a t d -> (a t) d")
            for t in range(TILES):
                sp.wait_ge(yo_ready, t + 1)
                dst = ya[t * P:(t + 1) * P, :] if t < LT else yc[:, :]
                sp.dma_start(dst, yo[t % 2]).then_inc(yo_written[t % 2], 16)
            sp.wait_ge(yo_written[0], 16 * 3)
            sp.wait_ge(yo_written[1], 16 * 2)
            sp.wait_ge(s_out, 16 * 4)

        @block.gpsimd
        def _(pool):
            chain = [0]

            def link(ins):
                chain[0] += 1
                ins.then_inc(pool_chain, 1)
                pool.wait_ge(pool_chain, chain[0])

            for m in range(2):
                pool.dma_start(bcol[:, m, :], b_ada[0, m * D:(m + 1) * D].rearrange("(p k) -> p k", k=KC)).then_inc(s_row, 16)
            pool.dma_start(n1col, norm1_w[0].rearrange("(p k) -> p k", k=KC)).then_inc(s_row, 16)
            with nc.allow_non_contiguous_dma(reason="small columns"):
                for d, v in enumerate((ggbf, ggbb)):
                    pool.dma_start(gbias[:, d, :], v[0].rearrange("(g p) -> p g", p=P)).then_inc(s_cols, 16)
                for d, v in enumerate((ret_norm_w, gla_norm_w)):
                    pool.dma_start(nw[:, 4 * d:4 * d + 4], v[0].rearrange("(h p) -> p h", p=P)).then_inc(s_cols, 16)
            for d, v in enumerate((rdf, rdb)):
                pool.dma_start(lg[:, d, :], v[0:1, :].partition_broadcast(P)).then_inc(s_cols, 16)
            link(nc.gpsimd.memset(wgate, 0.0))
            for d, v in enumerate((ggwf, ggwb)):
                pool.dma_start(wgate[RANK * d:RANK * (d + 1), d, :], v[0]).then_inc(s_gate, 16)
            link(nc.gpsimd.memset(power, -0.5))
            zero = onorm[0][0:SLOTS].rearrange("p a e -> p (a e)")
            link(nc.gpsimd.memset(zero, 0.0))
            link(nc.gpsimd.memset(wrow, 1.0))
            for cond in range(2):
                r0 = cond * 32
                pool.dma_start(brow[r0:r0 + 32, :], b_ada[0, 2 * D:6 * D].rearrange("(c n) -> c n", n=P)).then_inc(s_mrow, 16)
                pool.dma_start(wrow[r0 + 16:r0 + 24, :], norm2_w[0].rearrange("(c n) -> c n", n=P)).then_inc(s_mrow, 16)

            def root(ap, key, rkey):
                dve.wait(pool, key)
                pool_done(nc.gpsimd.tensor_tensor(ap, ap, power[:, 0:ap.shape[1]], ALU.pow), rkey)

            root(rstd, "ms0", "rs0")

            is_filled(pool, ("xTc", 1))
            for n, (dst, c0) in enumerate(((rel[0], R_RELF), (rel[1], R_RELB), (tft[0], R_TF), (tft[1], R_TB))):
                pool.dma_start(dst, rconsts[:, c0:c0 + dst.shape[1]]).then_inc(s_rc, 16)

            def level_exponents(n):
                h = LEVELS[n]
                nb = T // (2 * h)
                v = [cum[:, d].rearrange("p g (b two h) -> p g b two h", two=2, h=h) for d in range(2)]
                o = [lx[:, a].rearrange("p g (b two h) -> p g b two h", two=2, h=h) for a in range(2)]
                shape = [P, 2, nb, h]
                ref = [v[0][:, :, :, 0, h - 1:h].to_broadcast(shape), v[1][:, :, :, 1, 0:1].to_broadcast(shape)]
                if n == 0:
                    dve.wait(pool, "cum")
                else:
                    dve.wait(pool, ("lqk", n - 1))
                nc.gpsimd.tensor_tensor(o[0][:, :, :, 1], v[0][:, :, :, 1], ref[0], ALU.subtract)
                nc.gpsimd.tensor_tensor(o[0][:, :, :, 0], ref[1], v[1][:, :, :, 0], ALU.subtract)
                nc.gpsimd.tensor_tensor(o[1][:, :, :, 0], ref[0], v[0][:, :, :, 0], ALU.subtract)
                pool_done(nc.gpsimd.tensor_tensor(o[1][:, :, :, 1], v[1][:, :, :, 1], ref[1], ALU.subtract), ("sub", n))

            pool.wait_ge(s_tail, 16 * 2)
            for i, (name, _, w) in enumerate(IN_ITEMS):
                if name in ("rq", "rk"):
                    for c in range(2):
                        a, h = ("rq", "rk").index(name), 2 * ((i - 3) % 2) + c
                        n = 2 * (i - 3) + c
                        is_drained(pool, ("p", i, c, "lat"))
                        pool_done(nc.gpsimd.tensor_tensor(rqk[:, a, h, 0:N_LAT], raw[n % 2], cosT, ALU.mult), ("cos", i, c))
                if i == 7:
                    for half in range(2):
                        pool.dma_start(ys_dram[NE * SLOTS:, half * 512:(half + 1) * 512].rearrange("(b s) d -> s b d", s=SLOTS),
                                       zero.unsqueeze(1).to_broadcast([SLOTS, MAX_OVER, 512])).then_inc(s_zero, 16)
                if 7 <= i < 7 + HEADS:
                    h = i - 7
                    for d in range(2):
                        o = strips[:, h, :] if d == 0 else stmp[h % 2]
                        act.wait(pool, ("strip", h, d))
                        sgn = 1 - 2 * d
                        pool_done(nc.gpsimd.affine_select(out=o, in_=o, compare_op=ALU.is_ge, fill=0.0,
                                                          base=-sgn * (N_LAT - P), pattern=[[sgn, STRIP]],
                                                          channel_multiplier=-sgn), ("sel", h, d))
                if 0 <= i - LEVEL_AFTER + 1 < NL:
                    level_exponents(i - LEVEL_AFTER + 1)
                if i == CARRY_AFTER:
                    tb = [tot[:, 2 * d:2 * d + 2, :].unsqueeze(3).to_broadcast([P, 2, TILES, P]) for d in range(2)]
                    tv = [cum[:, d].rearrange("p g (t n) -> p g t n", n=P) for d in range(2)]
                    ov = [lx[:, a].rearrange("p g (t n) -> p g t n", n=P) for a in range(2)]
                    dve.wait(pool, ("lqk", NL - 1))
                    pool_done(nc.gpsimd.tensor_tensor(ov[1], tb[0], tv[0], ALU.subtract), "subF")
                    dve.wait(pool, "qkF")
                    pool_done(nc.gpsimd.tensor_tensor(ov[0], tb[1], tv[1], ALU.subtract), "subB")
                    act.wait(pool, "expB")
                    for d, v in enumerate((sgf, sgb)):
                        pool.dma_start(gst[:, d, 0], v[0, 0].rearrange("(g a) d e -> (a d) g e", a=2)).then_inc(s_gs0, 16)
            is_filled(pool, ("gu", 1, 3))
            for d, v in enumerate((srf, srb)):
                pool.dma_start(rstate[:, d], v[0, 0].rearrange("h d e -> d h e")).then_inc(s_rs0, 16)
            is_drained(pool, ("modT",))
            for cond in range(2):
                pool.dma_start(mod_dram[cond:cond + 1, 2 * D:6 * D].rearrange("a (c n) -> (a c) n", n=P),
                               modr[cond * 32:(cond + 1) * 32, :]).then_inc(s_modw, 16)

            def scaled_queries(h):
                act.wait(pool, ("qtab", h))
                if h >= 1:
                    is_filled(pool, ("o", "r", h - 1))
                link(nc.gpsimd.tensor_tensor(qd[0], rqk[:, 0, h, 0:N_LAT], qtab[0], ALU.mult))
                pool_done(nc.gpsimd.tensor_tensor(qd[1], rqk[:, 0, h, 0:N_LAT], qtab[1], ALU.mult), ("qd", h))

            def mod_rows(m, dst):
                for cond in range(2):
                    pool.dma_start(dst[cond], mod_dram[cond:cond + 1, m * D:(m + 1) * D].partition_broadcast(P)).then_inc(s_bc, 16)

            scaled_queries(0)
            for b in BLOCKS_OUT:
                if b[0] == "r" and b[1] != "ctx" and b[1] < HEADS - 1:
                    scaled_queries(b[1] + 1)
                root(st2, ("ms", b), ("rs", b))
                if b == ("r", "ctx"):
                    is_filled(pool, ("o", "g", HEADS - 1))
                    pool.wait_ge(s_modw, 32)
                    mod_rows(2, g1b)
                    mod_rows(3, b2b)
                    pool.dma_start(rtw[:, :, 0:NG], rgw[0].rearrange("(p k) n -> p k n", k=KC)).then_inc(s_rt, 16)
                    pool.dma_start(rtw[:, :, NG:NG + NE], rew[0].rearrange("(p k) n -> p k n", k=KC)).then_inc(s_rt, 16)
                    pool.dma_start(G[:, rk0:rk0 + C_END - C_ONES], consts[:, C_ONES:C_END]).then_inc(s_rt, 16)
                    pool.dma_start(rbias[:, 0:NG], rgb[0:1, :].partition_broadcast(P)).then_inc(s_rt, 16)
                    pool.dma_start(rbias[:, NG:NG + NE], reb[0:1, :].partition_broadcast(P)).then_inc(s_rt, 16)
                if b == ("r", HEADS - 2):
                    is_filled(pool, ("o", "r", HEADS - 2))
                    mod_rows(4, a2b)
            is_drained(pool, ("T", "r", HEADS - 1))
            for cond in range(2):
                pool.dma_start(g2b[cond], mod_dram[cond:cond + 1, 5 * D:6 * D].partition_broadcast(P)).then_inc(s_fin, 16)
            pool.dma_start(fnb, final_w.rearrange("(a n) -> a n", a=1).partition_broadcast(P)).then_inc(s_fin, 16)

            for t in range(TILES):
                root(rstd[:, t:t + 1], ("ms2", t), ("rs2", t))

            def gather_block(col, b):
                nc.gpsimd.tensor_copy(idxc[b][:, :], idx[:, col]).then_inc(idxc_set, 1)

            def gather_rows(b, count):
                pool.wait_ge(idxc_set, count)
                pool.sem_inc(gathers_begun, 1)
                pool.indirect_dma_start(xg[b], None, hn_dram[:, :], bass.IndirectOffsetOnAxis(ap=idxc[b][:, :].bitcast(U32), axis=0)
                                        ).then_inc(xg_landed[b], 16)

            dve.wait(pool, "idx")
            for n in range(2):
                pool.wait_ge(s_hnw[n], 16 * (3 - n))
            is_filled(pool, ("mix", CTX, 3))
            for b in range(4):
                gather_block(slice(b, b + 1), b)
                gather_rows(b, b + 1)
            with pool.Fori(1, NE // 4) as it:
                for b in range(4):
                    pool.wait_ge(xg_turned, 4 * it + b - 3)
                    gather_block(bass.ds(4 * it + b, 1), b)
                    gather_rows(b, 4 * it + b + 1)
            pool.wait_ge(xg_turned, NE - 3)
            gather_block(slice(NE, NE + 1), 0)
            gather_rows(0, NE + 1)
            dve.wait(pool, "dest")
            n_over = pool.value_load(over[0:1, 0:1], min_val=0, max_val=MAX_OVER)
            with pool.If(n_over > 0):
                with pool.Fori(0, n_over) as i:
                    pool.wait_ge(xg_turned, NE + 1 + i)
                    gather_block(bass.ds(NE + i, 1), 0)
                    gather_rows(0, NE + 2 + i)
            link(nc.gpsimd.tensor_copy(destc[:, :], dest[:, :]))
            pool.wait_ge(ys_written[0], n_over * 16 + 16 * (NE // 2))
            pool.wait_ge(ys_written[1], 16 * (NE // 2))
            pool.wait_ge(y_filled, n_over + NE)
            pool.sem_inc(gathers_begun, 1)

            def final_root(t):
                pool.wait_ge(ms3_ready, t + 1)
                nc.gpsimd.tensor_tensor(rstd[:, t:t + 1], rstd[:, t:t + 1], power[:, 0:1], ALU.pow).then_inc(rs3_ready, 1)

            for t in range(TILES):
                if t >= 2:
                    pool.wait_ge(y_used, t - 1)
                for k in range(2):
                    pool.indirect_dma_start(yp[t % 2][k], None, ys_dram[:, :],
                                            bass.IndirectOffsetOnAxis(ap=destc[:, k * TILES + t:k * TILES + t + 1].bitcast(U32), axis=0)
                                            ).then_inc(yp_landed[t % 2], 16)
                if t >= 1:
                    final_root(t - 1)
            final_root(CTX)

        @block.scalar
        def _(sc):
            chain = [0]

            def link(ins):
                chain[0] += 1
                ins.then_inc(act_chain, 1)
                sc.wait_ge(act_chain, chain[0])

            f = nc.scalar.activation
            for cond, v in enumerate((c_in[0], c_ctx)):
                sc.dma_start(cT[:, cond, :], v.rearrange("(p k) -> p k", k=KC)).then_inc(s_cond, 16)
            sc.dma_start(ident[:, :], consts[:, C_IDENT:C_IDENT + P]).then_inc(s_ident, 16)
            xs = x_sample.rearrange("a t d -> (a t) d")
            for t in range(TILES):
                sc.dma_start(X[:, t, :], xs[t * P:(t + 1) * P, :] if t < LT else x_prompt[0]).then_inc(s_x[t], 16)
            sc.dma_start(ccol, consts[:, C_IOTA:C_END]).then_inc(s_ident, 16)
            sc.dma_start(tail[:, 0:2048], consts[:, C_ROT:C_ONES]).then_inc(s_tail, 16)
            sc.dma_start(ones_s, consts[:, C_ONES:C_ONES + P]).then_inc(s_tail, 16)
            sc.wait_ge(s_cond, 32)
            act.done(f(cS, cT, ACT.Silu), "cS")
            for t in range(TILES):
                sc.wait_ge(s_x[t], 16)
                act.done(f(xn[:, t, :], X[:, t, :], ACT.Square, accum_out=ss[:, t:t + 1]), ("ss", t))
            pool_s.wait(sc, "rs0")
            for t in range(TILES):
                act.done(f(xn[:, t, :].rearrange("p (k j) -> p k j", k=KC), X[:, t, :].rearrange("p (j k) -> p k j", k=KC),
                           ACT.Copy, scale=rstd[:, t:t + 1]), ("xn", t))
            sc.wait_ge(s_cols, 16 * 6)
            link(f(lg, lg, ACT.Exp))
            act.done(f(lg, lg, ACT.Copy, scale=-1.0), "lg")

            for i, (name, _, w) in enumerate(IN_ITEMS):
                if name in ("gv", "rv"):
                    off = (512 if name == "gv" else 0) + ITEM * ((i - 7) % 2)
                    for t in range(TILES):
                        is_filled(sc, ("v", i, t))
                        drains(f(vv[:, t, off:off + ITEM], bk(("v", i, t))[:, 0:ITEM], ACT.Copy), ("v", i, t))
                else:
                    for c in range(max(1, w // P)):
                        n = 2 * (i - 3) + c
                        for part, lo, hi in (("lat", 0, N_LAT), ("ctx", N_LAT, T)):
                            job = ("p", i, c, part)
                            src = bk(job)[:, 0:hi - lo]
                            is_filled(sc, job)
                            if name == "gq":
                                drains(f(gqk[:, 0, c, lo:hi], src, ACT.Copy, scale=GLA_DK ** -0.5), job)
                            elif name == "gk":
                                drains(f(gqk[:, 1, c, lo:hi], src, ACT.Copy), job)
                            elif name == "glr":
                                drains(f(glrT[:, lo:hi], src[0:2 * RANK, :], ACT.Copy), job)
                            elif name in ("rq", "rk"):
                                a, h = ("rq", "rk").index(name), 2 * ((i - 3) % 2) + c
                                s = float(P) ** -0.5 if a else 1.0
                                if part == "lat":
                                    if n == 0:
                                        is_filled(sc, ("xTc", 1))
                                    if n >= 2:
                                        j = (3 + (n - 2) // 2, (n - 2) % 2)
                                        pool_s.wait(sc, ("cos", *j))
                                        is_filled(sc, ("rot", *j))
                                    drains(f(raw[n % 2], src, ACT.Copy, scale=s), job)
                                else:
                                    drains(f(rqk[:, a, h, lo:hi], src, ACT.Copy, scale=s), job)
                            else:
                                h = 2 * ((i - 11) % 2) + c + (4 if name == "gr" else 0)
                                if i == 11 and c == 0 and part == "lat":
                                    is_drained(sc, ("rot", 6, 1))
                                    dve.wait(sc, ("strip", HEADS - 1))
                                drains(f(gates[:, h, lo:hi], src, ACT.Silu), job)
                if name == "glr":
                    dve.wait(sc, "zb")
                    link(f(lx_f, cum_f, ACT.Abs))
                    link(f(lx_f, lx_f, ACT.Exp, scale=-1.0))
                    act.done(f(lx_f, lx_f, ACT.Ln, bias=1.0), "softplus")
                if 7 <= i < 7 + HEADS:
                    h = i - 7
                    if h == 0:
                        sc.wait_ge(s_rc, 16 * 4)
                    for d in range(2):
                        if d == 1 and h >= 2:
                            dve.wait(sc, ("strip", h - 2))
                        act.done(f(strips[:, h, :] if d == 0 else stmp[h % 2], rel[d], ACT.Exp, scale=lg[:, d, h:h + 1]),
                                 ("strip", h, d))
                n = i - LEVEL_AFTER + 1
                if 0 <= n < NL:
                    pool_s.wait(sc, ("sub", n))
                    act.done(f(lx_f, lx_f, ACT.Exp, scale=1.0 / 16.0), ("exp", n))
                if i == CARRY_AFTER:
                    link(f(dec, tot, ACT.Exp, scale=1.0 / 16.0))
                    pool_s.wait(sc, "subF")
                    link(f(lx[:, 1], lx[:, 1], ACT.Exp, scale=1.0 / 16.0))
                    act.done(f(lx[:, 0], cum[:, 0], ACT.Exp, scale=1.0 / 16.0), "expF")
                    pool_s.wait(sc, "subB")
                    link(f(lx[:, 0], lx[:, 0], ACT.Exp, scale=1.0 / 16.0))
                    act.done(f(lx[:, 1], cum[:, 1], ACT.Exp, scale=1.0 / 16.0), "expB")
                if i == CARRY_AFTER + 1:
                    for d in range(2):
                        for g in range(2):
                            job = ("kT", d, g)
                            is_filled(sc, job)
                            drains(f(kTok[:, 4 * d:4 * d + 4, g, :], bk(job)[:, :].rearrange("p (n c) -> p n c", n=4),
                                     ACT.Copy), job)
            for d, v in enumerate((new_gf, new_gb)):
                is_drained(sc, ("gu", d, 0))
                sc.dma_start(v[0, 0].rearrange("(g a) d e -> (a d) g e", a=2), gsout[:, d]).then_inc(s_out, 16)
            for d in range(2):
                for h in range(HEADS):
                    link(f(wcol[:, d, h:h + 1], ccol[:, C_POS - C_IOTA + 1 - d:C_POS - C_IOTA + 2 - d], ACT.Exp,
                           scale=lg[:, d, h:h + 1]))
            act.done(f(st3[:, 0:1], lg[:, 0, 0:1], ACT.Copy), "wcol")

            def query_tables(h):
                if h == 0:
                    dve.wait(sc, "qkB")
                else:
                    pool_s.wait(sc, ("qd", h - 1))
                link(f(qtab[0], tft[0], ACT.Exp, scale=lg[:, 0, h:h + 1]))
                act.done(f(qtab[1], tft[1], ACT.Exp, scale=lg[:, 1, h:h + 1]), ("qtab", h))

            query_tables(0)
            for job, b in plan_outputs():
                if job[0] == "o":
                    if b[0] == "r" and b[1] != "ctx" and b[1] < HEADS - 1:
                        query_tables(b[1] + 1)
                    if b == ("r", HEADS - 1):
                        dve.wait(sc, ("rm", HEADS - 1))
                        pool_s.wait(sc, ("qd", HEADS - 1))
                        for t in range(TILES):
                            sc.dma_start(X[:, t, :], xs[t * P:(t + 1) * P, :] if t < LT else x_prompt[0]).then_inc(s_x2[t], 16)
                    dve.wait(sc, ("cen", b))
                    act.done(f(sq, onorm[BLOCKS_OUT.index(b) % 2][:, :, :], ACT.Square), ("sq", b))
                if job[0] == "rst":
                    d = job[1]
                    is_filled(sc, job)
                    drains(f(rsout[:, d], bk(job)[:, :].rearrange("p (h e) -> p h e", h=HEADS), ACT.Copy), job)
                    is_drained(sc, job)
                    sc.dma_start((new_rf, new_rb)[d][0, 0].rearrange("h d e -> d h e"), rsout[:, d]).then_inc(s_out, 16)
            for t in range(TILES):
                dve.wait(sc, ("x2", t))
                if t >= 2:
                    dve.wait(sc, ("hn", t - 2))
                act.done(f(mt[t % 2], X[:, t, :], ACT.Square, accum_out=ss[:, t:t + 1]), ("ss2", t))
                dve.wait(sc, ("hn", t))
                sc.dma_start(hn_dram[t * P:(t + 1) * P, :].rearrange("t d -> t d"), hn[t % 2]).then_inc(s_hnw[t % 2], 16)
                for half in range(2):
                    job = ("hT", t, half)
                    is_filled(sc, job)
                    if t >= 1:
                        is_filled(sc, ("lg", t - 1))
                    drains(f(hnT[:, 4 * half:4 * half + 4, :], bk(job)[:, :].rearrange("p (k t) -> p k t", k=4), ACT.Copy), job)
            dve.wait(sc, "diffs")
            act.done(f(rdiff, rdiff, ACT.Exp), "rexp")

            def turned_tokens(e, n, free):
                sc.wait_ge(xg_turned, e + 1)
                if free is not None:
                    sc.wait_ge(gu_filled, free)
                f(xte[n], bank[n][:, :].rearrange("p (k s) -> p k s", k=KC), ACT.Copy).then_inc(xte_ready, 1)

            def silu(e, n, free):
                sc.wait_ge(gu_filled, e + 1)
                if free is not None:
                    sc.wait_ge(hid_ready, free)
                f(sil[n], bank[2 + n][:, 0:P], ACT.Silu).then_inc(sil_ready, 1)

            def half_rows(e, n, row, written):
                sc.wait_ge(y_filled, e + 1)
                if written is not None:
                    sc.wait_ge(ys_written[n], written)
                f(yb[n][:, 0:512], bank[4 + 2 * n][0:SLOTS, :], ACT.Copy).then_inc(y_half0, 1)
                sc.wait_ge(y_half0, e + 1)
                sc.wait_ge(y_half1, e + 1)
                sc.dma_start(ys_dram[bass.ds(row, SLOTS), :], yb[n]).then_inc(ys_written[n], 16)

            def experts(it, first):
                for b in range(4):
                    e = 4 * it + b
                    silu(e, b % 2, None if first and b < 2 else e - 1)
                    turned_tokens(e + 1, (b + 1) % 2, None if first and b < 1 else e)
                    half_rows(e, b % 2, e * SLOTS, None if first and b < 2 else 32 * it + 16 * (b // 2))

            for h in range(2):
                sc.wait_ge(s_hnw[h], 16 * (3 - h))
            sc.wait_ge(s_zero, 32)
            turned_tokens(0, 0, None)
            experts(0, True)
            with sc.Fori(1, NE // 4) as it:
                experts(it, False)
            dve.wait(sc, "dest")
            n_over = sc.value_load(over[0:1, 0:1], min_val=0, max_val=MAX_OVER)
            with sc.If(n_over > 0):
                with sc.Fori(0, n_over) as i:
                    turned_tokens(NE + 1 + i, 0, NE + i)
                    silu(NE + i, 0, NE + i)
                    half_rows(NE + i, 0, (NE + i) * SLOTS, 16 * (NE // 2) + 16 * i)
            for t in range(TILES):
                sc.wait_ge(x3_ready, t + 1)
                if t >= 2:
                    sc.wait_ge(yo_written[t % 2], 16 * (t // 2))
                f(yo[t % 2], X[:, t, :], ACT.Square, accum_out=ss[:, t:t + 1]).then_inc(ss3_ready, 1)

        @block.vector
        def _(dv):
            chain = [0]

            def link(ins):
                chain[0] += 1
                ins.then_inc(dve_chain, 1)
                dv.wait_ge(dve_chain, chain[0])

            v = nc.vector

            def mean_square(out, total, n):
                return v.tensor_scalar(out, total, 1.0 / n, EPS, ALU.mult, ALU.add)

            act.wait(dv, ("ss", CTX))
            dve.done(mean_square(rstd, ss, D), "ms0")
            dv.wait_ge(ada_used, 8)
            dv.wait_ge(s_row, 16 * 3)
            dv.wait_ge(s_ident, 32)
            link(v.tensor_tensor(mcol.rearrange("p (m a) k -> p m a k", m=2), mod_ps[:, 0:32].rearrange("p (m a k) -> p m a k", m=2, a=2),
                                 bcol.unsqueeze(2).to_broadcast([P, 2, 2, KC]), ALU.add))
            dve.done(v.scalar_tensor_tensor(mcol[:, 2:4], mcol[:, 2:4], 1.0, n1col.unsqueeze(1).to_broadcast([P, 2, KC]),
                                            ALU.add, ALU.mult), "mcol")
            dve.wait(dv, "mcol")
            for k in range(KC):
                job = ("xT", k)
                is_filled(dv, job)
                drains(v.tensor_scalar(hT[:, k, 0:N_LAT], bk(job)[:, :], mcol[:, 2, k:k + 1], mcol[:, 0, k:k + 1],
                                       ALU.mult, ALU.add), job)
            for half in range(2):
                job = ("xTc", half)
                is_filled(dv, job)
                for k in range(4 * half, 4 * half + 4):
                    ins = v.tensor_scalar(hT[:, k, N_LAT:T], bk(job)[:, (k % 4) * P:(k % 4 + 1) * P],
                                          mcol[:, 3, k:k + 1], mcol[:, 1, k:k + 1], ALU.mult, ALU.add)
                drains(ins, job)
            dve.done(v.memset(st3[:, 1:2], 0.0), "hT")

            def level_scores(n):
                for m, (t0, t1) in enumerate(LEV_TILES):
                    for a in range(2):
                        job = ("lev", n, m, a)
                        is_filled(dv, job)
                        w = 2 * (t1 - t0) * P
                        src = bk(job)[:, 0:w].rearrange("p (t g q) -> p t g q", g=2, q=P)
                        dst = att[:, t0:t1, a::2, :]
                        if n == 0:
                            drains(v.tensor_copy(dst, src), job)
                        else:
                            mask = masks[n - 1].bitcast(U32).unsqueeze(1).unsqueeze(1).to_broadcast([P, t1 - t0, 2, P])
                            if (m, a) == (0, 0):
                                is_drained(dv, ("lev", n - 1, 2, 1))
                            drains(v.copy_predicated(dst, mask, src), job)

            for i, (name, _, w) in enumerate(IN_ITEMS):
                if name == "glr":
                    dv.wait_ge(s_cols, 16 * 6)
                    for d in range(2):
                        for g in range(2):
                            for part, lo, hi in (("lat", 0, N_LAT), ("ctx", N_LAT, T)):
                                job = ("z", d, g, part)
                                is_filled(dv, job)
                                ins = v.tensor_scalar(cum[:, d, g, lo:hi], bk(job)[:, 0:hi - lo], gbias[:, d, g:g + 1], None, ALU.add)
                                drains(ins, job)
                    is_drained(dv, ("z", 1, 1, "ctx"))
                    dve.done(v.memset(st3[:, 2:3], 0.0), "zb")
                    act.wait(dv, "softplus")
                    link(v.scalar_tensor_tensor(lqk_f, cum_f, 0.0, lx_f, ALU.min, ALU.subtract))
                    dv.wait_ge(s_tail, 32)
                    for d in range(2):
                        for g in range(2):
                            for t in range(TILES):
                                tt = slice(t * P, (t + 1) * P)
                                ins = v.tensor_tensor_scan(cum[:, d, g, tt], ones_s, lqk[:, d, g, tt], 0.0, ALU.mult, ALU.add)
                    link(ins)
                    link(v.tensor_copy(tot, cum_f.rearrange("p (a t n) -> p a t n", a=4, n=P)[:, :, :, P - 1]))
                    dve.done(v.tensor_tensor(cum[:, 1], cum[:, 1], lqk[:, 1], ALU.subtract), "cum")
                if rots_after(i, 0) is not None or i in (3, 4, 5, 6):
                    for c in range(2):
                        j = rots_after(i, c)
                        if j is None:
                            continue
                        a, h = ("rq", "rk").index(IN_ITEMS[j[0]][0]), 2 * ((j[0] - 3) % 2) + j[1]
                        job = ("rot", *j)
                        is_filled(dv, job)
                        link(v.tensor_tensor(rsin, bk(job)[:, :], sinT, ALU.mult))
                        pool_s.wait(dv, ("cos", *j))
                        drains(v.tensor_tensor(rqk[:, a, h, 0:N_LAT], rqk[:, a, h, 0:N_LAT], rsin, ALU.add), job)
                        is_drained(dv, job)
                if 7 <= i < 7 + HEADS:
                    h = i - 7
                    pool_s.wait(dv, ("sel", h, 1))
                    dve.done(v.tensor_tensor(strips[:, h, :], strips[:, h, :], stmp[h % 2], ALU.add), ("strip", h))
                n = i - LEVEL_AFTER
                if 0 <= n <= NL:
                    level_scores(n)
                if 0 <= n + 1 < NL:
                    act.wait(dv, ("exp", n + 1))
                    if n >= 0:
                        is_filled(dv, ("lev", n, 2, 1))
                    dve.done(v.tensor_tensor(lqk_f, gqk_f, lx_f, ALU.mult), ("lqk", n + 1))
                elif n + 1 == NL:
                    is_filled(dv, ("lev", n, 2, 1))
                    dve.done(v.tensor_scalar(lqk[:, 0], gqk[:, 0], 2.0, None, ALU.mult), ("lqk", NL))
                if i == CARRY_AFTER:
                    act.wait(dv, "expF")
                    is_filled(dv, ("lev", NL, 2, 1))
                    dve.done(v.tensor_tensor(lqk_f, gqk_f, lx_f, ALU.mult), "qkF")
                    act.wait(dv, "expB")
                    dve.done(v.tensor_tensor(lx_f, gqk_f, lx_f, ALU.mult), "qkB")
                if i == CARRY_AFTER + 1:
                    dv.wait_ge(s_gs0, 32)
                    for n in range(4):
                        for d in range(2):
                            job = ("gu", d, n)
                            is_filled(dv, job)
                            src = bk(job)[:, 0:2 * P].rearrange("p (g e) -> p g e", g=2)
                            if n == 0:
                                drains(v.tensor_copy(gsout[:, d], src), job)
                                continue
                            t = (n - 1, LT - n)[d]
                            if n >= 2:
                                is_drained(dv, ("gu", d, n - 1))
                            link(v.scalar_tensor_tensor(gst[:, d, n, 0], gst[:, d, n - 1, 0], dec[:, 2 * d, t:t + 1], src[:, 0],
                                                        ALU.mult, ALU.add))
                            drains(v.scalar_tensor_tensor(gst[:, d, n, 1], gst[:, d, n - 1, 1], dec[:, 2 * d + 1, t:t + 1],
                                                          src[:, 1], ALU.mult, ALU.add), job)
            dv.wait_ge(ada_used, 24)
            dve.done(v.tensor_copy(modc, mod_ps[:, 64:128]), "modc")
            dv.wait_ge(s_mrow, 16 * 4)
            is_filled(dv, ("modT",))
            link(v.tensor_tensor(modr[0:64, :], bk(("modT",))[0:64, 0:P], brow[0:64, :], ALU.add))
            o = C_ONE - C_IOTA
            drains(v.scalar_tensor_tensor(modr[0:64, :], modr[0:64, :], ccol[0:64, o:o + 1], wrow[0:64, :], ALU.add, ALU.mult), ("modT",))

            def centre(b):
                job, n = ("o", *b), BLOCKS_OUT.index(b)
                is_filled(dv, job)
                if n >= 2:
                    is_filled(dv, ("T", *BLOCKS_OUT[n - 2]))
                src, o = bk(job)[:, :].rearrange("p (a e) -> p a e", a=4), onorm[n % 2][:, :, :]
                if b[0] == "r":
                    link(v.tensor_reduce(st1, src, AX, ALU.add))
                    link(v.tensor_scalar(st1, st1, 1.0 / P, None, ALU.mult))
                    ins = v.tensor_tensor(o, src, st1.unsqueeze(2).to_broadcast([P, 4, P]), ALU.subtract)
                else:
                    ins = v.tensor_copy(o, src)
                dve.done(ins, ("cen", b))
                drains(v.memset(st1[:, 3:4] if b[0] == "g" else st3[:, 3:4], 0.0), job)

            def squares(b):
                act.wait(dv, ("sq", b))
                if BLOCKS_OUT.index(b):
                    dve.wait(dv, ("on", BLOCKS_OUT[BLOCKS_OUT.index(b) - 1]))
                link(v.tensor_reduce(st2, sq, AX, ALU.add))
                dve.done(mean_square(st2, st2, P), ("ms", b))

            def scaled(b):
                pool_s.wait(dv, ("rs", b))
                o = onorm[BLOCKS_OUT.index(b) % 2][:, :, :]
                dve.done(v.tensor_tensor(o, o, st2.unsqueeze(2).to_broadcast([P, 4, P]), ALU.mult), ("on", b))

            def gate_block(b):
                job = ("T", *b)
                is_filled(dv, job)
                h0 = 4 if b[0] == "g" else 0
                if b[1] == "ctx":
                    for h in range(HEADS):
                        ins = v.scalar_tensor_tensor(hT[:, h0 + h, N_LAT:T], bk(job)[:, h * P:(h + 1) * P], nw[:, h0 + h:h0 + h + 1],
                                                     gates[:, h0 + h, N_LAT:T], ALU.mult, ALU.mult)
                    drains(ins, job)
                else:
                    h = h0 + b[1]
                    drains(v.scalar_tensor_tensor(hT[:, h, 0:N_LAT], bk(job)[:, :], nw[:, h:h + 1], gates[:, h, 0:N_LAT],
                                                  ALU.mult, ALU.mult), job)

            dv.wait_ge(s_zero, 32)
            dv.wait_ge(s_out, 32)
            for job, b in plan_outputs():
                if job[0] == "o":
                    n = BLOCKS_OUT.index(b)
                    centre(b)
                    if n:
                        scaled(BLOCKS_OUT[n - 1])
                    squares(b)
                elif job[0] == "T":
                    if job == ("T", "r", 2):
                        scaled(BLOCKS_OUT[-1])
                    gate_block(b)
                elif job == ("rs", "ctx"):
                    is_filled(dv, job)
                    drains(v.tensor_tensor(cmask, bk(job)[:, :].rearrange("p (h t) -> p h t", h=HEADS),
                                           strips[:, :, N_LAT - P:N_LAT], ALU.mult), job)
                    is_drained(dv, job)
                    dve.done(v.memset(st3[:, 0:1], 0.0), "cmask")
                elif job == ("rkT",):
                    is_filled(dv, job)
                    act.wait(dv, "wcol")
                    for d in range(2):
                        link(v.tensor_tensor(kdec[:, d], bk(job)[:, :].rearrange("p (h c) -> p h c", h=HEADS),
                                             wcol[:, d].unsqueeze(2).to_broadcast([P, HEADS, P]), ALU.mult))
                    drains(v.memset(st3[:, 1:2], 0.0), job)
                    dve.done(v.memset(st3[:, 2:3], 0.0), "kdec")
                elif job[0] == "rs":
                    _, h, s = job
                    is_filled(dv, job)
                    if h == HEADS - 1:
                        is_filled(dv, ("o", "r", 1))
                    x0 = N_LAT - P - s * P
                    drains(v.tensor_tensor(rmask[h][:, s], bk(job)[:, :], strips[:, h, x0:x0 + N_LAT], ALU.mult), job)
                    if s == LT - 1:
                        is_drained(dv, job)
                        dve.done(v.memset(st3[:, 3:4], 0.0), ("rm", h))

            dv.wait_ge(s_bc, 16 * 6)
            dv.wait_ge(s_rt, 16 * 5)
            for t in range(TILES):
                cond = int(t == CTX)
                for n in range(4):
                    job = ("mix", t, n)
                    cc = slice(n * ITEM, (n + 1) * ITEM)
                    is_filled(dv, job)
                    drains(v.tensor_tensor(mt[t % 2][:, cc], bk(job)[:, 0:ITEM], g1b[cond][:, cc], ALU.mult), job)
                is_drained(dv, job)
                dv.wait_ge(s_x2[t], 16)
                dve.done(v.tensor_tensor(X[:, t, :], X[:, t, :], mt[t % 2], ALU.add), ("x2", t))
                act.wait(dv, ("ss2", t))
                dve.done(mean_square(rstd[:, t:t + 1], ss[:, t:t + 1], D), ("ms2", t))
                pool_s.wait(dv, ("rs2", t))
                link(v.scalar_tensor_tensor(mt[t % 2], X[:, t, :], rstd[:, t:t + 1], a2b[cond], ALU.mult, ALU.mult))
                if t >= 2:
                    is_filled(dv, ("hT", t - 2, 1))
                    dv.wait_ge(s_hnw[t % 2], 16 * (t // 2))
                o = hn[t % 2].rearrange("p (k j) -> p k j", k=KC)
                dve.done(v.tensor_tensor(o, mt[t % 2].rearrange("p (j k) -> p k j", k=KC),
                                         b2b[cond].rearrange("p (j k) -> p k j", k=KC), ALU.add), ("hn", t))
                if t >= 1:
                    job = ("lg", t - 1)
                    is_filled(dv, job)
                    drains(v.tensor_tensor(lgt[:, t - 1, :], bk(job)[:, 0:36], rbias, ALU.add), job)
            job = ("lg", CTX)
            is_filled(dv, job)
            drains(v.tensor_tensor(lgt[:, CTX, :], bk(job)[:, 0:36], rbias, ALU.add), job)
            is_drained(dv, job)

            def bc(ap, n):
                return ap.unsqueeze(2).to_broadcast([P, ap.shape[1], n])

            def iota(n, rows=TILES):
                return kiota[:, 0:n].unsqueeze(1).to_broadcast([P, rows, n])

            def first_max(x, n):
                m, eq, i = rs(TILES), rs(TILES, n), rs(TILES)
                link(v.tensor_reduce(m, x, AX, ALU.max))
                link(v.tensor_tensor(eq, x, bc(m, n), ALU.is_equal))
                link(v.scalar_tensor_tensor(eq, eq, -100.0, iota(n), ALU.mult, ALU.add))
                link(v.tensor_reduce(i, eq, AX, ALU.min))
                link(v.tensor_scalar(i, i, 100.0, None, ALU.add))
                link(v.tensor_tensor(eq, iota(n), bc(i, n), ALU.is_equal))
                return m, i, eq

            gl = lgt[:, :, 0:NG]
            gm, gi, g_hot = first_max(gl, NG)
            gd = rdiff[:, 0:TILES * NG].rearrange("p (t g) -> p t g", t=TILES)
            link(v.tensor_tensor(gd, gl, bc(gm, NG), ALU.subtract))
            em, es = rs(TILES, NG, EPG), rs(TILES, EPG)
            for t in range(TILES):
                ins = v.tensor_tensor(em[:, t], lgt[:, t, NG:].rearrange("p (g j) -> p g j", g=NG), bc(g_hot[:, t], EPG), ALU.mult)
            link(ins)
            for t in range(TILES):
                ins = v.tensor_reduce(es[:, t], em[:, t].rearrange("p g j -> p j g"), AX, ALU.add)
            link(ins)
            m1, i1, hot1 = first_max(es, EPG)
            es2 = rs(TILES, EPG)
            link(v.scalar_tensor_tensor(es2, hot1, -3.0e38, es, ALU.mult, ALU.add))
            m2, i2, _ = first_max(es2, EPG)
            dve.done(v.tensor_tensor(rdiff[:, TILES * NG:], m2, m1, ALU.subtract), "diffs")
            pk_e, hot = rs(2 * TILES), rs(2 * TILES, NE)
            for k, i in enumerate((i1, i2)):
                link(v.scalar_tensor_tensor(pk_e[:, k * TILES:(k + 1) * TILES], gi, float(EPG), i, ALU.mult, ALU.add))
            link(v.tensor_tensor(hot, iota(NE, 2 * TILES), bc(pk_e, NE), ALU.is_equal))
            dve.done(v.tensor_tensor(oo, hot[:, 0:TILES], hot[:, TILES:], ALU.add), "OO")
            job = ("pos",)
            is_filled(dv, job)
            place = rs(TILES + 1, NE)
            drains(v.tensor_copy(place, bk(job)[:, 0:(TILES + 1) * NE].rearrange("p (t e) -> p t e", e=NE)), job)
            is_drained(dv, job)
            count = place[:, TILES]
            tmp = rs(2 * TILES, NE)
            for k in range(2):
                ks = slice(k * TILES, (k + 1) * TILES)
                link(v.tensor_tensor(tmp[:, ks], hot[:, ks], place[:, 0:TILES], ALU.mult))
            pk_p, q, slot = rs(2 * TILES), rs(2 * TILES), rs(2 * TILES)
            link(v.tensor_reduce(pk_p, tmp, AX, ALU.add))
            steps9 = kiota[:, 64:73]
            cmp9, n_ov, ov_end, ov_at = rs(NE, 9), rs(NE), rs(NE), rs(NE)
            link(v.tensor_tensor(cmp9, bc(count, 9), steps9.unsqueeze(1).to_broadcast([P, NE, 9]), ALU.is_gt))
            link(v.tensor_reduce(n_ov, cmp9, AX, ALU.add))
            link(v.tensor_tensor_scan(ov_end, kones[:, 0:NE], n_ov, 0.0, ALU.mult, ALU.add))
            link(v.tensor_tensor(ov_at, ov_end, n_ov, ALU.subtract))
            c2 = rs(2 * TILES, 9)
            link(v.tensor_tensor(c2, bc(pk_p, 9), steps9.unsqueeze(1).to_broadcast([P, 2 * TILES, 9]), ALU.is_ge))
            link(v.tensor_reduce(q, c2, AX, ALU.add))
            link(v.scalar_tensor_tensor(slot, q, -float(SLOTS), pk_p, ALU.mult, ALU.add))
            link(v.tensor_tensor(tmp, hot, ov_at.unsqueeze(1).to_broadcast([P, 2 * TILES, NE]), ALU.mult))
            va, blk, row = rs(2 * TILES), rs(2 * TILES), rs(2 * TILES)
            link(v.tensor_reduce(va, tmp, AX, ALU.add))
            link(v.tensor_tensor(va, va, q, ALU.add))
            link(v.scalar_tensor_tensor(va, va, float(NE - 1), pk_e, ALU.add, ALU.subtract))
            link(v.tensor_scalar(q, q, 1.0, None, ALU.min))
            link(v.tensor_tensor(va, va, q, ALU.mult))
            link(v.tensor_tensor(blk, va, pk_e, ALU.add))
            link(v.scalar_tensor_tensor(row, blk, float(SLOTS), slot, ALU.mult, ALU.add))
            link(v.tensor_tensor(oh_slot, iota(SLOTS, 2 * TILES), bc(slot, SLOTS), ALU.is_equal))
            link(v.tensor_tensor(oh_block, iota(BLOCKS, 2 * TILES), bc(blk, BLOCKS), ALU.is_equal))
            tok = kiota[:, C_TOK - C_IOTA:C_TOK - C_IOTA + TILES]
            for k in range(2):
                ks = slice(k * TILES, (k + 1) * TILES)
                ins = v.tensor_tensor(oh_block[:, ks], oh_block[:, ks], bc(tok, BLOCKS), ALU.mult)
            dve.done(ins, "onehots")
            job = ("idx",)
            is_filled(dv, job)
            drains(v.tensor_copy(idx[:, :], bk(job)[0:SLOTS, 0:BLOCKS]), job)
            is_drained(dv, job)
            dve.done(v.memset(st3[:, 3:4], 0.0), "idx")
            link(v.tensor_copy(dest[:, :], row))
            link(v.tensor_copy(over[0:1, 0:1], ov_end[0:1, NE - 1:NE]))
            cmpo, eob = rs(MAX_OVER, NE), rs(MAX_OVER)
            link(v.tensor_tensor(cmpo[0:1], ov_end[0:1].unsqueeze(1).to_broadcast([1, MAX_OVER, NE]),
                                 kiota[0:1, 0:MAX_OVER].unsqueeze(2).to_broadcast([1, MAX_OVER, NE]), ALU.is_le))
            link(v.tensor_reduce(eob[0:1], cmpo[0:1], AX, ALU.add))
            link(v.tensor_scalar(over[0:1, 1:], eob[0:1], float(NE - 1), None, ALU.min))
            act.wait(dv, "rexp")
            gs, p2 = rs(TILES), rdiff[:, TILES * NG:]
            link(v.tensor_reduce(gs, gd, AX, ALU.add))
            den = rs(TILES)
            link(v.tensor_scalar(den, p2, 1.0, None, ALU.add))
            link(v.tensor_tensor(den, den, gs, ALU.mult))
            link(v.reciprocal(pickw[:, 0, :], den))
            link(v.tensor_tensor(pickw[:, 1, :], pickw[:, 0, :], p2, ALU.mult))
            dve.done(v.memset(st3[:, 0:1], 0.0), "dest")

            def hidden(e, n, free):
                dv.wait_ge(sil_ready, e + 1)
                if free is not None:
                    dv.wait_ge(y_filled, free)
                v.tensor_tensor(hid[n], sil[n].rearrange("p (j s) -> p j s", j=FC),
                                bank[2 + n][:, P:2 * P].rearrange("p (j s) -> p j s", j=FC), ALU.mult).then_inc(hid_ready, 1)

            def half_rows(e, n, written):
                dv.wait_ge(y_filled, e + 1)
                if written is not None:
                    dv.wait_ge(ys_written[n], written)
                v.tensor_copy(yb[n][:, 512:D], bank[5 + 2 * n][0:SLOTS, :]).then_inc(y_half1, 1)

            def experts(it, first):
                for b in range(4):
                    e = 4 * it + b
                    hidden(e, b % 2, None if first and b < 2 else e - 1)
                    half_rows(e, b % 2, None if first and b < 2 else 32 * it + 16 * (b // 2))

            for h in range(2):
                dv.wait_ge(s_hnw[h], 16 * (3 - h))
            experts(0, True)
            with dv.Fori(1, NE // 4) as it:
                experts(it, False)
            n_over = dv.value_load(over[0:1, 0:1], min_val=0, max_val=MAX_OVER)
            with dv.If(n_over > 0):
                with dv.Fori(0, n_over) as i:
                    hidden(NE + i, 0, NE + i)
                    half_rows(NE + i, 0, 16 * (NE // 2) + 16 * i)
            dv.wait_ge(s_fin, 16 * 3)
            for t in range(TILES):
                cond = int(t == CTX)
                y1, y2 = yp[t % 2]
                dv.wait_ge(yp_landed[t % 2], 32 * (t // 2 + 1))
                link(v.tensor_scalar(y1, y1, pickw[:, 0, t:t + 1], None, ALU.mult))
                link(v.scalar_tensor_tensor(y2, y2, pickw[:, 1, t:t + 1], y1, ALU.mult, ALU.add))
                link(v.tensor_tensor(y2, y2, g2b[cond], ALU.mult))
                link(v.tensor_tensor(X[:, t, :], X[:, t, :], y2, ALU.add))
                v.memset(st3[:, 0:1], 0.0).then_inc(y_used, 1)
                v.memset(st3[:, 1:2], 0.0).then_inc(x3_ready, 1)
                dv.wait_ge(ss3_ready, t + 1)
                mean_square(rstd[:, t:t + 1], ss[:, t:t + 1], D).then_inc(ms3_ready, 1)
                dv.wait_ge(rs3_ready, t + 1)
                v.scalar_tensor_tensor(yo[t % 2], X[:, t, :], rstd[:, t:t + 1], fnb, ALU.mult, ALU.mult).then_inc(yo_ready, 1)

        @block.tensor
        def _(te):
            order = [0]

            def starts(job):
                assert JOBS[order[0]] == job, (JOBS[order[0]], job)
                order[0] += 1
                b, turn = where(job)
                if turn:
                    te.wait_ge(drained[b], turn)
                return bank[b]

            def fills(ins, job):
                ins.then_inc(filled[where(job)[0]], 1)

            mm, tr = nc.tensor.matmul, nc.tensor.transpose

            act.wait(te, "cS")
            mod_cols = mod_ps[:, 0:32].rearrange("p (m a k) -> p m a k", m=2, a=2)
            with te.Fori(0, 2) as m:
                for i in range(4):
                    te.wait_ge(landed[i], 16 * m + 16)
                    w = ring[i].rearrange("p (k c) -> p k c", k=2)
                    for kk in range(2):
                        for k in range(KC):
                            ins = mm(mod_cols[:, bass.ds(m, 1), :, k], w[:, kk, k::KC], cS[:, :, 2 * i + kk].unsqueeze(1),
                                     start=(i == kk == k == 0), stop=(i == 3 and kk == 1), skip_group_check=True)
                    ins.then_inc(ada_used, 1)

            def other_modulations(r):
                n = LOADS.index(("ada", 2 + r // 4, r % 4))
                load_ready(te, n)
                w = ring[n % RING].rearrange("p (k c) -> p k c", k=2)
                o = mod_ps[:, 64:128].rearrange("p (a n) -> p a n", a=2)
                for kk in range(2):
                    for c in range(KC):
                        ch = KC * (r // 4) + c
                        ins = mm(o[:, :, ch], w[:, kk, c * P:(c + 1) * P], cS[:, :, 2 * (r % 4) + kk],
                                 start=(r == kk == c == 0), stop=(r % 4 == 3 and kk == 1), skip_group_check=True)
                ins.then_inc(ada_used, 1)

            te.wait_ge(s_ident, 32)
            act.wait(te, ("xn", CTX))
            for k in range(KC):
                ps = starts(("xT", k))
                for t in range(LT):
                    ins = tr(ps[:, t * P:(t + 1) * P], xn[:, t, k * P:(k + 1) * P], ident[:, :])
                fills(ins, ("xT", k))
            for half in range(2):
                ps = starts(("xTc", half))
                for k in range(4 * half, 4 * half + 4):
                    ins = tr(ps[:, (k % 4) * P:(k % 4 + 1) * P], xn[:, CTX, k * P:(k + 1) * P], ident[:, :])
                fills(ins, ("xTc", half))

            def rotate(i, c):
                job = ("rot", i, c)
                is_drained(te, ("p", i, c, "lat"))
                if (i, c) == (3, 0):
                    te.wait_ge(s_tail, 32)
                ps = starts(job)
                fills(mm(ps[:, :], rot_m, raw[(2 * (i - 3) + c) % 2], start=True, stop=True), job)

            dve.wait(te, "hT")
            for i, (name, _, w) in enumerate(IN_ITEMS):
                n = LOADS.index(("in", i))
                load_ready(te, n)
                wt = ring[n % RING][:, 0:KC * w].rearrange("p (k c) -> p k c", k=KC)
                if name in ("gv", "rv"):
                    if rots_after(i, 0) is not None:
                        rotate(*rots_after(i, 0))
                    for t in range(TILES):
                        ps = starts(("v", i, t))
                        for k in range(KC):
                            ins = mm(ps[:, 0:ITEM], hT[:, k, t * P:(t + 1) * P], wt[:, k, :], start=(k == 0), stop=(k == KC - 1))
                        fills(ins, ("v", i, t))
                else:
                    for c in range(max(1, w // P)):
                        m = min(P, w)
                        for part, lo, hi in (("lat", 0, N_LAT), ("ctx", N_LAT, T)):
                            ps = starts(("p", i, c, part))
                            for k in range(KC):
                                ins = mm(ps[0:m, 0:hi - lo], wt[:, k, c * m:(c + 1) * m], hT[:, k, lo:hi],
                                         start=(k == 0), stop=(k == KC - 1))
                            fills(ins, ("p", i, c, part))
                        if rots_after(i, c) is not None:
                            rotate(*rots_after(i, c))
                other_modulations(i)
                if name == "glr":
                    te.wait_ge(s_gate, 32)
                    is_drained(te, ("p", i, 0, "ctx"))
                    is_drained(te, ("p", i, 0, "lat"))
                    for d in range(2):
                        for g in range(2):
                            for part, lo, hi in (("lat", 0, N_LAT), ("ctx", N_LAT, T)):
                                job = ("z", d, g, part)
                                ps = starts(job)
                                fills(mm(ps[:, 0:hi - lo], wgate[:, d, g * P:(g + 1) * P], glrT[:, lo:hi], start=True, stop=True), job)
                n = i - LEVEL_AFTER
                if 0 <= n <= NL:
                    dve.wait(te, ("lqk", n))
                    for m, (t0, t1) in enumerate(LEV_TILES):
                        for a in range(2):
                            job = ("lev", n, m, a)
                            ps = starts(job)
                            pp = slice(GLA_DK * a, GLA_DK * (a + 1))
                            for t in range(t0, t1):
                                for g in range(2):
                                    tt, o = slice(t * P, (t + 1) * P), (2 * (t - t0) + g) * P
                                    keys = (lqk if n < NL else gqk)[pp, 1, g, tt]
                                    ins = mm(ps[:, o:o + P], keys, lqk[pp, 0, g, tt], start=True, stop=True)
                            fills(ins, job)

                if i == CARRY_AFTER + 1:
                    for d in range(2):
                        dve.wait(te, ("qkF", "qkB")[d])
                        for g in range(2):
                            job = ("kT", d, g)
                            ps = starts(job)
                            for n in range(4):
                                t = CTX if n == 0 else (n - 1, LT - n)[d]
                                ins = tr(ps[:, n * P:(n + 1) * P], (lqk, lx)[d][:, 1, g, t * P:(t + 1) * P], ident[:, :])
                            fills(ins, job)
                    for n in range(4):
                        for d in range(2):
                            if n == 0:
                                is_drained(te, ("kT", d, 0))
                                is_drained(te, ("kT", d, 1))
                            job = ("gu", d, n)
                            ps = starts(job)
                            t = CTX if n == 0 else (n - 1, LT - n)[d]
                            for h in range(HEADS):
                                g, a = h // 2, h % 2
                                ins = mm(ps[GLA_DK * a:GLA_DK * (a + 1), g * P:(g + 1) * P],
                                         kTok[:, 4 * d + n, g, GLA_DK * a:GLA_DK * (a + 1)],
                                         vv[:, t, 512 + h * P:512 + (h + 1) * P], start=True, stop=True)
                            fills(ins, job)
            other_modulations(len(IN_ITEMS))
            dve.wait(te, "modc")
            ps = starts(("modT",))
            fills(tr(ps[0:64, 0:P], modc, ident[:, :]), ("modT",))

            for job, b in plan_outputs():
                if job == ("o", "g", 0):
                    te.wait_ge(s_gs0, 32)
                    for d in range(2):
                        is_drained(te, ("gu", d, 3))
                if job[0] == "T":
                    dve.wait(te, ("on", b))
                if job in (("rst", 0), ("rst", 1)):
                    dve.wait(te, "kdec")
                if job == ("o", "r", "ctx"):
                    dve.wait(te, "cmask")
                    te.wait_ge(s_rs0, 32)
                if job[0:2] == ("o", "r") and b[1] != "ctx":
                    dve.wait(te, ("rm", b[1]))
                    pool_s.wait(te, ("qd", b[1]))
                ps = starts(job)
                if job[0] == "T":
                    for a in range(4):
                        ins = tr(ps[:, a * P:(a + 1) * P], onorm[BLOCKS_OUT.index(b) % 2][:, a, :], ident[:, :])
                elif job == ("o", "g", "ctx"):
                    for h in range(HEADS):
                        ins = mm(ps[:, h * P:(h + 1) * P], att[:, CTX, h, :], vv[:, CTX, 512 + h * P:512 + (h + 1) * P],
                                 start=True, stop=True)
                elif job[0:2] == ("o", "g"):
                    h = b[1]
                    g, pp = h // 2, slice(GLA_DK * (h % 2), GLA_DK * (h % 2 + 1))
                    for t in range(LT):
                        o, tt = ps[:, t * P:(t + 1) * P], slice(t * P, (t + 1) * P)
                        mm(o, att[:, t, h, :], vv[:, t, 512 + h * P:512 + (h + 1) * P], start=True, stop=False)
                        mm(o, lqk[pp, 0, g, tt], gst[pp, 0, t, g, :], start=False, stop=False)
                        ins = mm(o, lx[pp, 0, g, tt], gst[pp, 1, LT - 1 - t, g, :], start=False, stop=True)
                elif job == ("rs", "ctx"):
                    for h in range(HEADS):
                        ins = mm(ps[:, h * P:(h + 1) * P], rqk[:, 1, h, N_LAT:T], rqk[:, 0, h, N_LAT:T], start=True, stop=True)
                elif job == ("rkT",):
                    for h in range(HEADS):
                        ins = tr(ps[:, h * P:(h + 1) * P], rqk[:, 1, h, N_LAT:T], ident[:, :])
                elif job[0] == "rst":
                    for h in range(HEADS):
                        ins = mm(ps[:, h * P:(h + 1) * P], kdec[:, job[1], h, :], vv[:, CTX, h * P:(h + 1) * P], start=True, stop=True)
                elif job[0] == "rs":
                    _, h, s = job
                    ins = mm(ps[:, :], rqk[:, 1, h, s * P:(s + 1) * P], rqk[:, 0, h, 0:N_LAT], start=True, stop=True)
                elif job == ("o", "r", "ctx"):
                    for h in range(HEADS):
                        ins = mm(ps[:, h * P:(h + 1) * P], cmask[:, h, :], vv[:, CTX, h * P:(h + 1) * P], start=True, stop=True)
                else:
                    h = b[1]
                    for t in range(LT):
                        o, tt = ps[:, t * P:(t + 1) * P], slice(t * P, (t + 1) * P)
                        for s in range(LT):
                            mm(o, rmask[h][:, s, tt], vv[:, s, h * P:(h + 1) * P], start=(s == 0), stop=False)
                        for d in range(2):
                            ins = mm(o, qd[d][:, tt], rstate[:, d, h, :], start=False, stop=(d == 1))
                fills(ins, job)

            def router(t):
                dve.wait(te, ("hn", t))
                for half in range(2):
                    ps = starts(("hT", t, half))
                    for k in range(4 * half, 4 * half + 4):
                        ins = tr(ps[:, (k % 4) * P:(k % 4 + 1) * P], hn[t % 2][:, k * P:(k + 1) * P], ident[:, :])
                    fills(ins, ("hT", t, half))
                te.wait_ge(s_rt, 16 * 5)
                ps = starts(("lg", t))
                for half in range(2):
                    is_drained(te, ("hT", t, half))
                for k in range(KC):
                    ins = mm(ps[:, 0:36], hnT[:, k, :], rtw[:, k, :], start=(k == 0), stop=(k == KC - 1))
                fills(ins, ("lg", t))

            is_drained(te, ("T", "r", HEADS - 1))
            for t in range(TILES):
                for n in range(4):
                    ld = LOADS.index(("out", n))
                    load_ready(te, ld)
                    wt = ring[ld % RING].rearrange("p (k c) -> p k c", k=KC)
                    ps = starts(("mix", t, n))
                    for k in range(KC):
                        ins = mm(ps[:, 0:ITEM], hT[:, k, t * P:(t + 1) * P], wt[:, k, :], start=(k == 0), stop=(k == KC - 1))
                    fills(ins, ("mix", t, n))
                if t >= 1:
                    router(t - 1)
            router(CTX)
            dve.wait(te, "OO")
            ps = starts(("pos",))
            for t in range(TILES):
                o = ps[:, t * NE:(t + 1) * NE]
                for s in range(t):
                    mm(o, kones, oo[:, s, :], start=(s == 0), stop=False)
                mm(o, ktri, oo[:, t, :], start=(t == 0), stop=True)
            for s in range(TILES):
                ins = mm(ps[:, TILES * NE:(TILES + 1) * NE], kones, oo[:, s, :], start=(s == 0), stop=(s == TILES - 1))
            fills(ins, ("pos",))
            dve.wait(te, "onehots")
            ps = starts(("idx",))
            for n in range(2 * TILES):
                ins = mm(ps[0:SLOTS, 0:BLOCKS], oh_slot[:, n, :], oh_block[:, n, :], start=(n == 0), stop=(n == 2 * TILES - 1))
            fills(ins, ("idx",))
            assert order[0] == len(JOBS)
            for j in JOBS[-NB1:]:
                is_drained(te, j)

            def turn_tokens(e, n, b, gathered, free):
                te.wait_ge(xg_landed[b], gathered)
                if free is not None:
                    te.wait_ge(xte_ready, free)
                te.sem_inc(turns_begun, 1)
                for k in range(KC):
                    ins = tr(bank[n][:, k * SLOTS:(k + 1) * SLOTS], xg[b][:, k * P:(k + 1) * P], ident[0:SLOTS, 0:SLOTS])
                ins.then_inc(xg_turned, 1)

            def gate_up(e, n, b, free):
                te.wait_ge(xte_ready, e + 1)
                if free is not None:
                    te.wait_ge(hid_ready, free)
                for a, w in enumerate((exg[b], exu[b])):
                    for j in range(FC):
                        o = bank[2 + n][:, (2 * a + j) * SLOTS:(2 * a + j + 1) * SLOTS]
                        for k in range(KC):
                            ins = mm(o, w[:, k, j::FC], xte[n][:, k, :], start=(k == 0), stop=(k == KC - 1))
                ins.then_inc(gu_filled, 1)

            def down(e, n, b, free):
                te.wait_ge(hid_ready, e + 1)
                if free is not None:
                    te.wait_ge(y_half0, free)
                    te.wait_ge(y_half1, free)
                for half in range(2):
                    for j in range(FC):
                        ins = mm(bank[4 + 2 * n + half][0:SLOTS, :], hid[n][:, j, :], exd[b][:, j, half * 512:(half + 1) * 512],
                                 start=(j == 0), stop=(j == FC - 1))
                ins.then_inc(y_filled, 1)

            def experts(it, first):
                for b in range(4):
                    e = 4 * it + b
                    te.wait_ge(ex_landed[b], 48 * it + 48)
                    gate_up(e, b % 2, b, None if first and b < 2 else e - 1)
                    nb = (b + 1) % 4
                    turn_tokens(e + 1, (b + 1) % 2, nb, 16 * it + (16 if b < 3 else 32), None if first and b == 0 else e)
                    down(e, b % 2, b, None if first and b < 2 else e - 1)

            turn_tokens(0, 0, 0, 16, None)
            experts(0, True)
            with te.Fori(1, NE // 4) as it:
                experts(it, False)
            dve.wait(te, "dest")
            n_over = te.value_load(over[0:1, 0:1], min_val=0, max_val=MAX_OVER)
            with te.If(n_over > 0):
                with te.Fori(0, n_over) as i:
                    turn_tokens(NE + 1 + i, 0, 0, 16 * (NE // 4 + 2) + 16 * i, NE + 1 + i)
                    te.wait_ge(ov_landed, 48 * i + 48)
                    te.wait_ge(xte_ready, NE + 2 + i)
                    for a, w in enumerate((exg[0], exu[0])):
                        for j in range(FC):
                            o = bank[2][:, (2 * a + j) * SLOTS:(2 * a + j + 1) * SLOTS]
                            for k in range(KC):
                                ins = mm(o, w[:, k, j::FC], xte[0][:, k, :], start=(k == 0), stop=(k == KC - 1))
                    ins.then_inc(gu_filled, 1)
                    down(NE + i, 0, 0, NE + i)


def host_constants():
    import numpy as np
    f = np.float32
    c = np.zeros((P, C_END), f)
    c[:, C_IDENT:C_IDENT + P] = np.eye(P)
    half, quarter = P // 2, P // 4
    rot = np.zeros((P, P), f)
    for base in (0, half):
        for i in range(quarter):
            rot[base + quarter + i, base + i] = -1.0
            rot[base + i, base + quarter + i] = 1.0
    c[:, C_ROT:C_ROT + P] = rot
    freqs = f(10000.0) ** (-np.arange(quarter, dtype=f) / f(quarter))
    t = np.arange(N_LAT)
    pos = np.stack([(t // GRID_W).astype(f), (t % GRID_W).astype(f)])
    for p in range(P):
        ang = (pos[p // half] * freqs[p % quarter]).astype(f)
        c[p, C_COS:C_COS + N_LAT] = np.cos(ang)
        c[p, C_SIN:C_SIN + N_LAT] = np.sin(ang)
    i, j = np.arange(P)[:, None], np.arange(P)[None, :]
    for n, h in enumerate(LEVELS[1:]):
        c[:, C_MASK + n * P:C_MASK + (n + 1) * P] = (i // (2 * h) == j // (2 * h)) & (i // h != j // h)
    c[:, C_MASK + 6 * P:C_MASK + 7 * P] = np.eye(P)
    c[:, C_ONES:C_ONES + P] = 1.0
    c[:, C_TRI:C_TRI + P] = i < j
    c[:, C_IOTA:C_IOTA + 64] = np.arange(64)
    c[:, C_IOTA + 64:C_IOTA + 73] = SLOTS * np.arange(1, 10)
    c[:, C_TOK:C_TOK + TILES] = np.arange(P)[:, None] + P * np.arange(TILES)
    c[:, C_POS] = np.arange(P)
    c[:, C_POS + 1] = P - 1 - np.arange(P)
    c[:, C_ONE] = (np.arange(P) % 32) // 8 == 2
    rc = np.zeros((P, R_END), f)
    rel = (np.arange(STRIP)[None, :] - np.arange(P)[:, None] - (N_LAT - P)).astype(f)
    rc[:, R_RELF:R_RELF + STRIP] = np.maximum(rel, 0)
    rc[:, R_RELB:R_RELB + STRIP] = np.maximum(-rel, 0)
    rc[:, R_TF:R_TF + N_LAT] = t + 1
    rc[:, R_TB:R_TB + N_LAT] = N_LAT - t
    return c, rc


_INS = ["x_prompt", "x_sample", "state_ret_fwd", "state_ret_bwd", "state_gla_fwd", "state_gla_bwd", "c", "c_ctx",
        "w_ada", "b_ada", "norm1_w", "w_in", "ret_decay_fwd", "ret_decay_bwd", "ret_norm_w", "gla_gate_w_fwd",
        "gla_gate_b_fwd", "gla_gate_w_bwd", "gla_gate_b_bwd", "gla_norm_w", "w_out", "norm2_w", "router_group_w",
        "router_group_b", "router_expert_w", "router_expert_b", "expert_w_gate", "expert_w_up", "expert_w_down",
        "final_norm_w"]
_OUTS = [(1, N_CTX, D), (1, N_LAT, D), (1, 1, HEADS, P, P), (1, 1, HEADS, P, P), (1, 1, HEADS, GLA_DK, P),
         (1, 1, HEADS, GLA_DK, P)]


def kernel(**inputs):
    import numpy as np
    import concourse.bacc as bacc
    from concourse.bass_utils import run_bass_kernel_spmd

    nc = bacc.Bacc("TRN2", target_bir_lowering=False, num_devices=1)
    arrays, ins = {}, []
    given = [(name, np.ascontiguousarray(inputs[name])) for name in _INS]
    for name, a in given + list(zip(("consts", "rconsts"), host_constants())):
        arrays[f"in_{name}"] = a
        ins.append(nc.dram_tensor(f"in_{name}", a.shape, mybir.dt.from_np(a.dtype), kind="ExternalInput").ap())
    outs = [nc.dram_tensor(f"out_{i}", shape, F32, kind="ExternalOutput").ap() for i, shape in enumerate(_OUTS)]
    build(nc, ins, outs)
    r = run_bass_kernel_spmd(nc, [arrays], core_ids=[0])
    return tuple(r.results[0][f"out_{i}"] for i in range(len(_OUTS)))
```

```python
from contextlib import ExitStack

import concourse.bass as bass
from concourse import mybir

P = 128
D = 1024
KC = D // P
N_LAT = 512
N_CTX = 128
T = N_LAT + N_CTX
TILES = T // P
CTX = TILES - 1
LT = N_LAT // P
HEADS = 4
GLA_DK = 64
GRID_W = 64
RANK = 16
NE = 32
NG = 4
EPG = NE // NG
DE = 256
FC = DE // P
SLOTS = 64
MAX_OVER = 19
BLOCKS = NE + MAX_OVER
EPS = 1e-6
ITEM = 256
UNIT = KC * ITEM
RING = 4
STRIP = N_LAT + N_LAT - P
LEVELS = [64, 32, 16, 8, 4, 2, 1]
LEV_TILES = [(0, 2), (2, 4), (4, 5)]
IN_COLS = 3616
POOL_TILES = 1

IN_ITEMS = [("gq", 2048, 256), ("gk", 2304, 256), ("glr", 3584, 32),
            ("rq", 0, 256), ("rq", 256, 256), ("rk", 512, 256), ("rk", 768, 256),
            ("gv", 2560, 256), ("gv", 2816, 256), ("rv", 1024, 256), ("rv", 1280, 256),
            ("gr", 3072, 256), ("gr", 3328, 256), ("rg", 1536, 256), ("rg", 1792, 256)]
CARRY_AFTER = 12
LEVEL_AFTER = 4

C_IDENT, C_ROT, C_COS, C_SIN, C_MASK = 0, 128, 256, 768, 1280
C_ONES = C_MASK + 7 * P
C_TRI = C_ONES + P
C_IOTA = C_TRI + P
C_TOK = C_IOTA + 64 + 9
C_POS = C_TOK + TILES
C_ONE = C_POS + 2
C_END = C_ONE + 1
R_RELF, R_RELB, R_TF, R_TB = 0, STRIP, 2 * STRIP, 2 * STRIP + N_LAT
R_END = 2 * STRIP + 2 * N_LAT

F32 = mybir.dt.float32
I32 = mybir.dt.int32
U32 = mybir.dt.uint32
ALU = mybir.AluOpType
ACT = mybir.ActivationFunctionType
AX = mybir.AxisListType.X


class Steps:

    def __init__(self, sem, order):
        self.sem, self.order, self.n = sem, list(order), 0

    def done(self, ins, key):
        assert self.order[self.n] == key, (self.order[self.n], key)
        self.n += 1
        ins.then_inc(self.sem, 1)

    def wait(self, eng, key):
        eng.wait_ge(self.sem, self.order.index(key) + 1)


def rots_after(i, c):
    seq = [(i, c) for i in range(3, 7) for c in range(2)] + [(7, 0)]
    return seq[seq.index((i, c)) - 1] if (i, c) in seq[1:] else None


def rest_after(i):
    return [0, 1] if i == 0 else [i + 1]


def sums_after(i):
    return {0: [], 2: [], 3: rest_after(1), 4: rest_after(2) + rest_after(3)}.get(i, rest_after(i - 1))


def plan_loads():
    loads = [("ada", m, i) for m in range(2) for i in range(4)]
    for i in range(len(IN_ITEMS)):
        loads += [("in", i)] + [("rest", r) for r in rest_after(i)]
    return loads + [("out", n) for n in range(D // ITEM)]


def plan_banks():
    jobs = [("mr", n) for n in range(4)] + [("xT", 0), ("xT", 1), ("mT",)]
    jobs += [("xT", k) for k in range(2, KC)] + [("xTc", 0), ("xTc", 1)]
    for i, (name, _, w) in enumerate(IN_ITEMS):
        if name in ("gv", "rv"):
            if rots_after(i, 0) is not None:
                jobs.append(("rot", *rots_after(i, 0)))
            jobs += [("v", i, t) for t in range(TILES)]
        else:
            for c in range(max(1, w // P)):
                jobs += [("p", i, c, "lat"), ("p", i, c, "ctx")]
                if rots_after(i, c) is not None:
                    jobs.append(("rot", *rots_after(i, c)))
        if name == "glr":
            jobs += [("z", d, g, part) for d in range(2) for g in range(2) for part in ("lat", "ctx")]
        n = i - LEVEL_AFTER
        if 0 <= n <= len(LEVELS):
            jobs += [("lev", n, m, a) for m in range(len(LEV_TILES)) for a in range(2)]
        if i == CARRY_AFTER + 1:
            jobs += [("kT", d, g) for d in range(2) for g in range(2)]
            jobs += [("gu", d, n) for n in range(4) for d in range(2)]
    jobs += [job for job, _ in plan_outputs()]
    for t in range(TILES):
        jobs += [("mix", t, n) for n in range(4)]
        if t >= 1:
            jobs += [("hT", t - 1, 0), ("hT", t - 1, 1), ("lg", t - 1)]
    jobs += [("hT", CTX, 0), ("hT", CTX, 1), ("lg", CTX)]
    jobs += [("pos",), ("idx",)]
    return jobs


def plan_outputs():
    order = [("o", "g", "ctx"), ("rs", "ctx"), ("rkT",), ("o", "g", 0), ("rs", 0, 0), ("rs", 0, 1), ("T", "g", "ctx"),
             ("o", "g", 1), ("rs", 0, 2), ("rs", 0, 3), ("T", "g", 0), ("modT",),
             ("o", "g", 2), ("rst", 0), ("rst", 1), ("T", "g", 1),
             ("o", "g", 3), ("T", "g", 2), ("o", "r", "ctx")] + [("rs", 1, s) for s in range(LT)]
    order += [("T", "g", 3), ("o", "r", 0)]
    for h in range(1, HEADS):
        order += [("rs", h + 1, s) for s in range(LT) if h + 1 < HEADS] + [("T", "r", "ctx" if h == 1 else h - 2), ("o", "r", h)]
    order += [("T", "r", 2), ("T", "r", 3)]
    return [(job, job[1:] if job[0] in "oT" else None) for job in order]


BLOCKS_OUT = [block for job, block in plan_outputs() if job[0] == "o"]


def build(nc, inp, outs):
    (x_prompt, x_sample, srf, srb, sgf, sgb, c_in, c_ctx, w_ada, b_ada, norm1_w, w_in, rdf, rdb,
     ret_norm_w, ggwf, ggbf, ggwb, ggbb, gla_norm_w, w_out, norm2_w, rgw, rgb, rew, reb,
     ewg, ewu, ewd, final_w, consts, rconsts) = inp
    y_prompt, y_sample, new_rf, new_rb, new_gf, new_gb = outs

    JOBS, LOADS = plan_banks(), plan_loads()
    NB1 = 7
    job_at = {j: n for n, j in enumerate(JOBS)}
    assert len(job_at) == len(JOBS)

    with ExitStack() as ctx:
        def sb(name, shape, dt=F32):
            return ctx.enter_context(nc.sbuf_tensor(name, shape, dt))

        def sem(name):
            return ctx.enter_context(nc.semaphore(name))

        mod_dram = nc.dram_tensor("mod_rows", (2, 6 * D), F32).ap()
        hn_dram = nc.dram_tensor("hn_rows", (T, D), F32).ap()
        ys_dram = nc.dram_tensor("expert_rows", (BLOCKS * SLOTS, D), F32).ap()

        W = sb("weights", [P, 6 * UNIT])
        X = sb("x_rows", [P, TILES, D])
        H = sb("h_cols", [P, KC * T])
        Q = sb("qkv_gates", [P, 3 * KC * T])
        G = sb("attention", [P, 5 * 4 * T])
        ident = sb("ident", [P, P])
        r_used = [0]

        def rs(*shape):
            n = 1
            for v in shape:
                n *= v
            ap = G[:, 5 * D + r_used[0]:5 * D + r_used[0] + n]
            r_used[0] += n
            return ap if len(shape) == 1 else ap.rearrange("p (a b) -> p a b", a=shape[0]) if len(shape) == 2 else \
                ap.rearrange("p (a b c) -> p a b c", a=shape[0], b=shape[1])

        onorm = [sb(f"onorm{n}", [P, 4, P]) for n in range(2)]
        idx = sb("slot_tokens", [SLOTS, BLOCKS], I32)
        idxc = [sb(f"slot_tokens_now{n}", [SLOTS, 1], I32) for n in range(4)]
        dest = sb("pick_rows", [P, 2 * TILES], I32)
        destc = sb("pick_rows_now", [P, 2 * TILES], I32)
        pickw = sb("pick_weights", [P, 2, TILES])
        over = sb("overflow", [1, 1 + MAX_OVER], I32)

        S = sb("small", [P, 1000])
        at = [0]

        def small(*shape):
            n = 1
            for v in shape:
                n *= v
            ap = S[:, at[0]:at[0] + n]
            at[0] += n
            if len(shape) == 2:
                ap = ap.rearrange("p (a b) -> p a b", a=shape[0])
            if len(shape) == 3:
                ap = ap.rearrange("p (a b c) -> p a b c", a=shape[0], b=shape[1])
            return ap

        ring = [W[:, u * UNIT:(u + 1) * UNIT] for u in range(RING)]
        tail = W[:, RING * UNIT:6 * UNIT]
        rot_m = tail[:, 0:P]
        cosT, sinT = tail[:, P:P + N_LAT], tail[:, P + N_LAT:P + 2 * N_LAT]
        masks = [tail[:, P + 2 * N_LAT + n * P:P + 2 * N_LAT + (n + 1) * P] for n in range(7)]
        glrT = tail[0:2 * RANK, 2048:2048 + T]
        wgate = tail[0:2 * RANK, 2688:3200].rearrange("p (d n) -> p d n", d=2)
        ones_s = tail[:, 3200:3328]
        sq = tail[:, 3584:4096].rearrange("p (a b) -> p a b", a=4)
        first_mod_rows = G[0:2, 16 * T:16 * T + 2 * D]
        rstate = tail[:, 0:1024].rearrange("p (d h e) -> p d h e", d=2, h=HEADS)
        kdec = tail[:, 1024:2048].rearrange("p (d h e) -> p d h e", d=2, h=HEADS)
        rsout = tail[:, 2048:3072].rearrange("p (d h e) -> p d h e", d=2, h=HEADS)
        cmask = tail[:, 3072:3584].rearrange("p (h t) -> p h t", h=HEADS)

        hT = H[:, :].rearrange("p (k t) -> p k t", k=KC)
        rqk = Q[:, 0:KC * T].rearrange("p (a h t) -> p a h t", a=2, h=HEADS)
        vv = Q[:, KC * T:2 * KC * T].rearrange("p (t c) -> p t c", t=TILES)
        gates = Q[:, 2 * KC * T:3 * KC * T].rearrange("p (h t) -> p h t", h=2 * HEADS)
        xn = Q[:, 2 * KC * T:3 * KC * T].rearrange("p (t c) -> p t c", t=TILES)
        g0 = 2 * KC * T
        raw = [Q[:, g0 + n * N_LAT:g0 + (n + 1) * N_LAT] for n in range(2)]
        rsin = Q[:, g0 + 2 * N_LAT:g0 + 3 * N_LAT]
        g4 = 4 * T
        gqk_f, cum_f, lx_f, lqk_f = (G[:, n * g4:(n + 1) * g4] for n in range(4))
        gqk, cum, lx, lqk = (v.rearrange("p (a g t) -> p a g t", a=2, g=2) for v in (gqk_f, cum_f, lx_f, lqk_f))
        att = G[:, 4 * g4:5 * g4].rearrange("p (t h q) -> p t h q", t=TILES, h=HEADS)
        kTok = tail[:, 0:2048].rearrange("p (n g c) -> p n g c", n=8, g=2)
        gst = G[:, g4:g4 + 2048].rearrange("p (d n g e) -> p d n g e", d=2, n=4, g=2)
        gsout = G[:, g4 + 2048:g4 + 2560].rearrange("p (d g e) -> p d g e", d=2, g=2)
        xf = X[:, :, :].rearrange("p t c -> p (t c)")
        strips = xf[:, 0:4 * STRIP].rearrange("p (h x) -> p h x", h=HEADS)
        tft = [xf[:, 4 * STRIP + n * N_LAT:4 * STRIP + (n + 1) * N_LAT] for n in range(2)]
        macc = [v.rearrange("p (a c) -> p a c", a=2) for v in (tail[:, 3328:3840], xf[:, 4 * STRIP + 2 * N_LAT:TILES * D])]
        rel = [Q[:, g0 + 3 * N_LAT + n * STRIP:g0 + 3 * N_LAT + (n + 1) * STRIP] for n in range(2)]
        stmp = [Q[:, g0 + 3 * N_LAT + n * STRIP:g0 + 3 * N_LAT + (n + 1) * STRIP] for n in range(2, 4)]
        qd = [G[:, n * N_LAT:(n + 1) * N_LAT] for n in range(2)]
        qtab = [G[:, (2 + n) * N_LAT:(3 + n) * N_LAT] for n in range(2)]
        rmask = [v.rearrange("p (s t) -> p s t", s=LT)
                 for v in (H[:, 0:2048], G[:, g4:g4 + 2048], G[:, g4 + 2048:g4 + 4096], G[:, g4:g4 + 2048])]
        hnT = G[:, 0:D].rearrange("p (k t) -> p k t", k=KC)
        mt = [G[:, (1 + n) * D:(2 + n) * D] for n in range(2)]
        hn = [G[:, (3 + n) * D:(4 + n) * D] for n in range(2)]
        a2b = [G[:, (5 + n) * D:(6 + n) * D] for n in range(2)]
        g1b = [G[:, (7 + n) * D:(8 + n) * D] for n in range(2)]
        b2b = [G[:, (9 + n) * D:(10 + n) * D] for n in range(2)]
        rtw = G[:, 11 * D:11 * D + KC * 36].rearrange("p (k n) -> p k n", k=KC)
        rk0 = 11 * D + KC * 36
        kones, ktri = G[:, rk0:rk0 + P], G[:, rk0 + P:rk0 + 2 * P]
        kiota = G[:, rk0 + 2 * P:rk0 + 2 * P + C_END - C_IOTA]
        rbias = G[:, rk0 + 400:rk0 + 436]
        lgt = G[:, rk0 + 440:rk0 + 440 + TILES * 36].rearrange("p (t n) -> p t n", t=TILES)
        g2b = [Q[:, 12288 + n * D:12288 + (n + 1) * D] for n in range(2)]
        fnb = Q[:, 12288 + 2 * D:12288 + 3 * D]
        exb = [Q[:, 0:3 * UNIT], Q[:, 3 * UNIT:6 * UNIT], W[:, 0:3 * UNIT], W[:, 3 * UNIT:6 * UNIT]]
        exg = [v[:, 0:UNIT].rearrange("p (k f) -> p k f", k=KC) for v in exb]
        exu = [v[:, UNIT:2 * UNIT].rearrange("p (k f) -> p k f", k=KC) for v in exb]
        exd = [v[:, 2 * UNIT:3 * UNIT].rearrange("p (j n) -> p j n", j=FC) for v in exb]
        xg = [H[0:SLOTS, n * D:(n + 1) * D] for n in range(4)]
        xte = [H[:, 4 * D + n * 512:4 * D + (n + 1) * 512].rearrange("p (k s) -> p k s", k=KC) for n in range(2)]
        yb = [G[0:SLOTS, (3 + n) * D:(4 + n) * D] for n in range(2)]
        sil = [G[:, D + n * P:D + (n + 1) * P] for n in range(2)]
        hid = [G[:, D + (2 + n) * P:D + (3 + n) * P].rearrange("p (j s) -> p j s", j=FC) for n in range(2)]
        yp = [[Q[:, (2 * t + k) * D:(2 * t + k + 1) * D] for k in range(2)] for t in range(TILES)]
        yo = [W[:, t * D:(t + 1) * D] for t in range(TILES)]

        cT, cS = small(2, KC), small(2, KC)
        modc, modr = small(64), small(P)
        brow, wrow = small(P), small(P)
        bcol, n1col = small(2, KC), small(KC)
        mcol = small(2 * 2, KC)
        ccol = small(C_END - C_IOTA)
        ss, rstd = small(TILES), small(TILES)
        lg = small(2, HEADS)
        gbias = small(2, 2)
        nw = small(2 * HEADS)
        tot, dec = small(4, TILES), small(4, TILES)
        wcol = small(2, HEADS)
        power = small(TILES)
        ones_c = small(1)
        marks = small(len(BLOCKS_OUT))
        st1, st2, st3 = small(4), small(4), small(4)

        rdiff = rs(TILES * (NG + 1))
        oo = rs(TILES, NE)
        oh_slot = rs(2 * TILES, SLOTS)
        oh_block = rs(2 * TILES, BLOCKS)

        bank = [ctx.enter_context(nc.psum_tensor(f"bank{n}", [P, 512], F32)) for n in range(8)]
        mod_ps = bank[7]

        filled = [sem(f"bank{n}_filled") for n in range(NB1)]
        drained = [sem(f"bank{n}_drained") for n in range(NB1)]

        def where(job):
            n = job_at[job]
            return n % NB1, n // NB1

        def bk(job):
            return bank[where(job)[0]]

        def is_filled(eng, job):
            b, turn = where(job)
            eng.wait_ge(filled[b], turn + 1)

        def is_drained(eng, job):
            b, turn = where(job)
            eng.wait_ge(drained[b], turn + 1)

        def drains(ins, job):
            ins.then_inc(drained[where(job)[0]], 1)

        landed = [sem(f"ring{n}_landed") for n in range(RING)]
        ada_used = sem("ada_used")
        mod_summed = sem("mod_summed")
        s_cond, s_ident, s_tail, s_cols, s_gate, s_row = (
            sem(n) for n in ("cond_landed", "ident_landed", "tables_landed", "columns_landed", "gate_landed", "rows_landed"))
        s_x = [sem(f"x{t}_landed") for t in range(TILES)]
        s_x2 = [sem(f"x{t}_again") for t in range(TILES)]
        s_modw = sem("mod_written")
        s_gs0, s_rc, s_rs0 = sem("gla_states_landed"), sem("strip_inputs_landed"), sem("ret_states_landed")
        s_zero, s_mrow = sem("zeros_written"), sem("mod_rows_landed")
        s_out, s_gout = sem("ret_states_written"), sem("gla_states_written")
        s_bc, s_rt, s_fin = sem("norm2_rows_landed"), sem("router_landed"), sem("final_rows_landed")
        s_hnw = [sem(f"hn_written{n}") for n in range(2)]
        dve_chain, act_chain, pool_chain = sem("vector_chain"), sem("scalar_chain"), sem("gpsimd_chain")

        NL = len(LEVELS)
        dve_order = ["ms0", "mcol", "hT"]
        act_order = ["cS"] + [("ss", t) for t in range(TILES)] + [("xn", t) for t in range(TILES)] + ["lg", "softplus"]
        pool_order = ["rs0"]
        for i in range(len(IN_ITEMS)):
            n = i - LEVEL_AFTER + 1
            if IN_ITEMS[i][0] == "glr":
                dve_order += ["zb", "cum"]
            if IN_ITEMS[i][0] in ("rq", "rk"):
                pool_order += [("cos", i, c) for c in range(2)]
            if 7 <= i < 7 + HEADS:
                act_order += [("strip", i - 7, d) for d in range(2)]
                pool_order += [("sel", i - 7, d) for d in range(2)]
                dve_order += [("strip", i - 7)]
            if 0 <= n < NL:
                pool_order += [("sub", n)]
                act_order += [("exp", n)]
            if 0 <= n <= NL:
                dve_order += [("lqk", n)]
            dve_order += [("acc", r) for r in rest_after(i)]
            if i == CARRY_AFTER:
                pool_order += ["subF", "subB"]
                act_order += ["expF", "expB"]
                dve_order += ["qkF", "qkB"]
        act_order += [("qtab", 0), "wcol"]
        pool_order += [("qd", 0)]
        for job, block in plan_outputs():
            n = BLOCKS_OUT.index(block) if block else None
            if job == ("o", "g", 0):
                dve_order += ["modc"]
            if job[0] == "o":
                dve_order += ([("cen", block)] if block[0] == "r" else []) + ([("on", BLOCKS_OUT[n - 1])] if n else []) + [("ms", block)]
                if block[0] == "r" and block[1] != "ctx" and block[1] < HEADS - 1:
                    act_order += [("qtab", block[1] + 1)]
                    pool_order += [("qd", block[1] + 1)]
                act_order += [("sq", block)]
                pool_order += [("rs", block)]
            elif job == ("rs", "ctx"):
                dve_order += ["cmask"]
            elif job == ("rkT",):
                dve_order += ["kdec"]
            elif job[0] == "rs" and job[2] == LT - 1:
                dve_order += [("rm", job[1])]
            if job == ("T", "r", 2):
                dve_order += [("on", BLOCKS_OUT[-1])]
        dve_order += [k for t in range(TILES) for k in (("x2", t), ("ms2", t), ("hn", t))]
        dve_order += ["diffs", "OO", "onehots", "idx", "dest"]
        act_order += [("ss2", t) for t in range(TILES)] + ["rexp"]
        pool_order += [("rs2", t) for t in range(TILES)]
        dve = Steps(sem("vector_steps"), dve_order)
        act = Steps(sem("scalar_steps"), act_order)
        pool_s = Steps(sem("gpsimd_steps"), pool_order)
        pool_done = pool_s.done

        def w_src(n):
            load, slot = LOADS[n], ring[n % RING]
            if load[0] == "ada":
                _, m, i = load
                return (w_ada[0].rearrange("(p k) c -> p k c", k=KC)[:, 2 * i:2 * i + 2, m * D:(m + 1) * D],
                        slot.rearrange("p (k c) -> p k c", k=2))
            if load[0] == "rest":
                c0 = 2 * D + load[1] * ITEM
                return (w_ada[0, :, c0:c0 + ITEM].rearrange("(p k) c -> p k c", k=KC), slot.rearrange("p (k c) -> p k c", k=KC))
            if load[0] == "in":
                _, c0, w = IN_ITEMS[load[1]]
                return (w_in[0, :, c0:c0 + w].rearrange("(p k) c -> p k c", k=KC),
                        slot[:, 0:KC * w].rearrange("p (k c) -> p k c", k=KC))
            return (w_out[0, :, load[1] * ITEM:(load[1] + 1) * ITEM].rearrange("(k p) c -> p k c", k=KC),
                    slot.rearrange("p (k c) -> p k c", k=KC))

        def load_used(eng, n):
            load = LOADS[n]
            if load[0] == "ada":
                _, m, i = load
                if i < 3:
                    eng.wait_ge(ada_used, 3 * m + i + 1)
                else:
                    is_filled(eng, ("mr", 2 * m + 1))
            elif load[0] == "rest":
                dve.wait(eng, ("acc", load[1]))
            elif load[0] == "in":
                name, _, w = IN_ITEMS[load[1]]
                is_filled(eng, ("v", load[1], CTX) if name in ("gv", "rv") else ("p", load[1], max(1, w // P) - 1, "ctx"))
            else:
                is_filled(eng, ("mix", CTX, load[1]))

        def load_ready(eng, n):
            eng.wait_ge(landed[n % RING], 16 * (n // RING + 1))

        ex_landed = [sem(f"expert_weights{n}_landed") for n in range(4)]
        xg_landed = [sem(f"tokens{n}_landed") for n in range(4)]
        xg_turned, xte_ready, gu_filled = sem("tokens_turned"), sem("tokens_ready"), sem("gate_up_filled")
        sil_ready, hid_ready, y_filled = sem("silu_ready"), sem("hidden_ready"), sem("expert_done")
        y_half0, y_half1 = sem("y_half0"), sem("y_half1")
        ys_written = [sem(f"expert_rows_written{n}") for n in range(2)]
        ov_landed = sem("overflow_weights_landed")
        idxc_set = sem("slot_tokens_set")
        turns_begun, gathers_begun = sem("turns_begun"), sem("gathers_begun")
        yp_landed = [[sem(f"pick{k}_rows{n}_landed") for k in range(2)] for n in range(TILES)]
        y1_scaled, x3_ready, ss3_ready, yo_ready = sem("first_picks_weighted"), sem("x3_ready"), sem("ss3_ready"), sem("final_ready")
        ms3_ready, rs3_ready = sem("final_squares_ready"), sem("final_roots_ready")
        yo_ready_pool = sem("final_ready_gpsimd")
        yo_scaled, yo_written = sem("final_scaled"), sem("final_written")

        block = ctx.enter_context(nc.Block())

        @block.sync
        def _(sp):
            for n in range(len(LOADS)):
                src, dst = w_src(n)
                if n >= RING:
                    load_used(sp, n - RING)
                sp.dma_start(dst, src).then_inc(landed[n % RING], 16)

            def load_expert(e, b, s):
                sp.dma_start(exb[b][:, 0:UNIT], ewg_v[bass.ds(e * P, P), :]).then_inc(s, 16)
                sp.dma_start(exb[b][:, UNIT:2 * UNIT], ewu_v[bass.ds(e * P, P), :]).then_inc(s, 16)
                sp.dma_start(exb[b][:, 2 * UNIT:3 * UNIT], ewd_v[bass.ds(e * P, P), :]).then_inc(s, 16)

            ewg_v = ewg.rearrange("a e (p k) f -> (a e p) (k f)", p=P)
            ewu_v = ewu.rearrange("a e (p k) f -> (a e p) (k f)", p=P)
            ewd_v = ewd.rearrange("a e (p j) n -> (a e p) (j n)", p=P)

            def mod_rows(m, dst):
                for cond in range(2):
                    sp.dma_start(dst[cond], mod_dram[cond:cond + 1, m * D:(m + 1) * D].partition_broadcast(P)).then_inc(s_bc, 16)

            is_drained(sp, ("modT",))
            for cond in range(2):
                sp.dma_start(mod_dram[cond:cond + 1, 2 * D:6 * D].rearrange("a (c n) -> (a c) n", n=P),
                               modr[cond * 32:(cond + 1) * 32, :]).then_inc(s_modw, 16)
            is_filled(sp, ("o", "g", HEADS - 1))
            sp.wait_ge(s_modw, 32)
            mod_rows(2, g1b)
            mod_rows(3, b2b)
            sp.dma_start(rtw[:, :, 0:NG], rgw[0].rearrange("(p k) n -> p k n", k=KC)).then_inc(s_rt, 16)
            sp.dma_start(rtw[:, :, NG:NG + NE], rew[0].rearrange("(p k) n -> p k n", k=KC)).then_inc(s_rt, 16)
            sp.dma_start(G[:, rk0:rk0 + C_END - C_ONES], consts[:, C_ONES:C_END]).then_inc(s_rt, 16)
            sp.dma_start(rbias[:, 0:NG], rgb[0:1, :].partition_broadcast(P)).then_inc(s_rt, 16)
            sp.dma_start(rbias[:, NG:NG + NE], reb[0:1, :].partition_broadcast(P)).then_inc(s_rt, 16)
            is_filled(sp, ("o", "r", HEADS - 2))
            mod_rows(4, a2b)
            is_drained(sp, ("T", "r", HEADS - 1))
            for b in range(2):
                load_expert(b, b, ex_landed[b])
            load_used(sp, len(LOADS) - 1)
            sp.wait_ge(s_out, 16 * 2)
            for b in range(2, 4):
                load_expert(b, b, ex_landed[b])
            for cond in range(2):
                sp.dma_start(g2b[cond], mod_dram[cond:cond + 1, 5 * D:6 * D].partition_broadcast(P)).then_inc(s_fin, 16)
            sp.dma_start(fnb, final_w.rearrange("(a n) -> a n", a=1).partition_broadcast(P)).then_inc(s_fin, 16)
            with sp.Fori(1, NE // 4) as it:
                for b in range(4):
                    sp.wait_ge(y_filled, 4 * it + b - 3)
                    load_expert(4 * it + b, b, ex_landed[b])
            dve.wait(sp, "dest")
            n_over = sp.value_load(over[0:1, 0:1], min_val=0, max_val=MAX_OVER)
            with sp.If(n_over > 0):
                with sp.Fori(0, n_over) as i:
                    e = sp.value_load(over[0:1, bass.ds(i + 1, 1)], min_val=0, max_val=NE - 1)
                    sp.wait_ge(y_filled, NE + i)
                    load_expert(e, 0, ov_landed)
            ya = y_sample.rearrange("a t d -> (a t) d")
            yc = y_prompt.rearrange("a t d -> (a t) d")
            for t in range(TILES):
                if t < POOL_TILES:
                    sp.wait_ge(yo_ready_pool, t + 1)
                else:
                    sp.wait_ge(yo_ready, t - POOL_TILES + 1)
                dst = ya[t * P:(t + 1) * P, :] if t < LT else yc[:, :]
                sp.dma_start(dst, yo[t]).then_inc(yo_written, 16)
            sp.wait_ge(yo_written, 16 * TILES)
            sp.wait_ge(s_out, 16 * 2)
            sp.wait_ge(s_gout, 16 * 2)

        @block.gpsimd
        def _(pool):
            chain = [0]

            def link(ins):
                chain[0] += 1
                ins.then_inc(pool_chain, 1)
                pool.wait_ge(pool_chain, chain[0])

            for m in range(2):
                pool.dma_start(bcol[:, m, :], b_ada[0, m * D:(m + 1) * D].rearrange("(p k) -> p k", k=KC)).then_inc(s_row, 16)
            pool.dma_start(n1col, norm1_w[0].rearrange("(p k) -> p k", k=KC)).then_inc(s_row, 16)
            with nc.allow_non_contiguous_dma(reason="small columns"):
                for d, v in enumerate((ggbf, ggbb)):
                    pool.dma_start(gbias[:, d, :], v[0].rearrange("(g p) -> p g", p=P)).then_inc(s_cols, 16)
                for d, v in enumerate((ret_norm_w, gla_norm_w)):
                    pool.dma_start(nw[:, 4 * d:4 * d + 4], v[0].rearrange("(h p) -> p h", p=P)).then_inc(s_cols, 16)
            for d, v in enumerate((rdf, rdb)):
                pool.dma_start(lg[:, d, :], v[0:1, :].partition_broadcast(P)).then_inc(s_cols, 16)
            link(nc.gpsimd.memset(wgate, 0.0))
            for d, v in enumerate((ggwf, ggwb)):
                pool.dma_start(wgate[RANK * d:RANK * (d + 1), d, :], v[0]).then_inc(s_gate, 16)
            link(nc.gpsimd.memset(power, -0.5))
            link(nc.gpsimd.memset(ones_c, 1.0))
            zero = onorm[0][0:SLOTS].rearrange("p a e -> p (a e)")
            link(nc.gpsimd.memset(zero, 0.0))
            link(nc.gpsimd.memset(wrow, 1.0))
            for cond in range(2):
                r0 = cond * 32
                pool.dma_start(brow[r0:r0 + 32, :], b_ada[0, 2 * D:6 * D].rearrange("(c n) -> c n", n=P)).then_inc(s_mrow, 16)
                pool.dma_start(wrow[r0 + 16:r0 + 24, :], norm2_w[0].rearrange("(c n) -> c n", n=P)).then_inc(s_mrow, 16)

            def root(ap, key, rkey):
                dve.wait(pool, key)
                pool_done(nc.gpsimd.tensor_tensor(ap, ap, power[:, 0:ap.shape[1]], ALU.pow), rkey)

            root(rstd, "ms0", "rs0")

            is_filled(pool, ("xTc", 1))
            for n, (dst, c0) in enumerate(((rel[0], R_RELF), (rel[1], R_RELB), (tft[0], R_TF), (tft[1], R_TB))):
                pool.dma_start(dst, rconsts[:, c0:c0 + dst.shape[1]]).then_inc(s_rc, 16)

            def level_exponents(n):
                h = LEVELS[n]
                nb = T // (2 * h)
                v = [cum[:, d].rearrange("p g (b two h) -> p g b two h", two=2, h=h) for d in range(2)]
                o = [lx[:, a].rearrange("p g (b two h) -> p g b two h", two=2, h=h) for a in range(2)]
                shape = [P, 2, nb, h]
                ref = [v[0][:, :, :, 0, h - 1:h].to_broadcast(shape), v[1][:, :, :, 1, 0:1].to_broadcast(shape)]
                if n == 0:
                    dve.wait(pool, "cum")
                else:
                    dve.wait(pool, ("lqk", n - 1))
                nc.gpsimd.tensor_tensor(o[0][:, :, :, 1], v[0][:, :, :, 1], ref[0], ALU.subtract)
                nc.gpsimd.tensor_tensor(o[0][:, :, :, 0], ref[1], v[1][:, :, :, 0], ALU.subtract)
                nc.gpsimd.tensor_tensor(o[1][:, :, :, 0], ref[0], v[0][:, :, :, 0], ALU.subtract)
                pool_done(nc.gpsimd.tensor_tensor(o[1][:, :, :, 1], v[1][:, :, :, 1], ref[1], ALU.subtract), ("sub", n))

            pool.wait_ge(s_tail, 16 * 2)
            for i, (name, _, w) in enumerate(IN_ITEMS):
                if name in ("rq", "rk"):
                    for c in range(2):
                        a, h = ("rq", "rk").index(name), 2 * ((i - 3) % 2) + c
                        n = 2 * (i - 3) + c
                        is_drained(pool, ("p", i, c, "lat"))
                        pool_done(nc.gpsimd.tensor_tensor(rqk[:, a, h, 0:N_LAT], raw[n % 2], cosT, ALU.mult), ("cos", i, c))
                if i == 7:
                    for half in range(2):
                        pool.dma_start(ys_dram[NE * SLOTS:, half * 512:(half + 1) * 512].rearrange("(b s) d -> s b d", s=SLOTS),
                                       zero.unsqueeze(1).to_broadcast([SLOTS, MAX_OVER, 512])).then_inc(s_zero, 16)
                if 7 <= i < 7 + HEADS:
                    h = i - 7
                    for d in range(2):
                        o = strips[:, h, :] if d == 0 else stmp[h % 2]
                        act.wait(pool, ("strip", h, d))
                        sgn = 1 - 2 * d
                        pool_done(nc.gpsimd.affine_select(out=o, in_=o, compare_op=ALU.is_ge, fill=0.0,
                                                          base=-sgn * (N_LAT - P), pattern=[[sgn, STRIP]],
                                                          channel_multiplier=-sgn), ("sel", h, d))
                if 0 <= i - LEVEL_AFTER + 1 < NL:
                    level_exponents(i - LEVEL_AFTER + 1)
                if i == CARRY_AFTER:
                    tb = [tot[:, 2 * d:2 * d + 2, :].unsqueeze(3).to_broadcast([P, 2, TILES, P]) for d in range(2)]
                    tv = [cum[:, d].rearrange("p g (t n) -> p g t n", n=P) for d in range(2)]
                    ov = [lx[:, a].rearrange("p g (t n) -> p g t n", n=P) for a in range(2)]
                    dve.wait(pool, ("lqk", NL - 1))
                    pool_done(nc.gpsimd.tensor_tensor(ov[1], tb[0], tv[0], ALU.subtract), "subF")
                    dve.wait(pool, "qkF")
                    pool_done(nc.gpsimd.tensor_tensor(ov[0], tb[1], tv[1], ALU.subtract), "subB")
                    act.wait(pool, "expB")
                    for d, v in enumerate((sgf, sgb)):
                        pool.dma_start(gst[:, d, 0], v[0, 0].rearrange("(g a) d e -> (a d) g e", a=2)).then_inc(s_gs0, 16)
            is_filled(pool, ("gu", 1, 3))
            for d, v in enumerate((srf, srb)):
                pool.dma_start(rstate[:, d], v[0, 0].rearrange("h d e -> d h e")).then_inc(s_rs0, 16)

            def scaled_queries(h):
                act.wait(pool, ("qtab", h))
                if h >= 1:
                    is_filled(pool, ("o", "r", h - 1))
                link(nc.gpsimd.tensor_tensor(qd[0], rqk[:, 0, h, 0:N_LAT], qtab[0], ALU.mult))
                pool_done(nc.gpsimd.tensor_tensor(qd[1], rqk[:, 0, h, 0:N_LAT], qtab[1], ALU.mult), ("qd", h))

            scaled_queries(0)
            for b in BLOCKS_OUT:
                if b[0] == "r" and b[1] != "ctx" and b[1] < HEADS - 1:
                    scaled_queries(b[1] + 1)
                root(st2, ("ms", b), ("rs", b))
            for t in range(TILES):
                root(rstd[:, t:t + 1], ("ms2", t), ("rs2", t))

            def gather_block(col, b):
                nc.gpsimd.tensor_copy(idxc[b][:, :], idx[:, col]).then_inc(idxc_set, 1)

            def gather_rows(b, count):
                pool.wait_ge(idxc_set, count)
                pool.sem_inc(gathers_begun, 1)
                pool.indirect_dma_start(xg[b], None, hn_dram[:, :], bass.IndirectOffsetOnAxis(ap=idxc[b][:, :].bitcast(U32), axis=0)
                                        ).then_inc(xg_landed[b], 16)

            dve.wait(pool, "idx")
            for n in range(2):
                pool.wait_ge(s_hnw[n], 16 * (3 - n))
            is_filled(pool, ("mix", CTX, 3))
            for b in range(4):
                gather_block(slice(b, b + 1), b)
                gather_rows(b, b + 1)
            with pool.Fori(1, NE // 4) as it:
                for b in range(4):
                    pool.wait_ge(xg_turned, 4 * it + b - 3)
                    gather_block(bass.ds(4 * it + b, 1), b)
                    gather_rows(b, 4 * it + b + 1)
            pool.wait_ge(xg_turned, NE - 3)
            gather_block(slice(NE, NE + 1), 0)
            gather_rows(0, NE + 1)
            dve.wait(pool, "dest")
            n_over = pool.value_load(over[0:1, 0:1], min_val=0, max_val=MAX_OVER)
            with pool.If(n_over > 0):
                with pool.Fori(0, n_over) as i:
                    pool.wait_ge(xg_turned, NE + 1 + i)
                    gather_block(bass.ds(NE + i, 1), 0)
                    gather_rows(0, NE + 2 + i)
            link(nc.gpsimd.tensor_copy(destc[:, :], dest[:, :]))
            pool.wait_ge(ys_written[0], n_over * 16 + 16 * (NE // 2))
            pool.wait_ge(ys_written[1], 16 * (NE // 2))
            pool.wait_ge(y_filled, n_over + NE)
            pool.sem_inc(gathers_begun, 1)

            for t in range(TILES):
                for k in range(2):
                    pool.indirect_dma_start(yp[t][k], None, ys_dram[:, :],
                                            bass.IndirectOffsetOnAxis(ap=destc[:, k * TILES + t:k * TILES + t + 1].bitcast(U32), axis=0)
                                            ).then_inc(yp_landed[t][k], 16)
            for t in range(TILES):
                pool.wait_ge(ms3_ready, t + 1)
                nc.gpsimd.tensor_tensor(rstd[:, t:t + 1], rstd[:, t:t + 1], power[:, 0:1], ALU.pow).then_inc(rs3_ready, 1)
                if t < POOL_TILES:
                    pool.wait_ge(yo_scaled, t + 1)
                    nc.gpsimd.tensor_tensor(yo[t], yo[t], fnb, ALU.mult).then_inc(yo_ready_pool, 1)

        @block.scalar
        def _(sc):
            chain = [0]

            def link(ins):
                chain[0] += 1
                ins.then_inc(act_chain, 1)
                sc.wait_ge(act_chain, chain[0])

            f = nc.scalar.activation
            for cond, v in enumerate((c_in[0], c_ctx)):
                sc.dma_start(cT[:, cond, :], v.rearrange("(p k) -> p k", k=KC)).then_inc(s_cond, 16)
            sc.dma_start(ident[:, :], consts[:, C_IDENT:C_IDENT + P]).then_inc(s_ident, 16)
            xs = x_sample.rearrange("a t d -> (a t) d")
            for t in range(TILES):
                sc.dma_start(X[:, t, :], xs[t * P:(t + 1) * P, :] if t < LT else x_prompt[0]).then_inc(s_x[t], 16)
            sc.dma_start(ccol, consts[:, C_IOTA:C_END]).then_inc(s_ident, 16)
            sc.wait_ge(s_cond, 32)
            act.done(f(cS, cT, ACT.Silu), "cS")
            for t in range(TILES):
                sc.wait_ge(s_x[t], 16)
                act.done(f(xn[:, t, :], X[:, t, :], ACT.Square, accum_out=ss[:, t:t + 1]), ("ss", t))
            pool_s.wait(sc, "rs0")
            for t in range(TILES):
                act.done(f(xn[:, t, :].rearrange("p (k j) -> p k j", k=KC), X[:, t, :].rearrange("p (j k) -> p k j", k=KC),
                           ACT.Copy, scale=rstd[:, t:t + 1]), ("xn", t))
            for n in (0, 2):
                is_filled(sc, ("mr", n))
                drains(f(first_mod_rows[:, n * 512:(n + 1) * 512], bk(("mr", n))[0:2, :], ACT.Copy), ("mr", n))
            sc.dma_start(tail[:, 0:2048], consts[:, C_ROT:C_ONES]).then_inc(s_tail, 16)
            sc.dma_start(ones_s, consts[:, C_ONES:C_ONES + P]).then_inc(s_tail, 16)
            dve.wait(sc, "mcol")
            for k in range(1, KC, 2):
                is_filled(sc, ("xT", k))
                drains(f(hT[:, k, 0:N_LAT], bk(("xT", k))[:, :], ACT.Identity, scale=mcol[:, 2, k:k + 1],
                         bias=mcol[:, 0, k:k + 1]), ("xT", k))
            sc.wait_ge(s_cols, 16 * 6)
            link(f(lg, lg, ACT.Exp))
            act.done(f(lg, lg, ACT.Copy, scale=-1.0), "lg")

            def query_tables(h):
                if h == 0:
                    dve.wait(sc, "qkB")
                else:
                    pool_s.wait(sc, ("qd", h - 1))
                link(f(qtab[0], tft[0], ACT.Exp, scale=lg[:, 0, h:h + 1]))
                act.done(f(qtab[1], tft[1], ACT.Exp, scale=lg[:, 1, h:h + 1]), ("qtab", h))

            for i, (name, _, w) in enumerate(IN_ITEMS):
                if name in ("gv", "rv"):
                    off = (512 if name == "gv" else 0) + ITEM * ((i - 7) % 2)
                    for t in range(TILES):
                        is_filled(sc, ("v", i, t))
                        drains(f(vv[:, t, off:off + ITEM], bk(("v", i, t))[:, 0:ITEM], ACT.Copy), ("v", i, t))
                else:
                    for c in range(max(1, w // P)):
                        n = 2 * (i - 3) + c
                        for part, lo, hi in (("lat", 0, N_LAT), ("ctx", N_LAT, T)):
                            job = ("p", i, c, part)
                            src = bk(job)[:, 0:hi - lo]
                            is_filled(sc, job)
                            if name == "gq":
                                drains(f(gqk[:, 0, c, lo:hi], src, ACT.Copy, scale=GLA_DK ** -0.5), job)
                            elif name == "gk":
                                drains(f(gqk[:, 1, c, lo:hi], src, ACT.Copy), job)
                            elif name == "glr":
                                drains(f(glrT[:, lo:hi], src[0:2 * RANK, :], ACT.Copy), job)
                            elif name in ("rq", "rk"):
                                a, h = ("rq", "rk").index(name), 2 * ((i - 3) % 2) + c
                                s = float(P) ** -0.5 if a else 1.0
                                if part == "lat":
                                    if n == 0:
                                        is_filled(sc, ("xTc", 1))
                                    if n >= 2:
                                        j = (3 + (n - 2) // 2, (n - 2) % 2)
                                        pool_s.wait(sc, ("cos", *j))
                                        is_filled(sc, ("rot", *j))
                                    drains(f(raw[n % 2], src, ACT.Copy, scale=s), job)
                                else:
                                    drains(f(rqk[:, a, h, lo:hi], src, ACT.Copy, scale=s), job)
                            else:
                                h = 2 * ((i - 11) % 2) + c + (4 if name == "gr" else 0)
                                if i == 11 and c == 0 and part == "lat":
                                    is_drained(sc, ("rot", 6, 1))
                                    dve.wait(sc, ("strip", HEADS - 1))
                                drains(f(gates[:, h, lo:hi], src, ACT.Silu), job)
                if name == "glr":
                    dve.wait(sc, "zb")
                    link(f(lx_f, cum_f, ACT.Abs))
                    link(f(lx_f, lx_f, ACT.Exp, scale=-1.0))
                    act.done(f(lx_f, lx_f, ACT.Ln, bias=1.0), "softplus")
                if 7 <= i < 7 + HEADS:
                    h = i - 7
                    if h == 0:
                        sc.wait_ge(s_rc, 16 * 4)
                    for d in range(2):
                        if d == 1 and h >= 2:
                            dve.wait(sc, ("strip", h - 2))
                        act.done(f(strips[:, h, :] if d == 0 else stmp[h % 2], rel[d], ACT.Exp, scale=lg[:, d, h:h + 1]),
                                 ("strip", h, d))
                n = i - LEVEL_AFTER + 1
                if 0 <= n < NL:
                    pool_s.wait(sc, ("sub", n))
                    act.done(f(lx_f, lx_f, ACT.Exp, scale=1.0 / 16.0), ("exp", n))
                if i == CARRY_AFTER:
                    link(f(dec, tot, ACT.Exp, scale=1.0 / 16.0))
                    pool_s.wait(sc, "subF")
                    link(f(lx[:, 1], lx[:, 1], ACT.Exp, scale=1.0 / 16.0))
                    act.done(f(lx[:, 0], cum[:, 0], ACT.Exp, scale=1.0 / 16.0), "expF")
                    pool_s.wait(sc, "subB")
                    link(f(lx[:, 0], lx[:, 0], ACT.Exp, scale=1.0 / 16.0))
                    act.done(f(lx[:, 1], cum[:, 1], ACT.Exp, scale=1.0 / 16.0), "expB")
                if i == CARRY_AFTER + 1:
                    for d in range(2):
                        for g in range(2):
                            job = ("kT", d, g)
                            is_filled(sc, job)
                            drains(f(kTok[:, 4 * d:4 * d + 4, g, :], bk(job)[:, :].rearrange("p (n c) -> p n c", n=4),
                                     ACT.Copy), job)
                    query_tables(0)
                    for d in range(2):
                        for h in range(HEADS):
                            ins = f(wcol[:, d, h:h + 1], ccol[:, C_POS - C_IOTA + 1 - d:C_POS - C_IOTA + 2 - d], ACT.Exp,
                                    scale=lg[:, d, h:h + 1])
                    act.done(ins, "wcol")
            for d, v in enumerate((new_gf, new_gb)):
                is_drained(sc, ("gu", d, 0))
                sc.dma_start(v[0, 0].rearrange("(g a) d e -> (a d) g e", a=2), gsout[:, d]).then_inc(s_gout, 16)
            for job, b in plan_outputs():
                if job[0] == "o":
                    if b[0] == "r" and b[1] != "ctx" and b[1] < HEADS - 1:
                        query_tables(b[1] + 1)
                    if b == ("r", HEADS - 1):
                        dve.wait(sc, ("rm", HEADS - 1))
                        pool_s.wait(sc, ("qd", HEADS - 1))
                        for t in range(TILES):
                            sc.dma_start(X[:, t, :], xs[t * P:(t + 1) * P, :] if t < LT else x_prompt[0]).then_inc(s_x2[t], 16)
                    if b[0] == "r":
                        dve.wait(sc, ("cen", b))
                        src = onorm[BLOCKS_OUT.index(b) % 2][:, :, :]
                    else:
                        is_filled(sc, job)
                        if BLOCKS_OUT.index(b):
                            dve.wait(sc, ("ms", BLOCKS_OUT[BLOCKS_OUT.index(b) - 1]))
                        src = bk(job)[:, :].rearrange("p (a e) -> p a e", a=4)
                    act.done(f(sq, src, ACT.Square), ("sq", b))
                if job[0] == "rst":
                    d = job[1]
                    is_filled(sc, job)
                    drains(f(rsout[:, d], bk(job)[:, :].rearrange("p (h e) -> p h e", h=HEADS), ACT.Copy), job)
                    is_drained(sc, job)
                    sc.dma_start((new_rf, new_rb)[d][0, 0].rearrange("h d e -> d h e"), rsout[:, d]).then_inc(s_out, 16)
            for t in range(TILES):
                dve.wait(sc, ("x2", t))
                if t >= 2:
                    dve.wait(sc, ("hn", t - 2))
                act.done(f(mt[t % 2], X[:, t, :], ACT.Square, accum_out=ss[:, t:t + 1]), ("ss2", t))
                dve.wait(sc, ("hn", t))
                sc.dma_start(hn_dram[t * P:(t + 1) * P, :].rearrange("t d -> t d"), hn[t % 2]).then_inc(s_hnw[t % 2], 16)
                for half in range(2):
                    job = ("hT", t, half)
                    is_filled(sc, job)
                    if t >= 1:
                        is_filled(sc, ("lg", t - 1))
                    drains(f(hnT[:, 4 * half:4 * half + 4, :], bk(job)[:, :].rearrange("p (k t) -> p k t", k=4), ACT.Copy), job)
            dve.wait(sc, "diffs")
            act.done(f(rdiff, rdiff, ACT.Exp), "rexp")

            def turned_tokens(e, n, free):
                sc.wait_ge(xg_turned, e + 1)
                if free is not None:
                    sc.wait_ge(gu_filled, free)
                f(xte[n], bank[n][:, :].rearrange("p (k s) -> p k s", k=KC), ACT.Copy).then_inc(xte_ready, 1)

            def silu(e, n, free):
                sc.wait_ge(gu_filled, e + 1)
                if free is not None:
                    sc.wait_ge(hid_ready, free)
                f(sil[n], bank[2 + n][:, 0:P], ACT.Silu).then_inc(sil_ready, 1)

            def half_rows(e, n, row, written):
                sc.wait_ge(y_filled, e + 1)
                if written is not None:
                    sc.wait_ge(ys_written[n], written)
                f(yb[n][:, 0:512], bank[4 + 2 * n][0:SLOTS, :], ACT.Copy).then_inc(y_half0, 1)
                sc.wait_ge(y_half0, e + 1)
                sc.wait_ge(y_half1, e + 1)
                sc.dma_start(ys_dram[bass.ds(row, SLOTS), :], yb[n]).then_inc(ys_written[n], 16)

            def experts(it, first=False, last=False):
                for b in range(4):
                    e = 4 * it + b
                    if not (last and b == 3):
                        silu(e + 1, (b + 1) % 2, None if first and b == 0 else e)
                        turned_tokens(e + 2, b % 2, e + 1)
                    half_rows(e, b % 2, e * SLOTS, None if first and b < 2 else 32 * it + 16 * (b // 2))

            for h in range(2):
                sc.wait_ge(s_hnw[h], 16 * (3 - h))
            sc.wait_ge(s_zero, 32)
            turned_tokens(0, 0, None)
            silu(0, 0, None)
            turned_tokens(1, 1, None)
            experts(0, first=True)
            with sc.Fori(1, NE // 4 - 1) as it:
                experts(it)
            experts(NE // 4 - 1, last=True)
            dve.wait(sc, "dest")
            n_over = sc.value_load(over[0:1, 0:1], min_val=0, max_val=MAX_OVER)
            with sc.If(n_over > 0):
                with sc.Fori(0, n_over) as i:
                    turned_tokens(NE + 1 + i, 0, NE + i)
                    silu(NE + i, 0, NE + i)
                    half_rows(NE + i, 0, (NE + i) * SLOTS, 16 * (NE // 2) + 16 * i)
            for t in range(max(TILES + 2, POOL_TILES + 4)):
                if t < TILES:
                    sc.wait_ge(yp_landed[t][0], 16)
                    f(yp[t][0], yp[t][0], ACT.Copy, scale=pickw[:, 0, t:t + 1]).then_inc(y1_scaled, 1)
                if 2 <= t < TILES + 2:
                    sc.wait_ge(x3_ready, t - 1)
                    f(yo[t - 2], X[:, t - 2, :], ACT.Square, accum_out=ss[:, t - 2:t - 1]).then_inc(ss3_ready, 1)
                if 4 <= t < POOL_TILES + 4:
                    sc.wait_ge(rs3_ready, t - 3)
                    f(yo[t - 4], X[:, t - 4, :], ACT.Copy, scale=rstd[:, t - 4:t - 3]).then_inc(yo_scaled, 1)

        @block.vector
        def _(dv):
            chain = [0]

            def link(ins):
                chain[0] += 1
                ins.then_inc(dve_chain, 1)
                dv.wait_ge(dve_chain, chain[0])

            v = nc.vector

            def mean_square(out, total, n):
                return v.tensor_scalar(out, total, 1.0 / n, EPS, ALU.mult, ALU.add)

            act.wait(dv, ("ss", CTX))
            dve.done(mean_square(rstd, ss, D), "ms0")
            for n in (1, 3):
                is_filled(dv, ("mr", n))
                drains(v.tensor_copy(first_mod_rows[:, n * 512:(n + 1) * 512], bk(("mr", n))[0:2, :]), ("mr", n))
            dv.wait_ge(s_row, 16 * 3)
            dv.wait_ge(s_ident, 32)
            is_filled(dv, ("mT",))
            drains(v.tensor_tensor(mcol.rearrange("p (m a) k -> p m a k", m=2),
                                   bk(("mT",))[:, 0:32].rearrange("p (m k a) -> p m a k", m=2, a=2),
                                   bcol.unsqueeze(2).to_broadcast([P, 2, 2, KC]), ALU.add), ("mT",))
            is_drained(dv, ("mT",))
            dve.done(v.scalar_tensor_tensor(mcol[:, 2:4], mcol[:, 2:4], 1.0, n1col.unsqueeze(1).to_broadcast([P, 2, KC]),
                                            ALU.add, ALU.mult), "mcol")
            dve.wait(dv, "mcol")
            for k in range(0, KC, 2):
                job = ("xT", k)
                is_filled(dv, job)
                drains(v.tensor_scalar(hT[:, k, 0:N_LAT], bk(job)[:, :], mcol[:, 2, k:k + 1], mcol[:, 0, k:k + 1],
                                       ALU.mult, ALU.add), job)
            for half in range(2):
                job = ("xTc", half)
                is_filled(dv, job)
                for k in range(4 * half, 4 * half + 4):
                    ins = v.tensor_scalar(hT[:, k, N_LAT:T], bk(job)[:, (k % 4) * P:(k % 4 + 1) * P],
                                          mcol[:, 3, k:k + 1], mcol[:, 1, k:k + 1], ALU.mult, ALU.add)
                drains(ins, job)
            dve.done(v.memset(st3[:, 1:2], 0.0), "hT")

            def level_scores(n):
                for m, (t0, t1) in enumerate(LEV_TILES):
                    for a in range(2):
                        job = ("lev", n, m, a)
                        is_filled(dv, job)
                        w = 2 * (t1 - t0) * P
                        src = bk(job)[:, 0:w].rearrange("p (t g q) -> p t g q", g=2, q=P)
                        dst = att[:, t0:t1, a::2, :]
                        if n == 0:
                            drains(v.tensor_copy(dst, src), job)
                        else:
                            mask = masks[n - 1].bitcast(U32).unsqueeze(1).unsqueeze(1).to_broadcast([P, t1 - t0, 2, P])
                            if (m, a) == (0, 0):
                                is_drained(dv, ("lev", n - 1, 2, 1))
                            drains(v.copy_predicated(dst, mask, src), job)

            def combine(r):
                n = LOADS.index(("rest", r))
                load_ready(dv, n)
                if r >= 2:
                    dv.wait_ge(mod_summed, r - 1)
                w = ring[n % RING].rearrange("p (k c) -> p k c", k=KC)
                for k in range(KC):
                    for a in range(2):
                        acc = macc[r % 2][:, a]
                        if k == 0:
                            ins = v.tensor_scalar(acc, w[:, k], cS[:, a, k:k + 1], None, ALU.mult)
                        else:
                            dv.wait_ge(dve_chain, chain[0] - 1)
                            ins = v.scalar_tensor_tensor(acc, w[:, k], cS[:, a, k:k + 1], acc, ALU.mult, ALU.add)
                        if (k, a) == (KC - 1, 1):
                            dve.done(ins, ("acc", r))
                        else:
                            chain[0] += 1
                            ins.then_inc(dve_chain, 1)

            for i, (name, _, w) in enumerate(IN_ITEMS):
                if name == "glr":
                    dv.wait_ge(s_cols, 16 * 6)
                    for d in range(2):
                        for g in range(2):
                            for part, lo, hi in (("lat", 0, N_LAT), ("ctx", N_LAT, T)):
                                job = ("z", d, g, part)
                                is_filled(dv, job)
                                ins = v.tensor_scalar(cum[:, d, g, lo:hi], bk(job)[:, 0:hi - lo], gbias[:, d, g:g + 1], None, ALU.add)
                                drains(ins, job)
                    is_drained(dv, ("z", 1, 1, "ctx"))
                    dve.done(v.memset(st3[:, 2:3], 0.0), "zb")
                    act.wait(dv, "softplus")
                    link(v.scalar_tensor_tensor(lqk_f, cum_f, 0.0, lx_f, ALU.min, ALU.subtract))
                    dv.wait_ge(s_tail, 32)
                    for d in range(2):
                        for g in range(2):
                            for t in range(TILES):
                                tt = slice(t * P, (t + 1) * P)
                                ins = v.tensor_tensor_scan(cum[:, d, g, tt], ones_s, lqk[:, d, g, tt], 0.0, ALU.mult, ALU.add)
                    link(ins)
                    link(v.tensor_copy(tot, cum_f.rearrange("p (a t n) -> p a t n", a=4, n=P)[:, :, :, P - 1]))
                    dve.done(v.tensor_tensor(cum[:, 1], cum[:, 1], lqk[:, 1], ALU.subtract), "cum")
                if rots_after(i, 0) is not None or i in (3, 4, 5, 6):
                    for c in range(2):
                        j = rots_after(i, c)
                        if j is None:
                            continue
                        a, h = ("rq", "rk").index(IN_ITEMS[j[0]][0]), 2 * ((j[0] - 3) % 2) + j[1]
                        job = ("rot", *j)
                        is_filled(dv, job)
                        link(v.tensor_tensor(rsin, bk(job)[:, :], sinT, ALU.mult))
                        pool_s.wait(dv, ("cos", *j))
                        drains(v.tensor_tensor(rqk[:, a, h, 0:N_LAT], rqk[:, a, h, 0:N_LAT], rsin, ALU.add), job)
                        is_drained(dv, job)
                if 7 <= i < 7 + HEADS:
                    h = i - 7
                    pool_s.wait(dv, ("sel", h, 1))
                    dve.done(v.tensor_tensor(strips[:, h, :], strips[:, h, :], stmp[h % 2], ALU.add), ("strip", h))
                n = i - LEVEL_AFTER
                if 0 <= n <= NL:
                    level_scores(n)
                if 0 <= n + 1 < NL:
                    act.wait(dv, ("exp", n + 1))
                    if n >= 0:
                        is_filled(dv, ("lev", n, 2, 1))
                    dve.done(v.tensor_tensor(lqk_f, gqk_f, lx_f, ALU.mult), ("lqk", n + 1))
                elif n + 1 == NL:
                    is_filled(dv, ("lev", n, 2, 1))
                    dve.done(v.tensor_scalar(lqk[:, 0], gqk[:, 0], 2.0, None, ALU.mult), ("lqk", NL))
                for r in rest_after(i):
                    combine(r)
                if i == CARRY_AFTER:
                    act.wait(dv, "expF")
                    is_filled(dv, ("lev", NL, 2, 1))
                    dve.done(v.tensor_tensor(lqk_f, gqk_f, lx_f, ALU.mult), "qkF")
                    act.wait(dv, "expB")
                    dve.done(v.tensor_tensor(lx_f, gqk_f, lx_f, ALU.mult), "qkB")
                if i == CARRY_AFTER + 1:
                    dv.wait_ge(s_gs0, 32)
                    for n in range(4):
                        for d in range(2):
                            job = ("gu", d, n)
                            is_filled(dv, job)
                            src = bk(job)[:, 0:2 * P].rearrange("p (g e) -> p g e", g=2)
                            if n == 0:
                                drains(v.tensor_copy(gsout[:, d], src), job)
                                continue
                            t = (n - 1, LT - n)[d]
                            if n >= 2:
                                is_drained(dv, ("gu", d, n - 1))
                            link(v.scalar_tensor_tensor(gst[:, d, n, 0], gst[:, d, n - 1, 0], dec[:, 2 * d, t:t + 1], src[:, 0],
                                                        ALU.mult, ALU.add))
                            drains(v.scalar_tensor_tensor(gst[:, d, n, 1], gst[:, d, n - 1, 1], dec[:, 2 * d + 1, t:t + 1],
                                                          src[:, 1], ALU.mult, ALU.add), job)
            def pieces(b):
                return bk(("o", *b))[:, :].rearrange("p (a e) -> p a e", a=4)

            def centre(b):
                job, n = ("o", *b), BLOCKS_OUT.index(b)
                is_filled(dv, job)
                if n >= 2:
                    is_filled(dv, ("T", *BLOCKS_OUT[n - 2]))
                link(v.tensor_reduce(st1, pieces(b), AX, ALU.add))
                link(v.tensor_scalar(st1, st1, 1.0 / P, None, ALU.mult))
                dve.done(v.tensor_tensor(onorm[n % 2][:, :, :], pieces(b), st1.unsqueeze(2).to_broadcast([P, 4, P]), ALU.subtract),
                         ("cen", b))
                drains(v.memset(marks[:, n:n + 1], 0.0), job)

            def squares(b):
                act.wait(dv, ("sq", b))
                if BLOCKS_OUT.index(b):
                    dve.wait(dv, ("on", BLOCKS_OUT[BLOCKS_OUT.index(b) - 1]))
                link(v.tensor_reduce(st2, sq, AX, ALU.add))
                dve.done(mean_square(st2, st2, P), ("ms", b))

            def scaled(b):
                pool_s.wait(dv, ("rs", b))
                n = BLOCKS_OUT.index(b)
                o, roots = onorm[n % 2][:, :, :], st2.unsqueeze(2).to_broadcast([P, 4, P])
                if b[0] == "g":
                    if n >= 2:
                        is_filled(dv, ("T", *BLOCKS_OUT[n - 2]))
                    dve.done(v.tensor_tensor(o, pieces(b), roots, ALU.mult), ("on", b))
                    drains(v.memset(marks[:, n:n + 1], 0.0), ("o", *b))
                else:
                    dve.done(v.tensor_tensor(o, o, roots, ALU.mult), ("on", b))

            def gate_block(b):
                job = ("T", *b)
                is_filled(dv, job)
                h0 = 4 if b[0] == "g" else 0
                if b[1] == "ctx":
                    for h in range(HEADS):
                        ins = v.scalar_tensor_tensor(hT[:, h0 + h, N_LAT:T], bk(job)[:, h * P:(h + 1) * P], nw[:, h0 + h:h0 + h + 1],
                                                     gates[:, h0 + h, N_LAT:T], ALU.mult, ALU.mult)
                    drains(ins, job)
                else:
                    h = h0 + b[1]
                    drains(v.scalar_tensor_tensor(hT[:, h, 0:N_LAT], bk(job)[:, :], nw[:, h:h + 1], gates[:, h, 0:N_LAT],
                                                  ALU.mult, ALU.mult), job)

            dv.wait_ge(s_zero, 32)
            for job, b in plan_outputs():
                if job == ("o", "g", 0):
                    dv.wait_ge(mod_summed, 16)
                    dve.done(v.tensor_copy(modc, mod_ps[:, 0:64]), "modc")
                if job == ("modT",):
                    dv.wait_ge(s_mrow, 16 * 4)
                    is_filled(dv, job)
                    link(v.tensor_tensor(modr[0:64, :], bk(job)[0:64, 0:P], brow[0:64, :], ALU.add))
                    o = C_ONE - C_IOTA
                    drains(v.scalar_tensor_tensor(modr[0:64, :], modr[0:64, :], ccol[0:64, o:o + 1], wrow[0:64, :],
                                                  ALU.add, ALU.mult), job)
                if job[0] == "o":
                    n = BLOCKS_OUT.index(b)
                    if b[0] == "r":
                        centre(b)
                    if n:
                        scaled(BLOCKS_OUT[n - 1])
                    squares(b)
                elif job[0] == "T":
                    if job == ("T", "r", 2):
                        scaled(BLOCKS_OUT[-1])
                    gate_block(b)
                elif job == ("rs", "ctx"):
                    is_filled(dv, job)
                    drains(v.tensor_tensor(cmask, bk(job)[:, :].rearrange("p (h t) -> p h t", h=HEADS),
                                           strips[:, :, N_LAT - P:N_LAT], ALU.mult), job)
                    is_drained(dv, job)
                    dve.done(v.memset(st3[:, 0:1], 0.0), "cmask")
                elif job == ("rkT",):
                    is_filled(dv, job)
                    act.wait(dv, "wcol")
                    for d in range(2):
                        link(v.tensor_tensor(kdec[:, d], bk(job)[:, :].rearrange("p (h c) -> p h c", h=HEADS),
                                             wcol[:, d].unsqueeze(2).to_broadcast([P, HEADS, P]), ALU.mult))
                    drains(v.memset(st3[:, 1:2], 0.0), job)
                    dve.done(v.memset(st3[:, 2:3], 0.0), "kdec")
                elif job[0] == "rs":
                    _, h, s = job
                    is_filled(dv, job)
                    if (h, s) == (2, 0):
                        dv.wait_ge(s_gout, 32)
                    if h == HEADS - 1:
                        is_filled(dv, ("o", "r", 1))
                    x0 = N_LAT - P - s * P
                    drains(v.tensor_tensor(rmask[h][:, s], bk(job)[:, :], strips[:, h, x0:x0 + N_LAT], ALU.mult), job)
                    if s == LT - 1:
                        is_drained(dv, job)
                        dve.done(v.memset(st3[:, 3:4], 0.0), ("rm", h))

            dv.wait_ge(s_bc, 16 * 6)
            dv.wait_ge(s_rt, 16 * 5)
            for t in range(TILES):
                cond = int(t == CTX)
                for n in range(4):
                    job = ("mix", t, n)
                    cc = slice(n * ITEM, (n + 1) * ITEM)
                    is_filled(dv, job)
                    drains(v.tensor_tensor(mt[t % 2][:, cc], bk(job)[:, 0:ITEM], g1b[cond][:, cc], ALU.mult), job)
                is_drained(dv, job)
                dv.wait_ge(s_x2[t], 16)
                dve.done(v.tensor_tensor(X[:, t, :], X[:, t, :], mt[t % 2], ALU.add), ("x2", t))
                act.wait(dv, ("ss2", t))
                dve.done(mean_square(rstd[:, t:t + 1], ss[:, t:t + 1], D), ("ms2", t))
                pool_s.wait(dv, ("rs2", t))
                link(v.scalar_tensor_tensor(mt[t % 2], X[:, t, :], rstd[:, t:t + 1], a2b[cond], ALU.mult, ALU.mult))
                if t >= 2:
                    is_filled(dv, ("hT", t - 2, 1))
                    dv.wait_ge(s_hnw[t % 2], 16 * (t // 2))
                o = hn[t % 2].rearrange("p (k j) -> p k j", k=KC)
                dve.done(v.tensor_tensor(o, mt[t % 2].rearrange("p (j k) -> p k j", k=KC),
                                         b2b[cond].rearrange("p (j k) -> p k j", k=KC), ALU.add), ("hn", t))
                if t >= 1:
                    job = ("lg", t - 1)
                    is_filled(dv, job)
                    drains(v.tensor_tensor(lgt[:, t - 1, :], bk(job)[:, 0:36], rbias, ALU.add), job)
            job = ("lg", CTX)
            is_filled(dv, job)
            drains(v.tensor_tensor(lgt[:, CTX, :], bk(job)[:, 0:36], rbias, ALU.add), job)
            is_drained(dv, job)

            def bc(ap, n):
                return ap.unsqueeze(2).to_broadcast([P, ap.shape[1], n])

            def iota(n, rows=TILES):
                return kiota[:, 0:n].unsqueeze(1).to_broadcast([P, rows, n])

            def first_max(x, n):
                m, eq, i = rs(TILES), rs(TILES, n), rs(TILES)
                link(v.tensor_reduce(m, x, AX, ALU.max))
                link(v.tensor_tensor(eq, x, bc(m, n), ALU.is_equal))
                link(v.scalar_tensor_tensor(eq, eq, -100.0, iota(n), ALU.mult, ALU.add))
                link(v.tensor_reduce(i, eq, AX, ALU.min))
                link(v.tensor_scalar(i, i, 100.0, None, ALU.add))
                link(v.tensor_tensor(eq, iota(n), bc(i, n), ALU.is_equal))
                return m, i, eq

            gl = lgt[:, :, 0:NG]
            gm, gi, g_hot = first_max(gl, NG)
            gd = rdiff[:, 0:TILES * NG].rearrange("p (t g) -> p t g", t=TILES)
            link(v.tensor_tensor(gd, gl, bc(gm, NG), ALU.subtract))
            em, es = rs(TILES, NG, EPG), rs(TILES, EPG)
            for t in range(TILES):
                ins = v.tensor_tensor(em[:, t], lgt[:, t, NG:].rearrange("p (g j) -> p g j", g=NG), bc(g_hot[:, t], EPG), ALU.mult)
            link(ins)
            for t in range(TILES):
                ins = v.tensor_reduce(es[:, t], em[:, t].rearrange("p g j -> p j g"), AX, ALU.add)
            link(ins)
            m1, i1, hot1 = first_max(es, EPG)
            es2 = rs(TILES, EPG)
            link(v.scalar_tensor_tensor(es2, hot1, -3.0e38, es, ALU.mult, ALU.add))
            m2, i2, _ = first_max(es2, EPG)
            dve.done(v.tensor_tensor(rdiff[:, TILES * NG:], m2, m1, ALU.subtract), "diffs")
            pk_e, hot = rs(2 * TILES), rs(2 * TILES, NE)
            for k, i in enumerate((i1, i2)):
                link(v.scalar_tensor_tensor(pk_e[:, k * TILES:(k + 1) * TILES], gi, float(EPG), i, ALU.mult, ALU.add))
            link(v.tensor_tensor(hot, iota(NE, 2 * TILES), bc(pk_e, NE), ALU.is_equal))
            dve.done(v.tensor_tensor(oo, hot[:, 0:TILES], hot[:, TILES:], ALU.add), "OO")
            job = ("pos",)
            is_filled(dv, job)
            place = rs(2 * TILES, NE)
            drains(v.tensor_copy(place, bk(job)[:, 0:2 * TILES * NE].rearrange("p (t e) -> p t e", e=NE)), job)
            is_drained(dv, job)
            for t in range(1, TILES):
                link(v.tensor_tensor(place[:, TILES + t], place[:, TILES + t], place[:, TILES + t - 1], ALU.add))
            link(v.tensor_tensor(place[:, 1:TILES], place[:, 1:TILES], place[:, TILES:2 * TILES - 1], ALU.add))
            count = place[:, 2 * TILES - 1]
            tmp = rs(2 * TILES, NE)
            for k in range(2):
                ks = slice(k * TILES, (k + 1) * TILES)
                link(v.tensor_tensor(tmp[:, ks], hot[:, ks], place[:, 0:TILES], ALU.mult))
            pk_p, q, slot = rs(2 * TILES), rs(2 * TILES), rs(2 * TILES)
            link(v.tensor_reduce(pk_p, tmp, AX, ALU.add))
            steps9 = kiota[:, 64:73]
            cmp9, n_ov, ov_end, ov_at = rs(NE, 9), rs(NE), rs(NE), rs(NE)
            link(v.tensor_tensor(cmp9, bc(count, 9), steps9.unsqueeze(1).to_broadcast([P, NE, 9]), ALU.is_gt))
            link(v.tensor_reduce(n_ov, cmp9, AX, ALU.add))
            link(v.tensor_tensor_scan(ov_end, kones[:, 0:NE], n_ov, 0.0, ALU.mult, ALU.add))
            link(v.tensor_tensor(ov_at, ov_end, n_ov, ALU.subtract))
            c2 = rs(2 * TILES, 9)
            link(v.tensor_tensor(c2, bc(pk_p, 9), steps9.unsqueeze(1).to_broadcast([P, 2 * TILES, 9]), ALU.is_ge))
            link(v.tensor_reduce(q, c2, AX, ALU.add))
            link(v.scalar_tensor_tensor(slot, q, -float(SLOTS), pk_p, ALU.mult, ALU.add))
            link(v.tensor_tensor(tmp, hot, ov_at.unsqueeze(1).to_broadcast([P, 2 * TILES, NE]), ALU.mult))
            va, blk, row = rs(2 * TILES), rs(2 * TILES), rs(2 * TILES)
            link(v.tensor_reduce(va, tmp, AX, ALU.add))
            link(v.tensor_tensor(va, va, q, ALU.add))
            link(v.scalar_tensor_tensor(va, va, float(NE - 1), pk_e, ALU.add, ALU.subtract))
            link(v.tensor_scalar(q, q, 1.0, None, ALU.min))
            link(v.tensor_tensor(va, va, q, ALU.mult))
            link(v.tensor_tensor(blk, va, pk_e, ALU.add))
            link(v.scalar_tensor_tensor(row, blk, float(SLOTS), slot, ALU.mult, ALU.add))
            link(v.tensor_tensor(oh_slot, iota(SLOTS, 2 * TILES), bc(slot, SLOTS), ALU.is_equal))
            link(v.tensor_tensor(oh_block, iota(BLOCKS, 2 * TILES), bc(blk, BLOCKS), ALU.is_equal))
            tok = kiota[:, C_TOK - C_IOTA:C_TOK - C_IOTA + TILES]
            for k in range(2):
                ks = slice(k * TILES, (k + 1) * TILES)
                ins = v.tensor_tensor(oh_block[:, ks], oh_block[:, ks], bc(tok, BLOCKS), ALU.mult)
            dve.done(ins, "onehots")
            job = ("idx",)
            is_filled(dv, job)
            drains(v.tensor_copy(idx[:, :], bk(job)[0:SLOTS, 0:BLOCKS]), job)
            is_drained(dv, job)
            dve.done(v.memset(st3[:, 3:4], 0.0), "idx")
            link(v.tensor_copy(dest[:, :], row))
            link(v.tensor_copy(over[0:1, 0:1], ov_end[0:1, NE - 1:NE]))
            cmpo, eob = rs(MAX_OVER, NE), rs(MAX_OVER)
            link(v.tensor_tensor(cmpo[0:1], ov_end[0:1].unsqueeze(1).to_broadcast([1, MAX_OVER, NE]),
                                 kiota[0:1, 0:MAX_OVER].unsqueeze(2).to_broadcast([1, MAX_OVER, NE]), ALU.is_le))
            link(v.tensor_reduce(eob[0:1], cmpo[0:1], AX, ALU.add))
            link(v.tensor_scalar(over[0:1, 1:], eob[0:1], float(NE - 1), None, ALU.min))
            act.wait(dv, "rexp")
            gs, p2 = rs(TILES), rdiff[:, TILES * NG:]
            link(v.tensor_reduce(gs, gd, AX, ALU.add))
            den = rs(TILES)
            link(v.tensor_scalar(den, p2, 1.0, None, ALU.add))
            link(v.tensor_tensor(den, den, gs, ALU.mult))
            link(v.reciprocal(pickw[:, 0, :], den))
            link(v.tensor_tensor(pickw[:, 1, :], pickw[:, 0, :], p2, ALU.mult))
            dve.done(v.memset(st3[:, 0:1], 0.0), "dest")

            def hidden(e, n, free):
                dv.wait_ge(sil_ready, e + 1)
                if free is not None:
                    dv.wait_ge(y_filled, free)
                v.tensor_tensor(hid[n], sil[n].rearrange("p (j s) -> p j s", j=FC),
                                bank[2 + n][:, P:2 * P].rearrange("p (j s) -> p j s", j=FC), ALU.mult).then_inc(hid_ready, 1)

            def half_rows(e, n, written):
                dv.wait_ge(y_filled, e + 1)
                if written is not None:
                    dv.wait_ge(ys_written[n], written)
                v.tensor_copy(yb[n][:, 512:D], bank[5 + 2 * n][0:SLOTS, :]).then_inc(y_half1, 1)

            def experts(it, first=False, last=False):
                for b in range(4):
                    e = 4 * it + b
                    if not (last and b == 3):
                        hidden(e + 1, (b + 1) % 2, None if first and b == 0 else e)
                    half_rows(e, b % 2, None if first and b < 2 else 32 * it + 16 * (b // 2))

            for h in range(2):
                dv.wait_ge(s_hnw[h], 16 * (3 - h))
            hidden(0, 0, None)
            experts(0, first=True)
            with dv.Fori(1, NE // 4 - 1) as it:
                experts(it)
            experts(NE // 4 - 1, last=True)
            n_over = dv.value_load(over[0:1, 0:1], min_val=0, max_val=MAX_OVER)
            with dv.If(n_over > 0):
                with dv.Fori(0, n_over) as i:
                    hidden(NE + i, 0, NE + i)
                    half_rows(NE + i, 0, 16 * (NE // 2) + 16 * i)
            dv.wait_ge(s_fin, 16 * 3)
            def mean_squares(t):
                dv.wait_ge(ss3_ready, t + 1)
                mean_square(rstd[:, t:t + 1], ss[:, t:t + 1], D).then_inc(ms3_ready, 1)

            def final_rows(t):
                dv.wait_ge(rs3_ready, t + 1)
                v.scalar_tensor_tensor(yo[t], X[:, t, :], rstd[:, t:t + 1], fnb, ALU.mult, ALU.mult).then_inc(yo_ready, 1)

            for t in range(TILES):
                y1, y2 = yp[t]
                dv.wait_ge(yp_landed[t][1], 16)
                dv.wait_ge(y1_scaled, t + 1)
                link(v.scalar_tensor_tensor(y2, y2, pickw[:, 1, t:t + 1], y1, ALU.mult, ALU.add))
                link(v.tensor_tensor(y2, y2, g2b[int(t == CTX)], ALU.mult))
                v.tensor_tensor(X[:, t, :], X[:, t, :], y2, ALU.add).then_inc(x3_ready, 1)
                if t >= 1:
                    mean_squares(t - 1)
            mean_squares(CTX)
            for t in range(POOL_TILES, TILES):
                final_rows(t)

        @block.tensor
        def _(te):
            order = [0]

            def starts(job):
                assert JOBS[order[0]] == job, (JOBS[order[0]], job)
                order[0] += 1
                b, turn = where(job)
                if turn:
                    te.wait_ge(drained[b], turn)
                return bank[b]

            def fills(ins, job):
                ins.then_inc(filled[where(job)[0]], 1)

            mm, tr = nc.tensor.matmul, nc.tensor.transpose

            def keep_warm(n):
                for _ in range(n):
                    mm(mod_ps[:, :].rearrange("p (a c) -> p a c", a=4), ident[:, :], ident[:, :].unsqueeze(1).to_broadcast([P, 4, P]),
                       start=True, stop=True)

            act.wait(te, "cS")
            mr = [starts(("mr", n)) for n in range(4)]
            for m in range(2):
                for i in range(4):
                    te.wait_ge(landed[i], 16 * m + 16)
                    w = ring[i].rearrange("p (k c) -> p k c", k=2)
                    for half in range(2):
                        for kk in range(2):
                            ins = mm(mr[2 * m + half][0:2, :], cS[:, :, 2 * i + kk], w[:, kk, half * 512:(half + 1) * 512],
                                     start=(i == kk == 0), stop=(i == 3 and kk == 1))
                        if i == 3:
                            fills(ins, ("mr", 2 * m + half))
                    if i < 3:
                        ins.then_inc(ada_used, 1)

            def turn_modulations():
                for n in range(4):
                    is_drained(te, ("mr", n))
                ps = starts(("mT",))
                for m in range(2):
                    for k in range(KC):
                        o = 2 * (m * KC + k)
                        ins = tr(ps[:, o:o + 2], first_mod_rows[:, m * D + k:(m + 1) * D:KC], ident[0:2, 0:2])
                fills(ins, ("mT",))

            def other_modulations(r):
                dve.wait(te, ("acc", r))
                if r == 0:
                    pool_s.wait(te, "rs0")
                o = mod_ps[:, 0:64].rearrange("p (a n) -> p a n", a=2)
                for a in range(2):
                    for c in range(2):
                        ins = mm(o[:, a, 2 * r + c:2 * r + c + 1], macc[r % 2][:, a, c * P:(c + 1) * P], ones_c, start=True, stop=True)
                ins.then_inc(mod_summed, 1)

            te.wait_ge(s_ident, 32)
            act.wait(te, ("xn", CTX))
            for k in range(KC):
                ps = starts(("xT", k))
                for t in range(LT):
                    ins = tr(ps[:, t * P:(t + 1) * P], xn[:, t, k * P:(k + 1) * P], ident[:, :])
                fills(ins, ("xT", k))
                if k == 1:
                    turn_modulations()
            for half in range(2):
                ps = starts(("xTc", half))
                for k in range(4 * half, 4 * half + 4):
                    ins = tr(ps[:, (k % 4) * P:(k % 4 + 1) * P], xn[:, CTX, k * P:(k + 1) * P], ident[:, :])
                fills(ins, ("xTc", half))

            def rotate(i, c):
                job = ("rot", i, c)
                is_drained(te, ("p", i, c, "lat"))
                if (i, c) == (3, 0):
                    te.wait_ge(s_tail, 32)
                ps = starts(job)
                fills(mm(ps[:, :], rot_m, raw[(2 * (i - 3) + c) % 2], start=True, stop=True), job)

            dve.wait(te, "hT")
            for k in range(1, KC, 2):
                is_drained(te, ("xT", k))
            for i, (name, _, w) in enumerate(IN_ITEMS):
                n = LOADS.index(("in", i))
                load_ready(te, n)
                wt = ring[n % RING][:, 0:KC * w].rearrange("p (k c) -> p k c", k=KC)
                if name in ("gv", "rv"):
                    if rots_after(i, 0) is not None:
                        rotate(*rots_after(i, 0))
                    for t in range(TILES):
                        ps = starts(("v", i, t))
                        for k in range(KC):
                            ins = mm(ps[:, 0:ITEM], hT[:, k, t * P:(t + 1) * P], wt[:, k, :], start=(k == 0), stop=(k == KC - 1))
                        fills(ins, ("v", i, t))
                else:
                    for c in range(max(1, w // P)):
                        m = min(P, w)
                        for part, lo, hi in (("lat", 0, N_LAT), ("ctx", N_LAT, T)):
                            ps = starts(("p", i, c, part))
                            for k in range(KC):
                                ins = mm(ps[0:m, 0:hi - lo], wt[:, k, c * m:(c + 1) * m], hT[:, k, lo:hi],
                                         start=(k == 0), stop=(k == KC - 1))
                            fills(ins, ("p", i, c, part))
                        if rots_after(i, c) is not None:
                            rotate(*rots_after(i, c))
                for r in sums_after(i):
                    other_modulations(r)
                if name == "glr":
                    te.wait_ge(s_gate, 32)
                    is_drained(te, ("p", i, 0, "ctx"))
                    is_drained(te, ("p", i, 0, "lat"))
                    for d in range(2):
                        for g in range(2):
                            for part, lo, hi in (("lat", 0, N_LAT), ("ctx", N_LAT, T)):
                                job = ("z", d, g, part)
                                ps = starts(job)
                                fills(mm(ps[:, 0:hi - lo], wgate[:, d, g * P:(g + 1) * P], glrT[:, lo:hi], start=True, stop=True), job)
                n = i - LEVEL_AFTER
                if 0 <= n <= NL:
                    dve.wait(te, ("lqk", n))
                    for m, (t0, t1) in enumerate(LEV_TILES):
                        for a in range(2):
                            job = ("lev", n, m, a)
                            ps = starts(job)
                            pp = slice(GLA_DK * a, GLA_DK * (a + 1))
                            for t in range(t0, t1):
                                for g in range(2):
                                    tt, o = slice(t * P, (t + 1) * P), (2 * (t - t0) + g) * P
                                    keys = (lqk if n < NL else gqk)[pp, 1, g, tt]
                                    ins = mm(ps[:, o:o + P], keys, lqk[pp, 0, g, tt], start=True, stop=True)
                            fills(ins, job)

                if i == CARRY_AFTER + 1:
                    for d in range(2):
                        dve.wait(te, ("qkF", "qkB")[d])
                        for g in range(2):
                            job = ("kT", d, g)
                            ps = starts(job)
                            for n in range(4):
                                t = CTX if n == 0 else (n - 1, LT - n)[d]
                                ins = tr(ps[:, n * P:(n + 1) * P], (lqk, lx)[d][:, 1, g, t * P:(t + 1) * P], ident[:, :])
                            fills(ins, job)
                    for n in range(4):
                        for d in range(2):
                            if n == 0:
                                is_drained(te, ("kT", d, 0))
                                is_drained(te, ("kT", d, 1))
                            job = ("gu", d, n)
                            ps = starts(job)
                            t = CTX if n == 0 else (n - 1, LT - n)[d]
                            for h in range(HEADS):
                                g, a = h // 2, h % 2
                                ins = mm(ps[GLA_DK * a:GLA_DK * (a + 1), g * P:(g + 1) * P],
                                         kTok[:, 4 * d + n, g, GLA_DK * a:GLA_DK * (a + 1)],
                                         vv[:, t, 512 + h * P:512 + (h + 1) * P], start=True, stop=True)
                            fills(ins, job)

            for job, b in plan_outputs():
                if job == ("o", "g", 0):
                    other_modulations(rest_after(len(IN_ITEMS) - 1)[-1])
                if job == ("modT",):
                    dve.wait(te, "modc")
                if job == ("o", "g", 0):
                    te.wait_ge(s_gs0, 32)
                    for d in range(2):
                        is_drained(te, ("gu", d, 3))
                if job[0] == "T":
                    dve.wait(te, ("on", b))
                if job in (("rst", 0), ("rst", 1)):
                    dve.wait(te, "kdec")
                if job == ("o", "r", "ctx"):
                    dve.wait(te, "cmask")
                    te.wait_ge(s_rs0, 32)
                if job[0:2] == ("o", "r") and b[1] != "ctx":
                    dve.wait(te, ("rm", b[1]))
                    pool_s.wait(te, ("qd", b[1]))
                ps = starts(job)
                if job[0] == "T":
                    for a in range(4):
                        ins = tr(ps[:, a * P:(a + 1) * P], onorm[BLOCKS_OUT.index(b) % 2][:, a, :], ident[:, :])
                elif job == ("modT",):
                    ins = tr(ps[0:64, 0:P], modc, ident[:, :])
                elif job == ("o", "g", "ctx"):
                    for h in range(HEADS):
                        ins = mm(ps[:, h * P:(h + 1) * P], att[:, CTX, h, :], vv[:, CTX, 512 + h * P:512 + (h + 1) * P],
                                 start=True, stop=True)
                elif job[0:2] == ("o", "g"):
                    h = b[1]
                    g, pp = h // 2, slice(GLA_DK * (h % 2), GLA_DK * (h % 2 + 1))
                    for t in range(LT):
                        o, tt = ps[:, t * P:(t + 1) * P], slice(t * P, (t + 1) * P)
                        mm(o, att[:, t, h, :], vv[:, t, 512 + h * P:512 + (h + 1) * P], start=True, stop=False)
                        mm(o, lqk[pp, 0, g, tt], gst[pp, 0, t, g, :], start=False, stop=False)
                        ins = mm(o, lx[pp, 0, g, tt], gst[pp, 1, LT - 1 - t, g, :], start=False, stop=True)
                elif job == ("rs", "ctx"):
                    for h in range(HEADS):
                        ins = mm(ps[:, h * P:(h + 1) * P], rqk[:, 1, h, N_LAT:T], rqk[:, 0, h, N_LAT:T], start=True, stop=True)
                elif job == ("rkT",):
                    for h in range(HEADS):
                        ins = tr(ps[:, h * P:(h + 1) * P], rqk[:, 1, h, N_LAT:T], ident[:, :])
                elif job[0] == "rst":
                    for h in range(HEADS):
                        ins = mm(ps[:, h * P:(h + 1) * P], kdec[:, job[1], h, :], vv[:, CTX, h * P:(h + 1) * P], start=True, stop=True)
                elif job[0] == "rs":
                    _, h, s = job
                    ins = mm(ps[:, :], rqk[:, 1, h, s * P:(s + 1) * P], rqk[:, 0, h, 0:N_LAT], start=True, stop=True)
                elif job == ("o", "r", "ctx"):
                    for h in range(HEADS):
                        ins = mm(ps[:, h * P:(h + 1) * P], cmask[:, h, :], vv[:, CTX, h * P:(h + 1) * P], start=True, stop=True)
                else:
                    h = b[1]
                    for t in range(LT):
                        o, tt = ps[:, t * P:(t + 1) * P], slice(t * P, (t + 1) * P)
                        for s in range(LT):
                            mm(o, rmask[h][:, s, tt], vv[:, s, h * P:(h + 1) * P], start=(s == 0), stop=False)
                        for d in range(2):
                            ins = mm(o, qd[d][:, tt], rstate[:, d, h, :], start=False, stop=(d == 1))
                fills(ins, job)

            def router(t):
                dve.wait(te, ("hn", t))
                for half in range(2):
                    ps = starts(("hT", t, half))
                    for k in range(4 * half, 4 * half + 4):
                        ins = tr(ps[:, (k % 4) * P:(k % 4 + 1) * P], hn[t % 2][:, k * P:(k + 1) * P], ident[:, :])
                    fills(ins, ("hT", t, half))
                te.wait_ge(s_rt, 16 * 5)
                ps = starts(("lg", t))
                for half in range(2):
                    is_drained(te, ("hT", t, half))
                for k in range(KC):
                    ins = mm(ps[:, 0:36], hnT[:, k, :], rtw[:, k, :], start=(k == 0), stop=(k == KC - 1))
                fills(ins, ("lg", t))

            is_drained(te, ("T", "r", HEADS - 1))
            for t in range(TILES):
                for n in range(4):
                    ld = LOADS.index(("out", n))
                    load_ready(te, ld)
                    wt = ring[ld % RING].rearrange("p (k c) -> p k c", k=KC)
                    ps = starts(("mix", t, n))
                    for k in range(KC):
                        ins = mm(ps[:, 0:ITEM], hT[:, k, t * P:(t + 1) * P], wt[:, k, :], start=(k == 0), stop=(k == KC - 1))
                    fills(ins, ("mix", t, n))
                if t >= 1:
                    router(t - 1)
            keep_warm(3)
            router(CTX)
            keep_warm(8)
            dve.wait(te, "OO")
            ps = starts(("pos",))
            both = oo.rearrange("p t e -> p (t e)")
            mm(ps[:, 0:TILES * NE], ktri, both, start=True, stop=True)
            ins = mm(ps[:, TILES * NE:2 * TILES * NE], kones, both, start=True, stop=True)
            fills(ins, ("pos",))
            keep_warm(11)
            dve.wait(te, "onehots")
            ps = starts(("idx",))
            for n in range(2 * TILES):
                ins = mm(ps[0:SLOTS, 0:BLOCKS], oh_slot[:, n, :], oh_block[:, n, :], start=(n == 0), stop=(n == 2 * TILES - 1))
            fills(ins, ("idx",))
            assert order[0] == len(JOBS)
            for j in JOBS[-NB1:]:
                is_drained(te, j)
            keep_warm(4)

            def turn_tokens(e, n, b, gathered, free):
                te.wait_ge(xg_landed[b], gathered)
                if free is not None:
                    te.wait_ge(xte_ready, free)
                te.sem_inc(turns_begun, 1)
                for k in range(KC):
                    ins = tr(bank[n][:, k * SLOTS:(k + 1) * SLOTS], xg[b][:, k * P:(k + 1) * P], ident[0:SLOTS, 0:SLOTS])
                ins.then_inc(xg_turned, 1)

            def gate_up(e, n, b, free):
                te.wait_ge(xte_ready, e + 1)
                if free is not None:
                    te.wait_ge(hid_ready, free)
                for a, w in enumerate((exg[b], exu[b])):
                    for j in range(FC):
                        o = bank[2 + n][:, (2 * a + j) * SLOTS:(2 * a + j + 1) * SLOTS]
                        for k in range(KC):
                            ins = mm(o, w[:, k, j::FC], xte[n][:, k, :], start=(k == 0), stop=(k == KC - 1))
                ins.then_inc(gu_filled, 1)

            def down(e, n, b, free):
                te.wait_ge(hid_ready, e + 1)
                if free is not None:
                    te.wait_ge(y_half0, free)
                    te.wait_ge(y_half1, free)
                for half in range(2):
                    for j in range(FC):
                        ins = mm(bank[4 + 2 * n + half][0:SLOTS, :], hid[n][:, j, :], exd[b][:, j, half * 512:(half + 1) * 512],
                                 start=(j == 0), stop=(j == FC - 1))
                ins.then_inc(y_filled, 1)

            def experts(it, first=False, last=False):
                for b in range(4):
                    e = 4 * it + b
                    if not (last and b == 3):
                        te.wait_ge(ex_landed[(b + 1) % 4], 48 * it + (48 if b < 3 else 96))
                        gate_up(e + 1, (b + 1) % 2, (b + 1) % 4, None if first and b == 0 else e)
                        turn_tokens(e + 2, b % 2, (b + 2) % 4, 16 * it + (16 if b < 2 else 32), e + 1)
                    down(e, b % 2, b, None if first and b < 2 else e - 1)

            turn_tokens(0, 0, 0, 16, None)
            te.wait_ge(ex_landed[0], 48)
            gate_up(0, 0, 0, None)
            keep_warm(1)
            turn_tokens(1, 1, 1, 16, None)
            keep_warm(1)
            experts(0, first=True)
            with te.Fori(1, NE // 4 - 1) as it:
                experts(it)
            experts(NE // 4 - 1, last=True)
            dve.wait(te, "dest")
            n_over = te.value_load(over[0:1, 0:1], min_val=0, max_val=MAX_OVER)
            with te.If(n_over > 0):
                with te.Fori(0, n_over) as i:
                    turn_tokens(NE + 1 + i, 0, 0, 16 * (NE // 4 + 2) + 16 * i, NE + 1 + i)
                    te.wait_ge(ov_landed, 48 * i + 48)
                    te.wait_ge(xte_ready, NE + 2 + i)
                    for a, w in enumerate((exg[0], exu[0])):
                        for j in range(FC):
                            o = bank[2][:, (2 * a + j) * SLOTS:(2 * a + j + 1) * SLOTS]
                            for k in range(KC):
                                ins = mm(o, w[:, k, j::FC], xte[0][:, k, :], start=(k == 0), stop=(k == KC - 1))
                    ins.then_inc(gu_filled, 1)
                    down(NE + i, 0, 0, NE + i)


def host_constants():
    import numpy as np
    f = np.float32
    c = np.zeros((P, C_END), f)
    c[:, C_IDENT:C_IDENT + P] = np.eye(P)
    half, quarter = P // 2, P // 4
    rot = np.zeros((P, P), f)
    for base in (0, half):
        for i in range(quarter):
            rot[base + quarter + i, base + i] = -1.0
            rot[base + i, base + quarter + i] = 1.0
    c[:, C_ROT:C_ROT + P] = rot
    freqs = f(10000.0) ** (-np.arange(quarter, dtype=f) / f(quarter))
    t = np.arange(N_LAT)
    pos = np.stack([(t // GRID_W).astype(f), (t % GRID_W).astype(f)])
    for p in range(P):
        ang = (pos[p // half] * freqs[p % quarter]).astype(f)
        c[p, C_COS:C_COS + N_LAT] = np.cos(ang)
        c[p, C_SIN:C_SIN + N_LAT] = np.sin(ang)
    i, j = np.arange(P)[:, None], np.arange(P)[None, :]
    for n, h in enumerate(LEVELS[1:]):
        c[:, C_MASK + n * P:C_MASK + (n + 1) * P] = (i // (2 * h) == j // (2 * h)) & (i // h != j // h)
    c[:, C_MASK + 6 * P:C_MASK + 7 * P] = np.eye(P)
    c[:, C_ONES:C_ONES + P] = 1.0
    c[:, C_TRI:C_TRI + P] = i < j
    c[:, C_IOTA:C_IOTA + 64] = np.arange(64)
    c[:, C_IOTA + 64:C_IOTA + 73] = SLOTS * np.arange(1, 10)
    c[:, C_TOK:C_TOK + TILES] = np.arange(P)[:, None] + P * np.arange(TILES)
    c[:, C_POS] = np.arange(P)
    c[:, C_POS + 1] = P - 1 - np.arange(P)
    c[:, C_ONE] = (np.arange(P) % 32) // 8 == 2
    rc = np.zeros((P, R_END), f)
    rel = (np.arange(STRIP)[None, :] - np.arange(P)[:, None] - (N_LAT - P)).astype(f)
    rc[:, R_RELF:R_RELF + STRIP] = np.maximum(rel, 0)
    rc[:, R_RELB:R_RELB + STRIP] = np.maximum(-rel, 0)
    rc[:, R_TF:R_TF + N_LAT] = t + 1
    rc[:, R_TB:R_TB + N_LAT] = N_LAT - t
    return c, rc


_INS = ["x_prompt", "x_sample", "state_ret_fwd", "state_ret_bwd", "state_gla_fwd", "state_gla_bwd", "c", "c_ctx",
        "w_ada", "b_ada", "norm1_w", "w_in", "ret_decay_fwd", "ret_decay_bwd", "ret_norm_w", "gla_gate_w_fwd",
        "gla_gate_b_fwd", "gla_gate_w_bwd", "gla_gate_b_bwd", "gla_norm_w", "w_out", "norm2_w", "router_group_w",
        "router_group_b", "router_expert_w", "router_expert_b", "expert_w_gate", "expert_w_up", "expert_w_down",
        "final_norm_w"]
_OUTS = [(1, N_CTX, D), (1, N_LAT, D), (1, 1, HEADS, P, P), (1, 1, HEADS, P, P), (1, 1, HEADS, GLA_DK, P),
         (1, 1, HEADS, GLA_DK, P)]


def kernel(**inputs):
    import numpy as np
    import concourse.bacc as bacc
    from concourse.bass_utils import run_bass_kernel_spmd

    nc = bacc.Bacc("TRN2", target_bir_lowering=False, num_devices=1)
    arrays, ins = {}, []
    given = [(name, np.ascontiguousarray(inputs[name])) for name in _INS]
    for name, a in given + list(zip(("consts", "rconsts"), host_constants())):
        arrays[f"in_{name}"] = a
        ins.append(nc.dram_tensor(f"in_{name}", a.shape, mybir.dt.from_np(a.dtype), kind="ExternalInput").ap())
    outs = [nc.dram_tensor(f"out_{i}", shape, F32, kind="ExternalOutput").ap() for i, shape in enumerate(_OUTS)]
    build(nc, ins, outs)
    r = run_bass_kernel_spmd(nc, [arrays], core_ids=[0])
    return tuple(r.results[0][f"out_{i}"] for i in range(len(_OUTS)))
```
